# Optimizing a Trainium2 kernel written in Bass

```python
import jax, jax.numpy as jnp
from jax import lax
import numpy as np

D_MODEL = 1024
BATCH = 1
SEQ = 256
DEPTH = 2

CTX_LEN = 256
GRID_W = 64
NORM_EPS = 1e-6
NEG_INF = -1e30

POOL_WINDOWS = (2, 4, 8, 16)
POOL_GROUPS = len(POOL_WINDOWS)
POOL_GROUP_DIM = D_MODEL // 16
POOL_DIM = POOL_GROUPS * POOL_GROUP_DIM

HEAD_DIM = 64
ATTN_HEADS = D_MODEL // 128
ATTN_KV_HEADS = ATTN_HEADS // 4
Q_PER_KV = ATTN_HEADS // ATTN_KV_HEADS
ATTN_DIM = ATTN_HEADS * HEAD_DIM
KV_DIM = ATTN_KV_HEADS * HEAD_DIM
ATTN_WINDOW = 128
ATTN_BLOCK = 128
ROPE_BASE = 10000.0
ROPE_AXIS_DIM = HEAD_DIM // 2

HG_HEADS = 4
HG_DIM = 64
HG_WIDTH = HG_HEADS * HG_DIM
HG_CHUNK = 64

MIX_WIDTH = POOL_DIM + ATTN_DIM + HG_WIDTH
IN_SIZES = (POOL_DIM, ATTN_DIM, KV_DIM, KV_DIM, HG_WIDTH, HG_WIDTH, HG_WIDTH, HG_WIDTH, HG_WIDTH)
IN_SPLITS = tuple(sum(IN_SIZES[:i + 1]) for i in range(len(IN_SIZES) - 1))
IN_COLS = sum(IN_SIZES)

N_GROUPS = 4
EXPERTS_PER_GROUP = 8
N_EXPERTS = N_GROUPS * EXPERTS_PER_GROUP
TOP_K = 2
EXPERT_HIDDEN = D_MODEL // 2
MOE_BLOCK = 256

kernel_name = 'hybrid_pool_swa_hgrn2_hmoe_dit'

def rms_norm(t, g):
    tf = t.astype(jnp.float32)
    y = tf * lax.rsqrt(jnp.mean(tf * tf, axis=-1, keepdims=True) + NORM_EPS)
    return (y * g.astype(jnp.float32)).astype(t.dtype)

def modulate(t, g, shift, scale):
    return rms_norm(t, g) * (1.0 + scale) + shift

def to_heads(t, n):
    return t.reshape(t.shape[0], t.shape[1], n, t.shape[-1] // n)

def axial_rope(n_rows):
    row = jnp.repeat(jnp.arange(n_rows, dtype=jnp.float32), GRID_W)
    col = jnp.tile(jnp.arange(GRID_W, dtype=jnp.float32), n_rows)
    inv = ROPE_BASE ** (-jnp.arange(0, ROPE_AXIS_DIM, 2, dtype=jnp.float32) / ROPE_AXIS_DIM)
    ang = jnp.concatenate([row[:, None] * inv, col[:, None] * inv], axis=-1)
    return jnp.cos(ang), jnp.sin(ang)

def apply_rope(t, cos, sin):
    tf = t.astype(jnp.float32)
    half = HEAD_DIM // 2
    t1, t2 = tf[..., :half], tf[..., half:]
    c, s = cos[:, None, :], sin[:, None, :]
    return jnp.concatenate([t1 * c - t2 * s, t2 * c + t1 * s], axis=-1).astype(t.dtype)

def pool_mixer(u, pool_w, pool_scale):
    B_, L, _ = u.shape
    uf = u.astype(jnp.float32)
    cs = jnp.concatenate([jnp.zeros((B_, 1, POOL_DIM), jnp.float32), jnp.cumsum(uf, axis=1)], axis=1)
    t = jnp.arange(L)
    means = []
    for gi, w in enumerate(POOL_WINDOWS):
        lo = jnp.clip(t - (w - 1) // 2, 0, L)
        hi = jnp.clip(t + w // 2 + 1, 0, L)
        csg = cs[..., gi * POOL_GROUP_DIM:(gi + 1) * POOL_GROUP_DIM]
        means.append((csg[:, hi] - csg[:, lo]) / (hi - lo).astype(jnp.float32)[None, :, None])
    pooled = jnp.concatenate(means, axis=-1) - uf
    y = jnp.einsum('blgc,gcd->blgd', pooled.reshape(B_, L, POOL_GROUPS, POOL_GROUP_DIM),
                   pool_w.astype(jnp.float32))
    return y.reshape(B_, L, POOL_DIM) * pool_scale.astype(jnp.float32)

def windowed_sink_attention(q, k, v, kc, vc, sink):
    B_, L = q.shape[:2]
    nb = L // ATTN_BLOCK
    scale = HEAD_DIM ** -0.5
    qb = q.reshape(B_, nb, ATTN_BLOCK, ATTN_KV_HEADS, Q_PER_KV, HEAD_DIM)

    def band_blocks(t):
        tp = jnp.pad(t, ((0, 0), (ATTN_BLOCK, ATTN_BLOCK), (0, 0), (0, 0)))
        tp = tp.reshape(B_, nb + 2, ATTN_BLOCK, ATTN_KV_HEADS, HEAD_DIM)
        return jnp.concatenate([tp[:, :-2], tp[:, 1:-1], tp[:, 2:]], axis=2)

    kb, vb = band_blocks(k), band_blocks(v)
    q_pos = jnp.arange(L).reshape(nb, ATTN_BLOCK)
    k_pos = jnp.arange(nb)[:, None] * ATTN_BLOCK - ATTN_BLOCK + jnp.arange(3 * ATTN_BLOCK)[None, :]
    band = ((jnp.abs(q_pos[:, :, None] - k_pos[:, None, :]) <= ATTN_WINDOW)
            & (k_pos[:, None, :] >= 0) & (k_pos[:, None, :] < L))
    s_loc = jnp.einsum('bnqkgd,bnskd->bkgnqs', qb, kb).astype(jnp.float32) * scale
    s_loc = jnp.where(band, s_loc, NEG_INF)
    s_ctx = jnp.einsum('bnqkgd,bckd->bkgnqc', qb, kc).astype(jnp.float32) * scale
    sink_l = jnp.broadcast_to(sink.astype(jnp.float32).reshape(1, ATTN_KV_HEADS, Q_PER_KV, 1, 1, 1),
                              s_loc.shape[:-1] + (1,))
    p = jax.nn.softmax(jnp.concatenate([s_loc, s_ctx, sink_l], axis=-1), axis=-1)
    n_loc = 3 * ATTN_BLOCK
    n_ctx = kc.shape[1]
    p_loc = p[..., :n_loc].astype(v.dtype)
    p_ctx = p[..., n_loc:n_loc + n_ctx].astype(v.dtype)
    o = (jnp.einsum('bkgnqs,bnskd->bnqkgd', p_loc, vb)
         + jnp.einsum('bkgnqc,bckd->bnqkgd', p_ctx, vc))
    return o.reshape(B_, L, ATTN_DIM)

def context_attention(qc, kc, vc, sink):
    B_, C = qc.shape[:2]
    qb = qc.reshape(B_, C, ATTN_KV_HEADS, Q_PER_KV, HEAD_DIM)
    s = jnp.einsum('bqkgd,bckd->bkgqc', qb, kc).astype(jnp.float32) * (HEAD_DIM ** -0.5)
    sink_c = jnp.broadcast_to(sink.astype(jnp.float32).reshape(1, ATTN_KV_HEADS, Q_PER_KV, 1, 1),
                              s.shape[:-1] + (1,))
    p = jax.nn.softmax(jnp.concatenate([s, sink_c], axis=-1), axis=-1)[..., :C]
    o = jnp.einsum('bkgqc,bckd->bqkgd', p.astype(vc.dtype), vc)
    return o.reshape(B_, C, ATTN_DIM)

def gla_chunk_scan(q, k, v, log_f, s0):
    B_, L, H, _ = q.shape
    dv = v.shape[-1]
    nc = L // HG_CHUNK

    def chunks(t):
        return t.astype(jnp.float32).reshape(B_, nc, HG_CHUNK, H, t.shape[-1]).transpose(1, 0, 3, 2, 4)

    tri = jnp.tril(jnp.ones((HG_CHUNK, HG_CHUNK), bool))[:, :, None]

    def step(S, inp):
        qi, ki, vi, gi = inp
        b = jnp.cumsum(gi, axis=2)
        diff = b[:, :, :, None, :] - b[:, :, None, :, :]
        decay = jnp.exp(jnp.where(tri, diff, NEG_INF))
        scores = jnp.einsum('bhtd,bhsd,bhtsd->bhts', qi, ki, decay)
        o = (jnp.einsum('bhts,bhsv->bhtv', scores, vi)
             + jnp.einsum('bhtd,bhdv->bhtv', qi * jnp.exp(b), S))
        b_end = b[:, :, -1:, :]
        S_new = (jnp.exp(b_end[:, :, 0, :])[..., None] * S
                 + jnp.einsum('bhsd,bhsv->bhdv', ki * jnp.exp(b_end - b), vi))
        return S_new, o

    s_fin, oc = lax.scan(step, s0.astype(jnp.float32), (chunks(q), chunks(k), chunks(v), chunks(log_f)))
    return oc.transpose(1, 0, 3, 2, 4).reshape(B_, L, H, dv), s_fin

def hgrn_forget(z, lb):
    f = lb + (1.0 - lb) * jax.nn.sigmoid(z)
    return jnp.log(f), (1.0 - lb) * jax.nn.sigmoid(-z)

def hgrn_prepare(parts, lb_f, lb_b):
    hq, hi, hzf, hzb, hgate = parts
    heads = lambda t: to_heads(t.astype(jnp.float32), HG_HEADS)
    q = jax.nn.silu(heads(hq))
    v = heads(hi)
    gf, kf = hgrn_forget(heads(hzf), lb_f.reshape(HG_HEADS, HG_DIM))
    gb, kb = hgrn_forget(heads(hzb), lb_b.reshape(HG_HEADS, HG_DIM))
    return q, v, gf, kf, gb, kb, heads(hgate)

def hgrn_readout(o, gate, norm_g):
    B_, L = o.shape[:2]
    return (rms_norm(o, norm_g) * jax.nn.silu(gate)).reshape(B_, L, HG_WIDTH)

def hgrn_mixer(lat_parts, ctx_parts, lb_f, lb_b, norm_g, ctx_out):
    q, v, gf, kf, gb, kb, gate = hgrn_prepare(lat_parts, lb_f, lb_b)
    qc, vc, gfc, kfc, gbc, kbc, gatec = hgrn_prepare(ctx_parts, lb_f, lb_b)
    rev = lambda t: jnp.flip(t, axis=1)
    s0 = jnp.zeros((q.shape[0], HG_HEADS, HG_DIM, HG_DIM), jnp.float32)
    oc_f, sc_f = gla_chunk_scan(qc, kfc, vc, gfc, s0)
    oc_b, sc_b = gla_chunk_scan(rev(qc), rev(kbc), rev(vc), rev(gbc), s0)
    o_f, _ = gla_chunk_scan(q, kf, v, gf, sc_f)
    o_b, _ = gla_chunk_scan(rev(q), rev(kb), rev(v), rev(gb), sc_b)
    out = hgrn_readout(o_f + rev(o_b), gate, norm_g)
    out_c = hgrn_readout(oc_f + rev(oc_b), gatec, norm_g) if ctx_out else None
    return out, out_c

def token_mixers(p, pc, pool_w, pool_scale, q_norm_g, k_norm_g, sink, lb_f, lb_b, hg_norm_g,
                 cos, sin, ctx_out):
    u, q, k, v, hq, hi, hzf, hzb, hgate = jnp.split(p, IN_SPLITS, axis=-1)
    uc, qc, kc, vc, hqc, hic, hzfc, hzbc, hgatec = jnp.split(pc, IN_SPLITS, axis=-1)
    dt = p.dtype
    a = pool_mixer(u, pool_w, pool_scale)
    q = apply_rope(rms_norm(to_heads(q, ATTN_HEADS), q_norm_g), cos, sin)
    k = apply_rope(rms_norm(to_heads(k, ATTN_KV_HEADS), k_norm_g), cos, sin)
    v = to_heads(v, ATTN_KV_HEADS)
    kc = rms_norm(to_heads(kc, ATTN_KV_HEADS), k_norm_g)
    vc = to_heads(vc, ATTN_KV_HEADS)
    b = windowed_sink_attention(q, k, v, kc, vc, sink)
    c_lat, c_ctx = hgrn_mixer((hq, hi, hzf, hzb, hgate), (hqc, hic, hzfc, hzbc, hgatec),
                              lb_f, lb_b, hg_norm_g, ctx_out)
    mix = jnp.concatenate([a.astype(dt), b.astype(dt), c_lat.astype(dt)], axis=-1)
    if not ctx_out:
        return mix, None
    ac = pool_mixer(uc, pool_w, pool_scale)
    bc = context_attention(rms_norm(to_heads(qc, ATTN_HEADS), q_norm_g), kc, vc, sink)
    mixc = jnp.concatenate([ac.astype(dt), bc.astype(dt), c_ctx.astype(dt)], axis=-1)
    return mix, mixc

def expert_ffn(h, expert_idx, gate_w, w_gate, w_up, w_down):
    T, D = h.shape
    A = T * TOP_K
    flat_e = expert_idx.reshape(-1)
    order = jnp.argsort(flat_e)
    sorted_e = flat_e[order]
    counts = jnp.bincount(flat_e, length=N_EXPERTS)
    padded = ((counts + MOE_BLOCK - 1) // MOE_BLOCK) * MOE_BLOCK
    padded_end = jnp.cumsum(padded)
    padded_start = padded_end - padded
    start = jnp.cumsum(counts) - counts
    dest = padded_start[sorted_e] + (jnp.arange(A) - start[sorted_e])
    n_blocks = -(-A // MOE_BLOCK) + N_EXPERTS
    P = n_blocks * MOE_BLOCK
    token_sorted = (order // TOP_K).astype(jnp.int32)
    token_of_slot = jnp.zeros((P,), jnp.int32).at[dest].set(token_sorted)
    block_expert = jnp.minimum(
        jnp.searchsorted(padded_end, jnp.arange(n_blocks) * MOE_BLOCK, side='right'), N_EXPERTS - 1)
    xs = h[token_of_slot].reshape(n_blocks, MOE_BLOCK, D)

    def run(args):
        xb, e = args
        hid = jax.nn.silu(xb @ w_gate[e]) * (xb @ w_up[e])
        return hid @ w_down[e]

    ys = lax.map(run, (xs, block_expert)).reshape(P, D)
    contrib = ys[dest].astype(jnp.float32) * gate_w.reshape(-1)[order][:, None]
    return jax.ops.segment_sum(contrib, token_sorted, num_segments=T).astype(h.dtype)

def hier_moe(h, wg, bg, we, be, w_gate, w_up, w_down):
    T = h.shape[0]
    lg = (h @ wg + bg).astype(jnp.float32)
    pg = jax.nn.softmax(lg, axis=-1)
    _, g_idx = lax.top_k(lg, 1)
    p_grp = jnp.take_along_axis(pg, g_idx, axis=-1)
    le = (h @ we + be).astype(jnp.float32).reshape(T, N_GROUPS, EXPERTS_PER_GROUP)
    le = jnp.take_along_axis(le, g_idx[:, :, None], axis=1)[:, 0]
    pe = jax.nn.softmax(le, axis=-1)
    w_top, e_top = lax.top_k(pe, TOP_K)
    w_top = w_top / jnp.sum(w_top, axis=-1, keepdims=True)
    expert_idx = g_idx * EXPERTS_PER_GROUP + e_top
    return expert_ffn(h, expert_idx, p_grp * w_top, w_gate, w_up, w_down)

def setup_inputs(seed: int = 0) -> dict:
    key = jax.random.key(seed)
    ks = jax.random.split(key, 24)
    f32 = jnp.float32
    d = D_MODEL

    def nrm(k, shape, s):
        return jax.random.normal(k, shape, f32) * s

    return {
        'x': nrm(ks[0], (BATCH, SEQ, d), 1.0),
        'c': nrm(ks[1], (BATCH, d), 1.0),
        'ctx': nrm(ks[2], (BATCH, CTX_LEN, d), 1.0),
        'c_ctx': nrm(ks[3], (d,), 1.0),
        'norm1_g': 1.0 + nrm(ks[4], (DEPTH, d), 0.05),
        'norm2_g': 1.0 + nrm(ks[5], (DEPTH, d), 0.05),
        'ada_w': nrm(ks[6], (DEPTH, d, 6 * d), 0.5 * d ** -0.5),
        'ada_b': nrm(ks[7], (DEPTH, 6 * d), 0.02),
        'w_in': nrm(ks[8], (DEPTH, d, IN_COLS), d ** -0.5),
        'w_out': nrm(ks[9], (DEPTH, MIX_WIDTH, d), MIX_WIDTH ** -0.5),
        'pool_w': nrm(ks[10], (DEPTH, POOL_GROUPS, POOL_GROUP_DIM, POOL_GROUP_DIM), POOL_GROUP_DIM ** -0.5),
        'pool_scale': 1.0 + nrm(ks[11], (DEPTH, POOL_DIM), 0.1),
        'q_norm_g': 1.0 + nrm(ks[12], (DEPTH, HEAD_DIM), 0.05),
        'k_norm_g': 1.0 + nrm(ks[13], (DEPTH, HEAD_DIM), 0.05),
        'attn_sink': nrm(ks[14], (DEPTH, ATTN_HEADS), 0.5),
        'hgrn_lb': nrm(ks[15], (DEPTH, 2, HG_WIDTH), 0.5),
        'hgrn_norm_g': 1.0 + nrm(ks[16], (DEPTH, HG_DIM), 0.05),
        'router_group_w': nrm(ks[17], (DEPTH, d, N_GROUPS), d ** -0.5),
        'router_group_b': nrm(ks[18], (DEPTH, N_GROUPS), 0.01),
        'router_expert_w': nrm(ks[19], (DEPTH, d, N_EXPERTS), d ** -0.5),
        'router_expert_b': nrm(ks[20], (DEPTH, N_EXPERTS), 0.01),
        'expert_w_gate': nrm(ks[21], (DEPTH, N_EXPERTS, d, EXPERT_HIDDEN), d ** -0.5),
        'expert_w_up': nrm(ks[22], (DEPTH, N_EXPERTS, d, EXPERT_HIDDEN), d ** -0.5),
        'expert_w_down': nrm(ks[23], (DEPTH, N_EXPERTS, EXPERT_HIDDEN, d), EXPERT_HIDDEN ** -0.5),
    }

def reference(x, c, ctx, c_ctx, norm1_g, norm2_g, ada_w, ada_b, w_in, w_out, pool_w, pool_scale,
              q_norm_g, k_norm_g, attn_sink, hgrn_lb, hgrn_norm_g, router_group_w, router_group_b,
              router_expert_w, router_expert_b, expert_w_gate, expert_w_up, expert_w_down):
    B_, L, _ = x.shape
    C = ctx.shape[1]
    n_rows = L // GRID_W
    cos, sin = axial_rope(n_rows)
    sm = jax.nn.softmax(hgrn_lb.astype(jnp.float32), axis=0)
    lb_all = jnp.cumsum(sm, axis=0) - sm[0]
    s_lat = jax.nn.silu(c)
    s_ctx = jax.nn.silu(c_ctx)
    for l in range(DEPTH):
        ctx_out = l < DEPTH - 1
        mod = (s_lat @ ada_w[l] + ada_b[l])[:, None, :]
        modc = s_ctx @ ada_w[l] + ada_b[l]
        sh1, sc1, g1, sh2, sc2, g2 = jnp.split(mod, 6, axis=-1)
        csh1, csc1, cg1, csh2, csc2, cg2 = jnp.split(modc, 6, axis=-1)
        h = modulate(x, norm1_g[l], sh1, sc1)
        hc = modulate(ctx, norm1_g[l], csh1, csc1)
        mix, mixc = token_mixers(h @ w_in[l], hc @ w_in[l], pool_w[l], pool_scale[l], q_norm_g[l],
                                 k_norm_g[l], attn_sink[l], lb_all[l, 0], lb_all[l, 1], hgrn_norm_g[l],
                                 cos, sin, ctx_out)
        x = x + g1 * (mix @ w_out[l])
        h2 = modulate(x, norm2_g[l], sh2, sc2).reshape(B_ * L, D_MODEL)
        moe_args = (router_group_w[l], router_group_b[l], router_expert_w[l], router_expert_b[l],
                    expert_w_gate[l], expert_w_up[l], expert_w_down[l])
        if ctx_out:
            ctx = ctx + cg1 * (mixc @ w_out[l])
            h2c = modulate(ctx, norm2_g[l], csh2, csc2).reshape(B_ * C, D_MODEL)
            y = hier_moe(jnp.concatenate([h2, h2c], axis=0), *moe_args)
            x = x + g2 * y[:B_ * L].reshape(B_, L, D_MODEL)
            ctx = ctx + cg2 * y[B_ * L:].reshape(B_, C, D_MODEL)
        else:
            y = hier_moe(h2, *moe_args)
            x = x + g2 * y.reshape(B_, L, D_MODEL)
    return x


_drawn_inputs = setup_inputs


def setup_inputs(seed=0):
    import zlib

    import numpy as np

    out = dict(_drawn_inputs(seed))
    spreads = {}
    factors = {'norm1_g': 3.452,
     'q_norm_g': 8.0,
     'k_norm_g': 8.0,
     'attn_sink': 8.0,
     'hgrn_lb': 6.455,
     'hgrn_norm_g': 5.697,
     'router_group_b': 23.582,
     'router_expert_b': 23.249}
    for name, (base, spread) in spreads.items():
        noise = np.random.default_rng([zlib.crc32(name.encode()), seed]).standard_normal(out[name].shape)
        drawn = base * np.exp(spread * noise) if base else spread * noise
        out[name] = __import__('jax').numpy.asarray(drawn.astype(out[name].dtype))
    for name, factor in factors.items():
        out[name] = (out[name] * factor).astype(out[name].dtype)
    return out
```

```python
from contextlib import ExitStack

import numpy as np
import concourse.bass as bass
from concourse import mybir

F32 = mybir.dt.float32
BF16 = mybir.dt.bfloat16
I8 = mybir.dt.int8
I32 = mybir.dt.int32
U32 = mybir.dt.uint32
ALU = mybir.AluOpType
ACT = mybir.ActivationFunctionType
AX = mybir.AxisListType.X

P = 128
DEPTH = 2
D = 1024
KT = D // P
CTX = 256
SEQ = 256
T = CTX + SEQ
NT = T // P
EPS = 1e-6
IN_COLS = 2304
HEADS, HD = 8, 64
LEVELS = 7
CAP = 64
E = 32
GROUPS, EPG = 4, 8
HID = 512
SLOT = 12288
FMIN = float(2.0 ** -63)
BIG = 4096.0
NEG = -3.0e38

RH, TOK, CH, BB, KK, EL = 0, 4096, 8192, 13312, 15360, 17408
ARENA = 21504
RT, RTAB = EL, EL + 1536
NB = E + 15
NBT = 2 * NB
SC, PT, OSB = 8192, 10240, 11264
QTO, KTO, PO = 20480, 22528, 23552
WOUT = SLOT
C_ID, C_BLK, C_ONE, C_IOTA, C_TOK, C_HALF, C_COS, C_SIN, C_SEL = 0, 128, 256, 384, 448, 452, 453, 581, 709
NCF = 711
B_ID, B_ONE, B_TRI, B_BAND = 0, 128, 256, 384
NCB = 896

WIN = [("u", SLOT, 256, [(0, 256)]),
       ("kvh", SLOT + 2048, 512, [(768, 256), (1280, 256)]),
       ("q", SLOT + 6144, 512, [(256, 512)]),
       ("z", 0, 512, [(1536, 512)]),
       ("hq", 4096, 256, [(1024, 256)]),
       ("gate", 6144, 256, [(2048, 256)])]
WIN_AT = {name: (i, off, w) for i, (name, off, w, _) in enumerate(WIN)}


class Layered:

    def __init__(self, handle, total):
        self.h, self.total = handle, total

    def at(self, l, value):
        return value + l * self.total


def in_groups(l):
    out = [("u", 0, "a"), ("u", 1, "a")]
    for t in range(NT):
        out.append(("kvh", t, "v"))
        if l == 0 or t >= 2:
            out.append(("q", t, "v"))
    out += [("z", i, "a") for i in range(4)]
    out += [("hq", 0, "a"), ("hq", 1, "a"), ("gate", 0, "a"), ("gate", 1, "a")]
    return out


def backbone(nc, x_in, c_in, ctx_in, cctx_in, norm1_g, norm2_g, ada_w, ada_b, w_in, w_out, pool_w,
             pool_scale, q_norm_g, k_norm_g, attn_sink, hgrn_lb, hgrn_norm_g, rg_w, rg_b, re_w, re_b,
             ew_gate, ew_up, ew_down, const_f, const_b, const_mask, const_cnt, out):
    with ExitStack() as ctx:
        def sb(name, shape, dt=F32):
            return ctx.enter_context(nc.sbuf_tensor(name, shape, dt))

        def sem(name):
            return ctx.enter_context(nc.semaphore(name))

        def layered(name, total):
            return Layered(sem(name), total)

        def sems(name):
            return [sem(f"{name}{l}") for l in range(DEPTH)]

        x = sb("x", [P, NT, D])
        wt = sb("wt", [P, 2 * SLOT])
        ar = sb("ar", [P, ARENA])
        cf = sb("cf", [P, NCF])
        cb = sb("cb", [P, NCB], BF16)
        mask = sb("mask", [P, LEVELS, P], I8)
        mod = sb("mod", [P, DEPTH, 6, KT, 2])
        A1 = sb("A1", [P, DEPTH, KT, 2])
        A2 = sb("A2", [P, DEPTH, KT, 2])
        cols = sb("cols", [P, 62])
        lb = sb("lb", [P, 4])
        omlb = sb("omlb", [P, 4])
        lbd = sb("lbd", [P, 4])
        wr = sb("wr", [P, KT, GROUPS + E])
        rb = sb("rb", [P, GROUPS + E])
        gain = sb("gain", [P, 2, HD])
        sink = sb("sink", [P, HEADS])
        epsc = sb("epsc", [P, 1])
        ss = sb("ss", [P, NT])
        rs = sb("rs", [P, NT])
        qss = sb("qss", [P, NT, 10])
        mx = sb("mx", [P, HEADS])
        mneg = sb("mneg", [P, 2, HEADS])
        den = sb("den", [P, 2, HEADS])
        esk = sb("esk", [P, HEADS])
        dec = sb("dec", [P, 2, 2, NT])
        gw = sb("gw", [P, NT, 2])
        idg = sb("idg", [P, E + 15], U32)
        ids = sb("ids", [P, E + 15], U32)
        idgc = sb("idgc", [P, 2], U32)
        idsc = sb("idsc", [P, 2], U32)
        ovi = sb("ovi", [1, 16], I32)
        ovf = sb("ovf", [1, 16])
        halfb = sb("halfb", [P, 1])
        selb = sb("selb", [P, NT, E], BF16)
        junk = sb("junk", [P, 1])
        dmb = sb("dmb", [P, 2, NT])
        tokid = sb("tokid", [P, NT])
        ps = ctx.enter_context(nc.psum_tensor("ps", [P, 8, 512], F32))

        rows_d = nc.dram_tensor("rows_d", (P, P), F32, kind="Internal").ap()
        h2_d = [nc.dram_tensor(f"h2_d{l}", (2 * (T if l == 0 else SEQ), 512), F32, kind="Internal").ap()
                for l in range(DEPTH)]
        y_d = [nc.dram_tensor(f"y_d{l}", (4 * (T if l == 0 else SEQ), 512), F32, kind="Internal").ap()
               for l in range(DEPTH)]

        ident = cf[:, C_ID:C_ID + P]
        ones = cf[:, C_ONE:C_ONE + P]

        def a_(off, n):
            return ar[:, off:off + n]

        hT = a_(RH, 4096).rearrange("p (k t) -> p k t", k=KT)
        mixT = hT
        adrow = a_(CH + 2048, 1024).rearrange("p (b n) -> p b n", b=2)
        silc = a_(CH + 1536, 32 * KT).rearrange("p (k s) -> p k s", s=32)
        tok = a_(TOK, 4096).rearrange("p (t n) -> p t n", t=NT)
        pooled = a_(CH, 1024).rearrange("p (i t) -> p i t", i=2)
        S_st = a_(CH, 1024).rearrange("p (d t h v) -> p d t h v", d=2, t=NT, h=2)
        hq = a_(CH + 1024, 1024).rearrange("p (i t) -> p i t", i=2)
        hg = a_(CH + 2048, 1024).rearrange("p (i t) -> p i t", i=2)
        sg = a_(CH + 3072, 2048).rearrange("p (d i t) -> p d i t", d=2, i=2)
        bb = a_(BB, 2048).rearrange("p (d i t) -> p d i t", d=2, i=2)
        kk = a_(KK, 2048).rearrange("p (d i t) -> p d i t", d=2, i=2)
        el = a_(EL, 4096).rearrange("p (b s i t) -> p b s i t", b=2, s=2, i=2)
        sc = wt[:, SC:SC + 2048].rearrange("p (c h t) -> p c h t", c=NT, h=4)
        pt = wt[:, PT:PT + 1024].rearrange("p (b k t) -> p b k t", b=2, k=4)
        osb = wt[:, OSB:OSB + 512]
        qT = wt[:, QTO:QTO + 2048].rearrange("p (h t) -> p h t", h=4)
        kT = wt[:, KTO:KTO + 1024].rearrange("p (h t) -> p h t", h=2)
        prob = wt[:, PO:PO + 1024].rearrange("p (b t) -> p b t", b=2)
        qtmp = wt[:, PO:PO + 640].rearrange("p (h d) -> p h d", h=10)
        PADL = 272
        up = a_(EL, 4 * PADL)
        w2 = a_(EL + 4 * PADL, 4 * PADL)
        w4 = a_(EL + 8 * PADL, 4 * PADL)
        icnt = a_(EL + 12 * PADL, 512).rearrange("p (i t) -> p i t", i=2)
        pwbd = sb("pwbd", [P, 2, P])
        row = [[a_(o + 1024 * s, 1024) for s in range(2)] for o in (CH, CH + 2048, BB, KK)]

        xg = a_(CH, 1024).rearrange("p (b n) -> p b n", b=2)
        hs = a_(CH + 1024, 1024).rearrange("p (b j n) -> p b j n", b=2, j=4)
        ysb = a_(CH + 2048, 1024).rearrange("p (b n) -> p b n", b=2)
        sil = a_(CH + 3072, 512)
        hid = a_(CH + 3584, 256)
        hidT = a_(CH + 4096, 256).rearrange("p (j n) -> p j n", j=4)
        yb = a_(TOK, 4096).rearrange("p (b k n) -> p b k n", b=2, k=2)

        s_cf, s_cb, s_rows, s_x, s_memz, s_up0 = (sem(n) for n in ("s_cf", "s_cb", "s_rows", "s_x", "s_memz", "s_up0"))
        s_dve, s_act, s_pool = sem("s_dve"), sem("s_act"), sem("s_pool")
        s_vt, s_cols, s_silc, s_lbd, s_sig, s_lb, s_bf = (sem(n) for n in ("s_vt", "s_cols", "s_silc", "s_lbd", "s_sig", "s_lb", "s_bf"))
        s_adaw = [sem(f"s_adaw{i}") for i in range(6)]
        s_rvt, s_rv, s_rvs, s_rd = sem("s_rvt"), sem("s_rv"), sem("s_rvs"), sem("s_rd")
        s_win = [sem(f"s_win{i}") for i in range(len(WIN))]
        s_wout, s_lw = sem("s_wout"), sem("s_lw")
        s_out = sem("s_out")
        s_go = sem("s_go")
        s_ada = layered("s_ada", 12)
        s_adr = layered("s_adr", 12)
        s_adc = layered("s_adc", 12)
        s_mod = layered("s_mod", 1)
        s_ss = layered("s_ss", 4)
        s_var = layered("s_var", 1)
        s_sq = layered("s_sq", 1)
        s_xn = layered("s_xn", 4)
        s_tr = layered("s_tr", 8)
        s_trv = layered("s_trv", 4)
        s_tra = layered("s_tra", 4)
        s_ip = layered("s_ip", 18)
        s_ipa = layered("s_ipa", 10)
        s_ipv = layered("s_ipv", 8)
        s_pl = layered("s_pl", 1)
        s_ply = layered("s_ply", 2)
        s_plm = layered("s_plm", 2)
        s_qsq = layered("s_qsq", 4)
        s_qss = layered("s_qss", 4)
        s_qsd = layered("s_qsd", 2)
        s_qrs = layered("s_qrs", 1)
        s_qr = layered("s_qr", 4)
        s_qt = layered("s_qt", 5)
        s_qtv = layered("s_qtv", 4)
        s_qta = layered("s_qta", 3)
        s_f = layered("s_f", 1)
        s_g = layered("s_g", 1)
        s_b = layered("s_b", 1)
        s_elx = layered("s_elx", 7)
        s_ele = layered("s_ele", 7)
        s_elm = layered("s_elm", 8)
        s_lv = layered("s_lv", 32)
        s_sc = layered("s_sc", 32)
        s_kdx = layered("s_kdx", 1)
        s_kde = layered("s_kde", 1)
        s_kd = layered("s_kd", 2)
        s_kdt = layered("s_kdt", 4)
        s_kdc = layered("s_kdc", 4)
        s_qde = layered("s_qde", 1)
        s_qd = layered("s_qd", 1)
        s_dec = layered("s_dec", 1)
        s_U = layered("s_U", 2)
        s_S = layered("s_S", 1)
        s_o = layered("s_o", 1)
        s_osq = layered("s_osq", 2)
        s_ms = layered("s_ms", 2)
        s_r = layered("s_r", 2)
        s_hm = layered("s_hm", 2)
        s_s = layered("s_s", 32)
        s_mn = layered("s_mn", 32)
        s_e = layered("s_e", 32)
        s_p2 = layered("s_p2", 32)
        s_p2v = layered("s_p2v", 32)
        s_pv = layered("s_pv", 32)
        s_on = layered("s_on", 4)
        s_ot = layered("s_ot", 4)
        s_otc = layered("s_otc", 4)
        s_es = layered("s_es", 4)
        s_em = layered("s_em", 4)
        s_row = layered("s_row", 128)
        s_op = layered("s_op", 8)
        s_x1 = layered("s_x1", 8)
        s_ss2 = layered("s_ss2", 4)
        s_var2 = layered("s_var2", 4)
        s_sq2 = layered("s_sq2", 4)
        s_h2 = layered("s_h2", 4)
        s_h2d = layered("s_h2d", 64)
        s_t2 = layered("s_t2", 4)
        s_t2v = layered("s_t2v", 4)
        s_t2a = layered("s_t2a", 4)
        s_lg = layered("s_lg", 1)
        s_r1 = layered("s_r1", 1)
        s_r2 = layered("s_r2", 1)
        s_r3 = layered("s_r3", 1)
        s_r4 = layered("s_r4", 1)
        s_oh = layered("s_oh", 1)
        s_rk = layered("s_rk", 1)
        s_tb = layered("s_tb", 8)
        s_tbm = layered("s_tbm", 1)
        s_ix = layered("s_ix", 1)
        s_ovi = layered("s_ovi", 1)
        s_gi = layered("s_gi", 32)
        s_si = layered("s_si", 32)
        s_gt = layered("s_gt", 32)
        s_gtc = layered("s_gtc", 32)
        s_gu = layered("s_gu", 32)
        s_sil = layered("s_sil", 32)
        s_hid = layered("s_hid", 32)
        s_ht = layered("s_ht", 32)
        s_htc = layered("s_htc", 32)
        s_dn = layered("s_dn", 32)
        s_y = layered("s_y", 32)
        s_x2 = layered("s_x2", 4)
        s_wgu = [layered(f"s_wgu{q}", 512) for q in range(2)]
        s_wdn = [layered(f"s_wdn{q}", 256) for q in range(2)]
        s_xg = [layered(f"s_xg{q}", 256) for q in range(2)]
        s_scat = [layered(f"s_scat{q}", 256) for q in range(2)]
        s_ov, s_ovw, s_ovx, s_ovs = (sems(n) for n in ("s_ov", "s_ovw", "s_ovx", "s_ovs"))
        s_yl = [sem(f"s_yl{q}") for q in range(2)]
        block = ctx.enter_context(nc.Block())

        QTL = [[0, 1, 2, 3], [2, 3]]
        T0 = [0, CTX]
        TK = [T, SEQ]
        NOV = [2 * n // CAP - 1 for n in TK]
        JMAX = [n // CAP - 1 for n in TK]

        def chain(eng, s):
            n = [0]

            def link(ins):
                n[0] += 1
                ins.then_inc(s, 1)
                eng.wait_ge(s, n[0])
            return link

        def units(l, step):
            every = [(t, h) for t in QTL[l] for h in range(HEADS)]
            n = len(every) // 8
            return [(step * n + i, t, h) for i, (t, h) in enumerate(every[step * n:(step + 1) * n])]

        def seln(l):
            return selb[:, 0:len(QTL[l])]

        def count(l, n, eng):
            return sum(g[2] == eng for g in in_groups(l)[:n])

        @block.sync
        def _(sp):
            def one(w, l, e):
                return w[l, e] if type(e) is int else w[l, bass.ds(e, 1)].rearrange("o a b -> (o a) b")

            def load_gu(l, e, q, s):
                for j, w in enumerate((ew_gate, ew_up)):
                    sp.dma_start(wt[:, q * SLOT + j * 4096:q * SLOT + (j + 1) * 4096].rearrange("p (k n) -> p k n", k=KT),
                                 one(w, l, e).rearrange("(k p) n -> p k n", p=P)).then_inc(s, 16)

            def load_dn(l, e, q, s):
                sp.dma_start(wt[:, q * SLOT + 8192:(q + 1) * SLOT].rearrange("p (k n) -> p k n", k=4),
                             one(ew_down, l, e).rearrange("(k p) n -> p k n", p=P)).then_inc(s, 16)

            sp.wait_ge(s_cf, 16)
            sp.wait_ge(s_rows, 16 * 9)
            for l in range(DEPTH):
                for c in range(12):
                    if l or c >= 6:
                        if c >= 6:
                            sp.wait_ge(s_ada.h, s_ada.at(l, c - 5))
                        else:
                            sp.wait_ge(s_ada.h, s_ada.at(l - 1, c + 7))
                    q = c % 6
                    sp.dma_start(wt[:, q * 4096:(q + 1) * 4096].rearrange("p (k n) -> p k n", k=KT),
                                 ada_w[l, :, c * 512:(c + 1) * 512].rearrange("(k p) n -> p k n", p=P)
                                 ).then_inc(s_adaw[q], 16)
            for l in range(DEPTH):
                for i in (3, 4, 5, 0, 1, 2) if l == 0 else (3, 4, 5):
                    name, off, w, srcs = WIN[i]
                    if l == 0:
                        sp.wait_ge(s_ada.h, s_ada.at(1, 7 + (off + KT * w - 1) // 4096))
                    a = 0
                    for (c0, cw) in srcs:
                        sp.dma_start(wt[:, off:off + KT * w].rearrange("p (k n) -> p k n", k=KT)[:, :, a:a + cw],
                                     w_in[l, :, c0:c0 + cw].rearrange("(k p) n -> p k n", p=P)
                                     ).then_inc(s_win[i], 16)
                        a += cw
                sp.wait_ge(s_ip.h, s_ip.at(l, len(in_groups(l))))
                sp.dma_start(wt[:, WOUT:WOUT + KT * D].rearrange("p (k n) -> p k n", k=KT),
                             w_out[l].rearrange("(k p) n -> p k n", p=P)).then_inc(s_wout, 16)
                load_gu(l, 0, 0, s_wgu[0].h)
                sp.wait_ge(s_hm.h, s_hm.at(l, 2))
                if l == 0:
                    sp.wait_ge(s_rd, 16)
                for v in range(4):
                    for s in range(2):
                        if l == 0 or s == 1:
                            r0 = (l * 4 + v) * 16 + s * 8
                            sp.dma_start(row[v][s], rows_d[r0:r0 + 8, :].rearrange("a b -> (a b)").partition_broadcast(P)
                                         ).then_inc(s_row.h, 16)
                sp.wait_ge(s_otc.h, s_otc.at(l, len(QTL[l])))
                load_dn(l, 0, 0, s_wdn[0].h)
                sp.wait_ge(s_op.h, s_op.at(l, 2 * len(QTL[l])))
                load_gu(l, 1, 1, s_wgu[1].h)
                load_dn(l, 1, 1, s_wdn[1].h)
                with sp.Fori(1, E // 2) as i:
                    for q in range(2):
                        sp.wait_ge(s_gu.h, s_gu.at(l, 2 * i + q - 1))
                        load_gu(l, 2 * i + q, q, s_wgu[q].h)
                        sp.wait_ge(s_dn.h, s_dn.at(l, 2 * i + q - 1))
                        load_dn(l, 2 * i + q, q, s_wdn[q].h)
                sp.wait_ge(s_dn.h, s_dn.at(l, E - 1))
                sp.wait_ge(s_ovi.h, s_ovi.at(l, 1))
                n_ov = sp.value_load(ovi[0:1, 0:1], min_val=0, max_val=NOV[l])
                with sp.Fori(0, NOV[l]) as j:
                    with sp.If(j < n_ov):
                        e = sp.value_load(ovi[0:1, bass.ds(j + 1, 1)], min_val=0, max_val=E - 1)
                        sp.wait_ge(s_ov[l], 11 * j + 1)
                        load_gu(l, e, 0, s_ovw[l])
                        load_dn(l, e, 0, s_ovw[l])
                if l == 0:
                    sp.wait_ge(s_dn.h, s_dn.at(l, E))
                    for i in range(3):
                        name, off, w, srcs = WIN[i]
                        a = 0
                        for (c0, cw) in srcs:
                            sp.dma_start(wt[:, off:off + KT * w].rearrange("p (k n) -> p k n", k=KT)[:, :, a:a + cw],
                                         w_in[1, :, c0:c0 + cw].rearrange("(k p) n -> p k n", p=P)
                                         ).then_inc(s_win[i], 16)
                            a += cw
                for q in range(2):
                    sp.wait_ge(s_scat[q].h, s_scat[q].at(l, 16 * E // 2))
                sp.wait_ge(s_ov[l], 11 * n_ov + 1)
                for n, t in enumerate(QTL[l]):
                    if n >= 2:
                        sp.wait_ge(s_x2.h, s_x2.at(l, n - 1))
                    sp.dma_start(yb[:, n % 2], y_d[l].rearrange("(k t p two) n -> t p k (two n)", k=2, p=P, two=2)[t - T0[l] // P]
                                 ).then_inc(s_yl[n % 2], 16)
                if l == 1:
                    for n in range(2):
                        sp.wait_ge(s_x2.h, s_x2.at(l, n + 1))
                        sp.dma_start(out[0, n * P:(n + 1) * P, :], x[:, 2 + n, :]).then_inc(s_out, 16)
                    sp.wait_ge(s_out, 32)
        @block.tensor
        def _(pe):
            mm = nc.tensor.matmul
            pe.wait_ge(s_cf, 16)
            pe.wait_ge(s_rows, 16 * 9)
            nc.tensor.transpose(ps[:, 6, 0:96], ar[0:96, TOK:TOK + P], ident[0:96, 0:96])
            nc.tensor.transpose(ps[:, 6, 96:158], ar[0:62, TOK + P:TOK + 2 * P], ident[0:62, 0:62]).then_inc(s_vt, 1)
            pe.wait_ge(s_silc, 1)
            def ada(l):
                with pe.Fori(0, 2) as i:
                    for q in range(6):
                        b = q % 2
                        pe.wait_ge(s_adaw[q], 32 * l + 16 * i + 16)
                        for kk_ in range(2):
                            for g in range(4):
                                ins = mm(ps[32 * g:32 * g + 32, b, :], silc[:, 2 * g + kk_, :],
                                         wt[:, q * 4096 + (2 * g + kk_) * 512:q * 4096 + (2 * g + kk_ + 1) * 512],
                                         start=(kk_ == 0), stop=(kk_ == 1), tile_position=(0, 32 * g))
                        ins.then_inc(s_ada.h, 1)
                        pe.wait_ge(s_adr.h, s_adr.at(l, 6 * i + q + 1))
                        for j in range(4):
                            ins = mm(ps[:, 7 - l, bass.ds(i * 48 + q * 8 + j * 2, 2)], adrow[:, b, j * P:(j + 1) * P],
                                     cf[:, C_SEL:C_SEL + 2], start=True, stop=True)
                        ins.then_inc(s_adc.h, 1)
            def norm_T(l):
                pe.wait_ge(s_xn.h, s_xn.at(l, NT))
                for k in range(KT):
                    if k >= 4:
                        h = s_tra if k % 2 else s_trv
                        pe.wait_ge(h.h, h.at(l, k // 2 - 1))
                    for t in range(NT):
                        ins = nc.tensor.transpose(ps[:, k % 4, t * P:(t + 1) * P], tok[:, t, k * P:(k + 1) * P], ident)
                    ins.then_inc(s_tr.h, 1)

            ada(0)
            norm_T(0)
            pe.wait_ge(s_trv.h, s_trv.at(0, KT // 2))
            pe.wait_ge(s_tra.h, s_tra.at(0, KT // 2))
            ada(1)
            pe.wait_ge(s_rvt, 1)
            nc.tensor.transpose(ps[:, 5, 0:P], ar[:, CH:CH + P], ident).then_inc(s_rv, 1)

            for l in range(DEPTH):
                t0 = T0[l]
                if l:
                    norm_T(l)
                pe.wait_ge(s_trv.h, s_trv.at(l, KT // 2))
                pe.wait_ge(s_tra.h, s_tra.at(l, KT // 2))
                groups = in_groups(l)
                for n, (name, i, _) in enumerate(groups):
                    gi, off, w = WIN_AT[name]
                    if n >= 4:
                        e = groups[n - 4][2]
                        h = s_ipa if e == "a" else s_ipv
                        pe.wait_ge(h.h, h.at(l, count(l, n - 3, e)))
                    pe.wait_ge(s_win[gi], (l + 1) * 16 * len(WIN[gi][3]))
                    W = wt[:, off:off + KT * w].rearrange("p (k n) -> p k n", k=KT)
                    for k in range(KT):
                        if name in ("kvh", "q"):
                            ins = mm(ps[:, n % 4, :], hT[:, k, i * P:(i + 1) * P], W[:, k, :], start=(k == 0), stop=(k == KT - 1))
                        else:
                            a = 0 if name == "z" else t0
                            ins = mm(ps[:, n % 4, a:T], W[:, k, i * P:(i + 1) * P], hT[:, k, a:T], start=(k == 0), stop=(k == KT - 1))
                    ins.then_inc(s_ip.h, 1)
                pe.wait_ge(s_pl.h, s_pl.at(l, 1))
                pe.wait_ge(s_lw, 16 * 12 * (l + 1))
                for i in range(2):
                    mm(ps[:, 4 + i, t0:T], pwbd[:, i, :], pooled[:, i, t0:T], start=True, stop=True).then_inc(s_ply.h, 1)
                for j in range(5):
                    b = 4 + (j + 2) % 4
                    tiles = QTL[l] if j < 4 else range(NT)
                    pe.wait_ge(s_qr.h, s_qr.at(l, NT))
                    if j == 2 or j == 3:
                        pe.wait_ge(s_plm.h, s_plm.at(l, j - 1))
                    if j == 4:
                        pe.wait_ge(s_qtv.h, s_qtv.at(l, 1))
                    for t in tiles:
                        c0 = j * P
                        ins = nc.tensor.transpose(ps[:, b, t * P:(t + 1) * P], tok[:, t, c0:c0 + P], ident)
                    ins.then_inc(s_qt.h, 1)
                pe.wait_ge(s_qtv.h, s_qtv.at(l, 4))
                pe.wait_ge(s_qta.h, s_qta.at(l, 3))

                def attn_scores(u, t, h):
                    b = 4 + u % 2
                    r = 64 * (h % 2)
                    if u >= 2:
                        pe.wait_ge(s_e.h, s_e.at(l, u - 1))
                    n = T if t >= 2 else CTX
                    ins = mm(ps[:, b, 0:n], qT[r:r + 64, h // 2, t * P:(t + 1) * P], kT[r:r + 64, h // 4, 0:n],
                             start=True, stop=(t < 2))
                    if t >= 2:
                        ins = mm(ps[:, b, CTX:T], cb[:, B_ID:B_ID + P], cb[:, B_BAND + (t - 2) * 256:B_BAND + (t - 1) * 256],
                                 start=False, stop=True)
                    ins.then_inc(s_s.h, 1)

                def attn_transpose(u, t, h):
                    nk = 4 if t >= 2 else 2
                    pe.wait_ge(s_e.h, s_e.at(l, u + 1))
                    if u >= 1:
                        pe.wait_ge(s_p2v.h, s_p2v.at(l, u))
                    for j in range(nk):
                        ins = nc.tensor.transpose(ps[:, 6, j * P:(j + 1) * P], prob[:, u % 2, j * P:(j + 1) * P], ident)
                    ins.then_inc(s_p2.h, 1)

                def attn_pv(u, t, h):
                    nk = 4 if t >= 2 else 2
                    pe.wait_ge(s_p2v.h, s_p2v.at(l, u + 1))
                    if h == 0 and u >= HEADS:
                        pe.wait_ge(s_otc.h, s_otc.at(l, u // HEADS))
                    for j in range(nk):
                        ins = mm(ps[:, 7, h * HD:(h + 1) * HD], pt[:, u % 2, j, :],
                                 tok[:, j, 640 + 64 * (h // 4):704 + 64 * (h // 4)], start=(j == 0), stop=(j == nk - 1))
                    ins.then_inc(s_pv.h, 1)
                    if h == HEADS - 1:
                        pe.wait_ge(s_on.h, s_on.at(l, u // HEADS + 1))
                        for j in range(4):
                            ins = nc.tensor.transpose(ps[:, 7, j * P:(j + 1) * P], osb[:, j * P:(j + 1) * P], ident)
                        ins.then_inc(s_ot.h, 1)

                late = []
                for step in range(LEVELS + 1):
                    pe.wait_ge(s_elm.h, s_elm.at(l, step + 1))
                    buf = (step + 1) % 2
                    for n in range(0, len(QTL[l]), 2):
                        if step:
                            pe.wait_ge(s_sc.h, s_sc.at(l, (step - 1) * len(QTL[l]) + n + 2))
                        q = hq if step == 0 else el[:, buf, 1]
                        for j in range(4):
                            c, i = QTL[l][n] + j // 2, j % 2
                            for odd in range(2):
                                r = 64 * odd
                                ins = mm(ps[:, QTL[l][n] + odd, j * P:(j + 1) * P], el[r:r + 64, buf, 0, i, c * P:(c + 1) * P],
                                         q[r:r + 64, i, c * P:(c + 1) * P], start=True, stop=True)
                                if j == 3:
                                    ins.then_inc(s_lv.h, 1)
                    for (u, t, h) in units(l, step):
                        attn_scores(u, t, h)
                        if late:
                            attn_transpose(*late[-1])
                        if len(late) > 1:
                            attn_pv(*late[-2])
                        late.append((u, t, h))
                attn_transpose(*late[-1])
                attn_pv(*late[-2])
                attn_pv(*late[-1])
                kdT = el[:, 1].rearrange("p s i (c t) -> p (s i) c t", c=4)
                for c in range(NT):
                    pe.wait_ge(s_kd.h, s_kd.at(l, 2))
                    pe.wait_ge(s_sc.h, s_sc.at(l, 8 * len(QTL[l])))
                    for j in range(4):
                        ins = nc.tensor.transpose(ps[:, c, j * P:(j + 1) * P], sg[:, j // 2, j % 2, c * P:(c + 1) * P], ident)
                    ins.then_inc(s_kdt.h, 1)
                kdt = a_(EL + 2048, 2048).rearrange("p (c j n) -> p c j n", c=NT, j=4)
                pe.wait_ge(s_kdc.h, s_kdc.at(l, NT))
                for d in range(2):
                    for c in range(NT):
                        for h in range(4):
                            r = 64 * (h % 2)
                            o = c * P + (h // 2) * 64
                            ins = mm(ps[r:r + 64, d, o:o + 64], kdt[:, c, 2 * d + h // 2, r:r + 64],
                                     tok[:, c, 768 + 64 * h:832 + 64 * h], start=True, stop=True)
                    ins.then_inc(s_U.h, 1)
                pe.wait_ge(s_S.h, s_S.at(l, 1))
                pe.wait_ge(s_qd.h, s_qd.at(l, 1))
                qd = a_(EL, 2048).rearrange("p (d i t) -> p d i t", d=2, i=2)
                for c in QTL[l]:
                    for h in range(4):
                        r = 64 * (h % 2)
                        i = h // 2
                        o = ps[r:r + 64, 2 + i, c * P:(c + 1) * P]
                        mm(o, tok[:, c, 768 + 64 * h:832 + 64 * h], sc[:, c - c % 2 + h % 2, 2 * (c % 2) + i, :], start=True, stop=False)
                        dirs = [d for d in range(2) if c != d]
                        for d in dirs:
                            ins = mm(o, S_st[r:r + 64, d, c, i, :], qd[r:r + 64, d, i, c * P:(c + 1) * P],
                                     start=False, stop=(d == dirs[-1]))
                ins.then_inc(s_o.h, 1)
                for i in range(2):
                    pe.wait_ge(s_osq.h, s_osq.at(l, i + 1))
                    mm(ps[:, i, t0:T], cf[:, C_BLK:C_BLK + P], a_(EL + 2048 + 512 * i, 512)[:, t0:T], start=True, stop=True).then_inc(s_ms.h, 1)
                pe.wait_ge(s_hm.h, s_hm.at(l, 2))
                pe.wait_ge(s_otc.h, s_otc.at(l, len(QTL[l])))
                pe.wait_ge(s_plm.h, s_plm.at(l, 2))
                pe.wait_ge(s_wout, 16 * (l + 1))
                ta = t0 // P
                nt = NT - ta

                def h2_T(n):
                    t = ta + n
                    pe.wait_ge(s_h2.h, s_h2.at(l, n + 1))
                    if n:
                        pe.wait_ge(s_t2v.h, s_t2v.at(l, n))
                        pe.wait_ge(s_t2a.h, s_t2a.at(l, n))
                    for k in range(KT):
                        ins = nc.tensor.transpose(ps[:, k // 4, (k % 4) * P:(k % 4 + 1) * P], tok[:, t, k * P:(k + 1) * P], ident)
                    ins.then_inc(s_t2.h, 1)

                def logits(n):
                    t = ta + n
                    pe.wait_ge(s_t2v.h, s_t2v.at(l, n + 1))
                    pe.wait_ge(s_t2a.h, s_t2a.at(l, n + 1))
                    for k in range(KT):
                        ins = mm(ps[:, 2, t * 36:(t + 1) * 36], hT[:, k, t * P:(t + 1) * P], wr[:, k, :], start=(k == 0), stop=(k == KT - 1))
                    return ins

                for n, t in enumerate(QTL[l]):
                    for hf in range(2):
                        m = 2 * n + hf
                        if m >= 4:
                            pe.wait_ge(s_x1.h, s_x1.at(l, m - 3))
                        for k in range(KT):
                            ins = mm(ps[:, 4 + m % 4, :], mixT[:, k, t * P:(t + 1) * P],
                                     wt[:, WOUT + k * D + hf * 512:WOUT + k * D + (hf + 1) * 512], start=(k == 0), stop=(k == KT - 1))
                        ins.then_inc(s_op.h, 1)
                    if n >= 1:
                        h2_T(n - 1)
                    if n >= 2:
                        logits(n - 2)
                h2_T(nt - 1)
                logits(nt - 2)
                logits(nt - 1).then_inc(s_lg.h, 1)
                S = seln(l)
                pe.wait_ge(s_oh.h, s_oh.at(l, 1))
                for t in range(nt):
                    for u in range(t + 1):
                        mm(ps[:, 5, t * E:(t + 1) * E], cb[:, B_TRI:B_TRI + P] if u == t else cb[:, B_ONE:B_ONE + P], S[:, u, :],
                           start=(u == 0), stop=(u == t))
                for u in range(nt):
                    ins = mm(ps[:, 5, 128:160], cb[:, B_ONE:B_ONE + P], S[:, u, :], start=(u == 0), stop=(u == nt - 1))
                ins.then_inc(s_rk.h, 1)
                Rm, Cm = a_(RTAB, 8 * P).rearrange("p (a n) -> p a n", a=8), a_(RTAB + 8 * P, 8 * NBT).rearrange("p (a n) -> p a n", a=8)
                for a in range(2 * nt):
                    pe.wait_ge(s_tb.h, s_tb.at(l, a + 1))
                    ins = mm(ps[:, 6, 0:NBT], Rm[:, a, :], Cm[:, a, :], start=(a == 0), stop=(a == 2 * nt - 1))
                ins.then_inc(s_tbm.h, 1)

                def gather_T(q, src, s):
                    for j in range(4):
                        ins = nc.tensor.transpose(ps[:, 2, j * P:(j + 1) * P], src[:, j * P:(j + 1) * P], ident)
                    ins.then_inc(s, 1)

                def gate_up(q, w0, s):
                    for k in range(KT):
                        for u in range(2):
                            ins = mm(ps[64 * u:64 * u + 64, q, :], hs[:, q, k % 4, 64 * (k // 4):64 * (k // 4) + 64],
                                     wt[:, w0 + u * 4096 + k * 512:w0 + u * 4096 + (k + 1) * 512], start=(k == 0), stop=(k == KT - 1))
                    ins.then_inc(s, 1)

                def hid_T(s):
                    for c in range(2):
                        ins = nc.tensor.transpose(ps[:, 3, c * P:(c + 1) * P], hid[:, c * P:(c + 1) * P], ident)
                    ins.then_inc(s, 1)

                def down(q, w0, s):
                    for j in range(4):
                        for u in range(2):
                            ins = mm(ps[64 * u:64 * u + 64, 4 + q, :], hidT[:, 2 * (j % 2) + j // 2, :],
                                     wt[:, w0 + 8192 + j * D + u * 512:w0 + 8192 + j * D + (u + 1) * 512], start=(j == 0), stop=(j == 3))
                    ins.then_inc(s, 1)

                def expert(i, q, last):
                    e = 2 * i + q
                    pe.wait_ge(s_gtc.h, s_gtc.at(l, e + 1))
                    pe.wait_ge(s_wgu[q].h, s_wgu[q].at(l, 32 * i + 32))
                    gate_up(q, q * SLOT, s_gu.h)
                    if not last:
                        pe.wait_ge(s_xg[1 - q].h, s_xg[1 - q].at(l, 16 * i + 16 * (q + 1) if q == 1 else 16 * i + 16))
                        gather_T(1 - q, xg[:, 1 - q], s_gt.h)
                    pe.wait_ge(s_hid.h, s_hid.at(l, e + 1))
                    hid_T(s_ht.h)
                    pe.wait_ge(s_htc.h, s_htc.at(l, e + 1))
                    pe.wait_ge(s_wdn[q].h, s_wdn[q].at(l, 16 * i + 16))
                    if type(i) is not int or i > 0:
                        pe.wait_ge(s_y.h, s_y.at(l, e - 1))
                    down(q, q * SLOT, s_dn.h)

                pe.wait_ge(s_xg[0].h, s_xg[0].at(l, 16))
                gather_T(0, xg[:, 0], s_gt.h)
                expert(0, 0, False)
                expert(0, 1, False)
                with pe.Fori(1, E // 2 - 1) as i:
                    expert(i, 0, False)
                    expert(i, 1, False)
                expert(E // 2 - 1, 0, False)
                expert(E // 2 - 1, 1, True)
                pe.wait_ge(s_y.h, s_y.at(l, E))
                pe.wait_ge(s_ovi.h, s_ovi.at(l, 1))
                n_ov = pe.value_load(ovi[0:1, 0:1], min_val=0, max_val=NOV[l])
                with pe.Fori(0, NOV[l]) as j:
                    with pe.If(j < n_ov):
                        pe.wait_ge(s_ovx[l], 16 * j + 16)
                        gather_T(0, xg[:, 0], s_ov[l])
                        pe.wait_ge(s_ov[l], 11 * j + 4)
                        pe.wait_ge(s_ovw[l], 48 * j + 48)
                        gate_up(0, 0, s_ov[l])
                        pe.wait_ge(s_ov[l], 11 * j + 7)
                        hid_T(s_ov[l])
                        pe.wait_ge(s_ov[l], 11 * j + 9)
                        down(0, 0, s_ov[l])

        @block.scalar
        def _(act):
            A = nc.scalar.activation
            link = chain(act, s_act)
            act.dma_start(cf[:, :], const_f).then_inc(s_cf, 16)
            r0 = TOK
            act.dma_start(ar[0:96, r0:r0 + P], ada_b.rearrange("l (a p) -> (l a) p", p=P)).then_inc(s_rows, 16)
            r0 = TOK + P
            act.dma_start(ar[0:8, r0:r0 + P], cctx_in.rearrange("(a p) -> a p", p=P)).then_inc(s_rows, 16)
            act.dma_start(ar[8:16, r0:r0 + P], c_in.rearrange("b (a p) -> (b a) p", p=P)).then_inc(s_rows, 16)
            act.dma_start(ar[16:32, r0:r0 + P], norm1_g.rearrange("l (a p) -> (l a) p", p=P)).then_inc(s_rows, 16)
            act.dma_start(ar[32:48, r0:r0 + P], norm2_g.rearrange("l (a p) -> (l a) p", p=P)).then_inc(s_rows, 16)
            act.dma_start(ar[48:52, r0:r0 + P], pool_scale.rearrange("l (a p) -> (l a) p", p=P)).then_inc(s_rows, 16)
            act.dma_start(ar[52:60, r0:r0 + P], hgrn_lb.rearrange("l d (a p) -> (l d a) p", p=P)).then_inc(s_rows, 16)
            act.dma_start(ar[60:62, r0:r0 + 64], hgrn_norm_g).then_inc(s_rows, 16)
            act.dma_start(ar[60:62, r0 + 64:r0 + P], hgrn_norm_g).then_inc(s_rows, 16)
            act.dma_start(x[:, 0:2, :], ctx_in.rearrange("b (t p) n -> p (b t) n", p=P)).then_inc(s_x, 16)
            act.dma_start(x[:, 2:4, :], x_in.rearrange("b (t p) n -> p (b t) n", p=P)).then_inc(s_x, 16)
            act.dma_start(a_(EL, 640), const_b).then_inc(s_cb, 16)
            act.dma_start(a_(EL + 640, LEVELS * P), const_mask).then_inc(s_cb, 16)

            act.wait_ge(s_memz, 1)
            act.wait_ge(s_cols, 1)
            A(silc[:, :, 0:2].rearrange("p k s -> p s k"), cols[:, 0:16].rearrange("p (s k) -> p s k", s=2), ACT.Silu).then_inc(s_silc, 1)
            act.wait_ge(s_lbd, 1)
            A(lb[:, :], lbd[:, :], ACT.Sigmoid).then_inc(s_sig, 1)
            def ada_rows(l):
                with act.Fori(0, 6) as i:
                    for b in range(2):
                        act.wait_ge(s_ada.h, s_ada.at(l, 2 * i + b + 1))
                        A(adrow[:, b], ps[:, b, :], ACT.Copy).then_inc(s_adr.h, 1)

            def params(l):
                if l == 1:
                    act.wait_ge(s_ix.h, s_ix.at(0, 1))
                act.dma_start(gain[:, 0, :], q_norm_g[l].partition_broadcast(P)).then_inc(s_lw, 16)
                act.dma_start(gain[:, 1, :], k_norm_g[l].partition_broadcast(P)).then_inc(s_lw, 16)
                act.dma_start(sink[:], attn_sink[l].partition_broadcast(P)).then_inc(s_lw, 16)
                act.dma_start(rb[:, 0:GROUPS], rg_b[l].partition_broadcast(P)).then_inc(s_lw, 16)
                act.dma_start(rb[:, GROUPS:], re_b[l].partition_broadcast(P)).then_inc(s_lw, 16)
                act.dma_start(wr[:, :, 0:GROUPS], rg_w[l].rearrange("(k p) n -> p k n", p=P)).then_inc(s_lw, 16)
                act.dma_start(wr[:, :, GROUPS:], re_w[l].rearrange("(k p) n -> p k n", p=P)).then_inc(s_lw, 16)
                if l == 0:
                    act.wait_ge(s_memz, 1)
                for g in range(4):
                    r = 64 * (g % 2)
                    act.dma_start(pwbd[r:r + 64, g // 2, r:r + 64], pool_w[l, g]).then_inc(s_lw, 16)
                act.wait_ge(s_bf, 1)
                act.dma_start(icnt, const_cnt.rearrange("p (i t) -> p i t", i=2)).then_inc(s_lw, 16)

            def norm_in(l):
                if l == 0:
                    act.wait_ge(s_x, 32)
                    act.wait_ge(s_adc.h, s_adc.at(0, 12))
                for t in range(NT):
                    if l == 1:
                        act.wait_ge(s_x2.h, s_x2.at(0, t + 1))
                    if t:
                        act.wait_ge(s_ss.h, s_ss.at(l, t))
                    A(ps[:, 2:4, :].rearrange("p a n -> p (a n)"), x[:, t, :], ACT.Square, accum_out=ss[:, t:t + 1]).then_inc(s_ss.h, 1)
                act.wait_ge(s_var.h, s_var.at(l, 1))
                A(rs[:, :], ss[:, :], ACT.Sqrt).then_inc(s_sq.h, 1)
                for k in range(1, KT, 2):
                    act.wait_ge(s_tr.h, s_tr.at(l, k + 1))
                    for s in range(2):
                        ins = A(hT[:, k, s * CTX:(s + 1) * CTX], ps[:, k % 4, s * CTX:(s + 1) * CTX], ACT.Identity,
                                scale=A1[:, l, k, s:s + 1], bias=mod[:, l, 0, k, s:s + 1])
                    ins.then_inc(s_tra.h, 1)

            params(0)
            ada_rows(0)
            norm_in(0)
            ada_rows(1)
            for l in range(DEPTH):
                t0 = T0[l]
                if l:
                    params(l)
                    norm_in(l)
                act.wait_ge(s_up0, l + 1)
                for n, (name, i, e) in enumerate(in_groups(l)):
                    if e != "a":
                        continue
                    if name == "hq" and i == 0:
                        act.wait_ge(s_f.h, s_f.at(l, 1))
                        A(sg[:], sg[:], ACT.Ln).then_inc(s_g.h, 1)
                    act.wait_ge(s_ip.h, s_ip.at(l, n + 1))
                    b = n % 4
                    if name == "u":
                        v = up.rearrange("p (i s t) -> p i s t", i=2, s=2)[:, i, l:2, 8:8 + 256]
                        A(v, ps[:, b, t0:T].rearrange("p (s t) -> p s t", t=256), ACT.Copy).then_inc(s_ipa.h, 1)
                    elif name == "z":
                        A(sg[:, i // 2, i % 2, :], ps[:, b, :], ACT.Sigmoid)
                        A(kk[:, i // 2, i % 2, :], ps[:, b, :], ACT.Sigmoid, scale=-1.0).then_inc(s_ipa.h, 1)
                    else:
                        A((hq if name == "hq" else hg)[:, i, t0:T], ps[:, b, t0:T], ACT.Silu).then_inc(s_ipa.h, 1)
                    if name == "z" and i == 0:
                        act.wait_ge(s_qsd.h, s_qsd.at(l, 1))
                        A(qss[:].rearrange("p t h -> p (t h)"), qss[:].rearrange("p t h -> p (t h)"), ACT.Sqrt).then_inc(s_qrs.h, 1)
                for i in range(2):
                    act.wait_ge(s_ply.h, s_ply.at(l, i + 1))
                    A(mixT[:, i, t0:T], ps[:, 4 + i, t0:T], ACT.Copy, scale=cols[:, 48 + 2 * l + i:49 + 2 * l + i]).then_inc(s_plm.h, 1)
                for j in (1, 3):
                    act.wait_ge(s_qt.h, s_qt.at(l, j + 1))
                    A(qT[:, j, t0:T], ps[:, 4 + (j + 2) % 4, t0:T], ACT.Copy).then_inc(s_qta.h, 1)
                act.wait_ge(s_qt.h, s_qt.at(l, 5))
                A(kT[0:64, 0, :], ps[0:64, 6, :], ACT.Copy)
                A(kT[64:128, 0, :], ps[0:64, 6, :], ACT.Copy).then_inc(s_qta.h, 1)

                def softmax(u, t, h):
                    n = T if t >= 2 else CTX
                    b = u // HEADS % 2
                    act.wait_ge(s_mn.h, s_mn.at(l, u + 1))
                    if u >= 2:
                        act.wait_ge(s_p2.h, s_p2.at(l, u - 1))
                    A(prob[:, u % 2, 0:n], ps[:, 4 + u % 2, 0:n], ACT.Exp, bias=mneg[:, b, h:h + 1], scale=HD ** -0.5,
                      accum_out=den[:, b, h:h + 1]).then_inc(s_e.h, 1)

                def sink_exp(u, t, h):
                    if h == HEADS - 1:
                        act.wait_ge(s_es.h, s_es.at(l, u // HEADS + 1))
                        A(esk[:, :], esk[:, :], ACT.Exp).then_inc(s_em.h, 1)

                act.wait_ge(s_kdx.h, s_kdx.at(l, 1))
                A(sg[:], sg[:], ACT.Exp).then_inc(s_kde.h, 1)
                bc = bb[:].rearrange("p d i (c t) -> p d i c t", c=NT)
                A(dec[:, 0], bc[:, 0, :, :, P - 1], ACT.Exp)
                A(dec[:, 1], bc[:, 1, :, :, 0], ACT.Exp).then_inc(s_dec.h, 1)
                pend = None
                for step in range(LEVELS + 1):
                    if step < LEVELS:
                        act.wait_ge(s_elx.h, s_elx.at(l, step + 1))
                        v = el[:, step % 2, :, :, t0:T]
                        v = v.rearrange("p s i t -> p (s i) t")
                        A(v, v, ACT.Exp).then_inc(s_ele.h, 1)
                    for un in units(l, step):
                        softmax(*un)
                        if pend:
                            sink_exp(*pend)
                        pend = un
                sink_exp(*pend)
                act.wait_ge(s_lv.h, s_lv.at(l, 7 * len(QTL[l])))
                act.wait_ge(s_elm.h, s_elm.at(l, 8))
                qd = a_(EL, 2048).rearrange("p (j t) -> p j t", j=4)
                A(qd[:, :, t0:T], bb[:].rearrange("p d i t -> p (d i) t")[:, :, t0:T], ACT.Exp).then_inc(s_qde.h, 1)
                for i in range(2):
                    act.wait_ge(s_o.h, s_o.at(l, 1))
                    A(a_(EL + 2048 + 512 * i, 512)[:, t0:T], ps[:, 2 + i, t0:T], ACT.Square).then_inc(s_osq.h, 1)
                for i in range(2):
                    r = a_(EL + 512 * i, 512)[:, t0:T]
                    act.wait_ge(s_ms.h, s_ms.at(l, i + 1))
                    link(A(r, ps[:, i, t0:T], ACT.Ln, scale=1.0 / HD, bias=epsc[:, 0:1]))
                    A(r, r, ACT.Exp, scale=-0.5).then_inc(s_r.h, 1)
                ta = t0 // P

                def evac_h2(n):
                    act.wait_ge(s_t2.h, s_t2.at(l, n + 1))
                    A(hT[:, 4:8, t0 + n * P:t0 + (n + 1) * P], ps[:, 1, :].rearrange("p (k t) -> p k t", k=4), ACT.Copy).then_inc(s_t2a.h, 1)

                for n, t in enumerate(QTL[l]):
                    act.wait_ge(s_x1.h, s_x1.at(l, 2 * n + 2))
                    A(tok[:, t, :], x[:, t, :], ACT.Square, accum_out=ss[:, t:t + 1]).then_inc(s_ss2.h, 1)
                    act.wait_ge(s_var2.h, s_var2.at(l, n + 1))
                    A(rs[:, t:t + 1], ss[:, t:t + 1], ACT.Sqrt).then_inc(s_sq2.h, 1)
                    if n:
                        evac_h2(n - 1)
                evac_h2(len(QTL[l]) - 1)
                act.wait_ge(s_r1.h, s_r1.at(l, 1))
                g4 = a_(RT + 144, 16)[:, 4 * ta:]
                A(g4, g4, ACT.Exp).then_inc(s_r2.h, 1)
                act.wait_ge(s_r3.h, s_r3.at(l, 1))
                dv = a_(RT + 160, 4)[:, ta:]
                A(dv, dv, ACT.Exp).then_inc(s_r4.h, 1)

                def evac_hs(q, s):
                    A(hs[:, q], ps[:, 2, :].rearrange("p (j n) -> p j n", j=4), ACT.Copy).then_inc(s, 1)

                def evac_y(q, s):
                    A(ysb[:, q], ps[:, 4 + q, :], ACT.Copy).then_inc(s, 1)

                def silu(q, s):
                    A(sil[64:128, :], ps[0:64, q, :], ACT.Silu).then_inc(s, 1)

                def expert(i, q, last):
                    e = 2 * i + q
                    if not last:
                        act.wait_ge(s_gt.h, s_gt.at(l, e + 2))
                        if type(i) is not int or i > 0 or q:
                            act.wait_ge(s_gu.h, s_gu.at(l, e))
                        evac_hs(1 - q, s_gtc.h)
                    act.wait_ge(s_gu.h, s_gu.at(l, e + 1))
                    if type(i) is not int or i > 0 or q:
                        act.wait_ge(s_hid.h, s_hid.at(l, e))
                    silu(q, s_sil.h)
                    act.wait_ge(s_dn.h, s_dn.at(l, e + 1))
                    if type(i) is not int or i > 0:
                        act.wait_ge(s_scat[q].h, s_scat[q].at(l, 16 * i))
                    evac_y(q, s_y.h)

                act.wait_ge(s_gt.h, s_gt.at(l, 1))
                evac_hs(0, s_gtc.h)
                expert(0, 0, False)
                expert(0, 1, False)
                with act.Fori(1, E // 2 - 1) as i:
                    expert(i, 0, False)
                    expert(i, 1, False)
                expert(E // 2 - 1, 0, False)
                expert(E // 2 - 1, 1, True)
                act.wait_ge(s_scat[0].h, s_scat[0].at(l, 16 * E // 2))
                n_ov = act.value_load(ovi[0:1, 0:1], min_val=0, max_val=NOV[l])
                with act.Fori(0, NOV[l]) as j:
                    with act.If(j < n_ov):
                        act.wait_ge(s_ov[l], 11 * j + 3)
                        evac_hs(0, s_ov[l])
                        act.wait_ge(s_ov[l], 11 * j + 5)
                        silu(0, s_ov[l])
                        act.wait_ge(s_ov[l], 11 * j + 10)
                        evac_y(0, s_ov[l])

        @block.vector
        def _(v):
            V = nc.vector
            link = chain(v, s_dve)
            V.memset(epsc[:], EPS)
            V.memset(cb[:, B_ONE:B_ONE + P], 1.0)
            V.memset(silc[:], 0.0)
            V.memset(pwbd[:], 0.0).then_inc(s_memz, 1)
            v.wait_ge(s_vt, 1)
            V.tensor_copy(a_(CH + 1024, 96), ps[:, 6, 0:96])
            V.tensor_copy(cols[:], ps[:, 6, 96:158]).then_inc(s_cols, 1)
            v.wait_ge(s_cols, 1)
            V.tensor_tensor(lbd[:], cols[:, 56:60], cols[:, 52:56], ALU.subtract).then_inc(s_lbd, 1)
            v.wait_ge(s_sig, 1)
            V.tensor_scalar(omlb[:], lb[:], -1.0, 1.0, ALU.mult, ALU.add).then_inc(s_lb, 1)
            v.wait_ge(s_cf, 16)
            v.wait_ge(s_cb, 32)
            V.tensor_scalar(halfb[:], cf[:, C_HALF:C_HALF + 1], 2.0 * BIG, None, ALU.add)
            V.tensor_copy(cb[:, B_ID:B_ID + P], ident)
            V.tensor_copy(mask[:].rearrange("p l t -> p (l t)"), a_(EL + 640, LEVELS * P))
            V.tensor_copy(cb[:, B_TRI:], a_(EL, 640)).then_inc(s_bf, 1)
            rv = a_(CH, P).rearrange("p (l v s k) -> p l v s k", l=2, v=4, s=2)

            def modulation(l):
                v.wait_ge(s_adc.h, s_adc.at(l, 12))
                m = mod[:, l].rearrange("p a k s -> p (a k) s")
                link(V.tensor_tensor(m, ps[:, 7 - l, 0:96].rearrange("p (a s) -> p a s", s=2),
                                     a_(CH + 1024 + 48 * l, 48).unsqueeze(2).to_broadcast([P, 48, 2]), ALU.add))
                for (Ax, part, g0) in ((A1, 1, 16), (A2, 4, 32)):
                    g = cols[:, g0 + 8 * l:g0 + 8 * l + 8].unsqueeze(2).to_broadcast([P, KT, 2])
                    ins = V.scalar_tensor_tensor(out=Ax[:, l], in0=mod[:, l, part], scalar=1.0, in1=g, op0=ALU.add, op1=ALU.mult)
                ins.then_inc(s_mod.h, 1)
                v.wait_ge(s_mod.h, s_mod.at(l, 1))
                for i, src in enumerate((mod[:, l, 2], A2[:, l], mod[:, l, 3], mod[:, l, 5])):
                    ins = V.tensor_copy(rv[:, l, i], src.rearrange("p k s -> p s k"))
                return ins

            def norm_in(l):
                v.wait_ge(s_ss.h, s_ss.at(l, NT))
                V.tensor_scalar(ss[:], ss[:], 1.0 / D, EPS, ALU.mult, ALU.add).then_inc(s_var.h, 1)
                v.wait_ge(s_sq.h, s_sq.at(l, 1))
                link(V.reciprocal(rs[:], rs[:]))
                for t in range(NT):
                    V.tensor_scalar(tok[:, t, :], x[:, t, :], rs[:, t:t + 1], None, ALU.mult).then_inc(s_xn.h, 1)
                for k in range(0, KT, 2):
                    v.wait_ge(s_tr.h, s_tr.at(l, k + 1))
                    for s in range(2):
                        ins = V.tensor_scalar(hT[:, k, s * CTX:(s + 1) * CTX], ps[:, k % 4, s * CTX:(s + 1) * CTX],
                                              A1[:, l, k, s:s + 1], mod[:, l, 0, k, s:s + 1], ALU.mult, ALU.add)
                    ins.then_inc(s_trv.h, 1)

            modulation(0)
            norm_in(0)
            modulation(1).then_inc(s_rvt, 1)
            v.wait_ge(s_rv, 1)
            V.tensor_copy(a_(CH + 128, P), ps[:, 5, 0:P]).then_inc(s_rvs, 1)
            for l in range(DEPTH):
                t0 = T0[l]
                if l:
                    norm_in(l)
                for n, (name, i, e) in enumerate(in_groups(l)):
                    if e != "v":
                        continue
                    v.wait_ge(s_ip.h, s_ip.at(l, n + 1))
                    dst = tok[:, i, 512:1024] if name == "kvh" else tok[:, i, 0:512]
                    V.tensor_copy(dst, ps[:, n % 4, :]).then_inc(s_ipv.h, 1)
                for t in range(NT):
                    v.wait_ge(s_qsq.h, s_qsq.at(l, t + 1))
                    h0 = 0 if l == 0 or t >= 2 else 8
                    V.tensor_reduce(qss[:, t, h0:], qtmp[:, h0:, :], AX, ALU.add).then_inc(s_qss.h, 1)
                v.wait_ge(s_qss.h, s_qss.at(l, NT))
                q40 = qss[:].rearrange("p t h -> p (t h)")
                V.tensor_scalar(q40, q40, 1.0 / HD, EPS, ALU.mult, ALU.add).then_inc(s_qsd.h, 1)
                v.wait_ge(s_qrs.h, s_qrs.at(l, 1))
                V.reciprocal(q40, q40).then_inc(s_qsd.h, 1)
                v.wait_ge(s_ipa.h, s_ipa.at(l, count(l, len(in_groups(l)) - 4, "a")))
                if l == 1:
                    for d in range(2):
                        for i in range(2):
                            j = 2 * d + i
                            V.tensor_scalar(sg[:, d, i], sg[:, d, i], omlb[:, j:j + 1], lb[:, j:j + 1], ALU.mult, ALU.add)
                            link(V.tensor_scalar(kk[:, d, i], kk[:, d, i], omlb[:, j:j + 1], None, ALU.mult))
                V.tensor_scalar(sg[:], sg[:], FMIN, None, ALU.max).then_inc(s_f.h, 1)
                v.wait_ge(s_g.h, s_g.at(l, 1))
                for d in range(2):
                    for i in range(2):
                        for c in range(NT):
                            s = slice(c * P, (c + 1) * P)
                            ins = V.tensor_tensor_scan(bb[:, d, i, s], ones, sg[:, d, i, s], 0.0, ALU.mult, ALU.add)
                link(ins)
                bc = bb[:].rearrange("p d i (c t) -> p d (i c) t", c=NT)
                sgc = sg[:].rearrange("p d i (c t) -> p d (i c) t", c=NT)
                link(V.tensor_tensor(sgc[:, 1], sgc[:, 1], bc[:, 1], ALU.subtract))
                tot = den[:].rearrange("p a b -> p (a b)")[:, 0:8]
                link(V.tensor_copy(tot, bc[:, 1, :, P - 1]))
                V.tensor_tensor(bc[:, 1], sgc[:, 1], tot.unsqueeze(2).to_broadcast([P, 8, P]), ALU.add).then_inc(s_b.h, 1)
                v.wait_ge(s_b.h, s_b.at(l, 1))
                for d in range(2):
                    e = bc[:, d, :, P - 1] if d == 0 else bc[:, d, :, 0]
                    ins = V.tensor_tensor(sgc[:, d], e.unsqueeze(2).to_broadcast([P, 8, P]), bc[:, d], ALU.subtract)
                ins.then_inc(s_kdx.h, 1)
                for j in (0, 2):
                    v.wait_ge(s_qt.h, s_qt.at(l, j + 1))
                    V.tensor_copy(qT[:, j, t0:T], ps[:, 4 + (j + 2) % 4, t0:T]).then_inc(s_qtv.h, 1)
                v.wait_ge(s_qt.h, s_qt.at(l, 5))
                V.tensor_copy(kT[0:64, 1, :], ps[64:128, 6, :]).then_inc(s_qtv.h, 1)
                V.tensor_copy(kT[64:128, 1, :], ps[64:128, 6, :]).then_inc(s_qtv.h, 1)

                def rowmax(u, t, h):
                    n = T if t >= 2 else CTX
                    b = u // HEADS % 2
                    v.wait_ge(s_s.h, s_s.at(l, u + 1))
                    link(V.reduce_max(mx[:, h:h + 1], ps[:, 4 + u % 2, 0:n], AX))
                    link(V.tensor_scalar(mx[:, h:h + 1], mx[:, h:h + 1], HD ** -0.5, sink[:, h:h + 1], ALU.mult, ALU.max))
                    V.tensor_scalar(mneg[:, b, h:h + 1], mx[:, h:h + 1], -1.0, None, ALU.mult).then_inc(s_mn.h, 1)

                def evac_p(u, t, h):
                    nk = 4 if t >= 2 else 2
                    v.wait_ge(s_p2.h, s_p2.at(l, u + 1))
                    if u >= 2:
                        v.wait_ge(s_pv.h, s_pv.at(l, u - 1))
                    V.tensor_copy(pt[:, u % 2, 0:nk, :], ps[:, 6, 0:nk * P].rearrange("p (k t) -> p k t", k=nk)).then_inc(s_p2v.h, 1)

                def finish(u, t, h):
                    if h == HEADS - 1:
                        w = u // HEADS
                        b = w % 2
                        v.wait_ge(s_mn.h, s_mn.at(l, u + 1))
                        if w:
                            v.wait_ge(s_em.h, s_em.at(l, w))
                        V.tensor_tensor(esk[:], sink[:], mneg[:, b], ALU.add).then_inc(s_es.h, 1)
                        v.wait_ge(s_em.h, s_em.at(l, w + 1))
                        v.wait_ge(s_e.h, s_e.at(l, u + 1))
                        link(V.tensor_tensor(den[:, b], den[:, b], esk[:], ALU.add))
                        link(V.reciprocal(den[:, b], den[:, b]))
                        v.wait_ge(s_pv.h, s_pv.at(l, u + 1))
                        V.tensor_tensor(osb.rearrange("p (h d) -> p h d", h=HEADS), ps[:, 7, :].rearrange("p (h d) -> p h d", h=HEADS),
                                        den[:, b].unsqueeze(2).to_broadcast([P, HEADS, HD]), ALU.mult).then_inc(s_on.h, 1)
                        v.wait_ge(s_ot.h, s_ot.at(l, w + 1))
                        V.tensor_copy(mixT[:, 2:6, t * P:(t + 1) * P], ps[:, 7, :].rearrange("p (j t) -> p j t", j=4)).then_inc(s_otc.h, 1)

                v.wait_ge(s_lw, 16 * 12 * (l + 1))
                v.wait_ge(s_ipa.h, s_ipa.at(l, count(l, len(in_groups(l)), "a")))
                V.tensor_tensor(el[:, 1, 0, :, t0:T], kk[:, 0, :, t0:T], kk[:, 1, :, t0:T], ALU.add).then_inc(s_elm.h, 1)
                late = []

                def operands(step):
                    b = (step + 1) % 2
                    m = 1 << (step - 1)
                    v.wait_ge(s_ele.h, s_ele.at(l, step))

                    def halves(a):
                        return a.rearrange("p i (n h m) -> p i n h m", h=2, m=m)
                    K = halves(el[:, b, 0, :, t0:T])
                    kf, kb = halves(kk[:, 0, :, t0:T]), halves(kk[:, 1, :, t0:T])
                    V.tensor_tensor(K[:, :, :, 0, :], K[:, :, :, 0, :], kf[:, :, :, 0, :], ALU.mult)
                    V.tensor_tensor(K[:, :, :, 1, :], K[:, :, :, 1, :], kb[:, :, :, 1, :], ALU.mult)
                    V.tensor_tensor(el[:, b, 1, :, t0:T], el[:, b, 1, :, t0:T], hq[:, :, t0:T], ALU.mult).then_inc(s_elm.h, 1)

                for step in range(LEVELS + 1):
                    for n, c in enumerate(QTL[l]):
                        v.wait_ge(s_lv.h, s_lv.at(l, step * len(QTL[l]) + n + 1))
                        src = ps[:, c, :].rearrange("p (h t) -> p h t", h=4)
                        if step == 0:
                            V.tensor_tensor(sc[:, c], src, ident.unsqueeze(1).to_broadcast([P, 4, P]), ALU.mult).then_inc(s_sc.h, 1)
                        else:
                            if n == 0:
                                v.wait_ge(s_sc.h, s_sc.at(l, step * len(QTL[l])))
                            V.copy_predicated(sc[:, c], mask[:, step - 1].unsqueeze(1).to_broadcast([P, 4, P]), src).then_inc(s_sc.h, 1)
                    for n, un in enumerate(units(l, step)):
                        rowmax(*un)
                        if late:
                            evac_p(*late[-1])
                        if len(late) > 1:
                            finish(*late[-2])
                        late.append(un)
                        if n == 0 and step < LEVELS:
                            operands(step + 1)
                evac_p(*late[-1])
                finish(*late[-2])
                finish(*late[-1])
                v.wait_ge(s_kde.h, s_kde.at(l, 1))
                for d in range(2):
                    V.tensor_tensor(sg[:, d], sg[:, d], kk[:, d], ALU.mult).then_inc(s_kd.h, 1)
                v.wait_ge(s_qde.h, s_qde.at(l, 1))
                qd = a_(EL, 2048).rearrange("p (d i t) -> p d i t", d=2, i=2)
                for d in range(2):
                    ins = V.tensor_tensor(qd[:, d, :, t0:T], qd[:, d, :, t0:T], hq[:, :, t0:T], ALU.mult)
                ins.then_inc(s_qd.h, 1)
                kdt = a_(EL + 2048, 2048).rearrange("p (c n) -> p c n", c=NT)
                for c in range(NT):
                    v.wait_ge(s_kdt.h, s_kdt.at(l, c + 1))
                    V.tensor_copy(kdt[:, c], ps[:, c, :]).then_inc(s_kdc.h, 1)
                v.wait_ge(s_U.h, s_U.at(l, 2))
                v.wait_ge(s_dec.h, s_dec.at(l, 1))
                for d, order in ((0, (0, 1, 2, 3)), (1, (1, 0, 3, 2))):
                    U = ps[:, d, :].rearrange("p (c i v) -> p c i v", c=NT, i=2)
                    link(V.tensor_copy(S_st[:, d, order[1]], U[:, order[0]]))
                    for a, b in ((order[1], order[2]), (order[2], order[3])):
                        for i in range(2):
                            ins = V.scalar_tensor_tensor(out=S_st[:, d, b, i], in0=S_st[:, d, a, i], scalar=dec[:, d, i, a:a + 1],
                                                         in1=U[:, a, i], op0=ALU.mult, op1=ALU.add)
                        link(ins)
                V.tensor_copy(mx[:, 0:1], epsc[:, 0:1]).then_inc(s_S.h, 1)
                for i in range(2):
                    r = a_(EL + 512 * i, 512)[:, t0:T]
                    v.wait_ge(s_r.h, s_r.at(l, i + 1))
                    link(V.tensor_tensor(r, r, ps[:, 2 + i, t0:T], ALU.mult))
                    V.scalar_tensor_tensor(out=mixT[:, 6 + i, t0:T], in0=r, scalar=cols[:, 60 + l:61 + l], in1=hg[:, i, t0:T],
                                           op0=ALU.mult, op1=ALU.mult).then_inc(s_hm.h, 1)
                v.wait_ge(s_row.h, s_row.at(l, 16 * (8 if l == 0 else 4)))
                def evac_h2(n):
                    v.wait_ge(s_t2.h, s_t2.at(l, n + 1))
                    V.tensor_copy(hT[:, 0:4, t0 + n * P:t0 + (n + 1) * P], ps[:, 0, :].rearrange("p (k t) -> p k t", k=4)).then_inc(s_t2v.h, 1)

                for n, t in enumerate(QTL[l]):
                    for hf in range(2):
                        m = 2 * n + hf
                        tmp = a_(EL + 1024 + 512 * (m % 2), 512)
                        v.wait_ge(s_op.h, s_op.at(l, m + 1))
                        link(V.tensor_tensor(tmp, ps[:, 4 + m % 4, :], row[0][t // 2][:, hf * 512:(hf + 1) * 512], ALU.mult))
                        V.tensor_tensor(x[:, t, hf * 512:(hf + 1) * 512], x[:, t, hf * 512:(hf + 1) * 512], tmp, ALU.add).then_inc(s_x1.h, 1)
                    v.wait_ge(s_ss2.h, s_ss2.at(l, n + 1))
                    V.tensor_scalar(ss[:, t:t + 1], ss[:, t:t + 1], 1.0 / D, EPS, ALU.mult, ALU.add).then_inc(s_var2.h, 1)
                    v.wait_ge(s_sq2.h, s_sq2.at(l, n + 1))
                    link(V.reciprocal(rs[:, t:t + 1], rs[:, t:t + 1]))
                    link(V.scalar_tensor_tensor(out=tok[:, t, :], in0=x[:, t, :], scalar=rs[:, t:t + 1], in1=row[1][t // 2], op0=ALU.mult, op1=ALU.mult))
                    V.tensor_tensor(tok[:, t, :], tok[:, t, :], row[2][t // 2], ALU.add).then_inc(s_h2.h, 1)
                    if n:
                        evac_h2(n - 1)
                evac_h2(len(QTL[l]) - 1)
                ta = t0 // P
                nt = NT - ta

                iota = cf[:, C_IOTA:C_IOTA + 64]

                def rt(off, n):
                    return a_(RT + off, n)
                L = rt(0, 36 * nt).rearrange("p (t n) -> p t n", t=nt)
                v.wait_ge(s_lg.h, s_lg.at(l, 1))
                link(V.tensor_tensor(L, ps[:, 2, 36 * ta:144].rearrange("p (t n) -> p t n", t=nt), rb[:].unsqueeze(1).to_broadcast([P, nt, 36]), ALU.add))
                g8 = rt(200, 8 * nt).rearrange("p (t n) -> p t n", t=nt)
                link(V.memset(g8, NEG))
                link(V.tensor_copy(g8[:, :, 0:4], L[:, :, 0:4]))
                gm = rt(240, 8 * nt).rearrange("p (t n) -> p t n", t=nt)
                gi = rt(280, 8 * nt).bitcast(U32).rearrange("p (t n) -> p t n", t=nt)
                for t in range(nt):
                    ins = V.max(gm[:, t], g8[:, t])
                link(ins)
                for t in range(nt):
                    ins = V.max_index(gi[:, t], gm[:, t], g8[:, t])
                link(ins)
                ex = rt(144, 16)[:, 4 * ta:].rearrange("p (t n) -> p t n", t=nt)
                V.tensor_tensor(ex, L[:, :, 0:4], gm[:, :, 0:1].to_broadcast([P, nt, 4]), ALU.subtract).then_inc(s_r1.h, 1)
                gidx = rt(320, nt)
                link(V.tensor_copy(gidx, gi[:, :, 0]))
                oh4 = rt(324, 4 * nt).rearrange("p (t n) -> p t n", t=nt)
                link(V.tensor_tensor(oh4, iota[:, 0:4].unsqueeze(1).to_broadcast([P, nt, 4]), gidx.unsqueeze(2).to_broadcast([P, nt, 4]), ALU.is_equal))
                sel = rt(340, 32 * nt)
                link(V.tensor_tensor(sel.rearrange("p (t g e) -> p t g e", t=nt, g=4), L[:, :, 4:36].rearrange("p t (g e) -> p t g e", g=4),
                                     oh4.unsqueeze(3).to_broadcast([P, nt, 4, 8]), ALU.mult))
                le = rt(468, 8 * nt).rearrange("p (t n) -> p t n", t=nt)
                link(V.tensor_reduce(le, sel.rearrange("p (t g e) -> p t e g", t=nt, g=4), AX, ALU.add))
                lm = rt(500, 8 * nt).rearrange("p (t n) -> p t n", t=nt)
                li = rt(532, 8 * nt).bitcast(U32).rearrange("p (t n) -> p t n", t=nt)
                for t in range(nt):
                    ins = V.max(lm[:, t], le[:, t])
                link(ins)
                for t in range(nt):
                    ins = V.max_index(li[:, t], lm[:, t], le[:, t])
                link(ins)
                dv = rt(160, 4)[:, ta:]
                V.tensor_tensor(dv, lm[:, :, 1], lm[:, :, 0], ALU.subtract).then_inc(s_r3.h, 1)
                eid = rt(564, 2 * nt).rearrange("p (k t) -> p k t", k=2)
                link(V.tensor_copy(eid, li[:, :, 0:2].rearrange("p t k -> p k t")))
                link(V.scalar_tensor_tensor(out=eid, in0=gidx.unsqueeze(1).to_broadcast([P, 2, nt]), scalar=8.0, in1=eid, op0=ALU.mult, op1=ALU.add))
                oh = rt(572, 64 * nt).rearrange("p (k t e) -> p k t e", k=2, t=nt)
                for k in range(2):
                    ins = V.tensor_tensor(oh[:, k], iota[:, 0:E].unsqueeze(1).to_broadcast([P, nt, E]), eid[:, k].unsqueeze(2).to_broadcast([P, nt, E]), ALU.is_equal)
                link(ins)
                V.tensor_tensor(seln(l), oh[:, 0], oh[:, 1], ALU.add).then_inc(s_oh.h, 1)
                pg = rt(828, nt)
                v.wait_ge(s_r2.h, s_r2.at(l, 1))
                link(V.tensor_reduce(pg, ex, AX, ALU.add))
                link(V.reciprocal(pg, pg))
                v.wait_ge(s_r4.h, s_r4.at(l, 1))
                w0 = rt(832, nt)
                link(V.tensor_scalar(w0, dv, 1.0, None, ALU.add))
                link(V.reciprocal(w0, w0))
                link(V.tensor_tensor(gw[:, ta:, 0], w0, pg, ALU.mult))
                V.tensor_tensor(gw[:, ta:, 1], gw[:, ta:, 0], dv, ALU.mult)
                V.tensor_scalar(tokid[:, ta:], cf[:, C_TOK + ta:C_TOK + NT], -float(t0), None, ALU.add)
                for k in range(2):
                    V.tensor_scalar(dmb[:, k, ta:], cf[:, C_TOK + ta:C_TOK + NT], k * TK[l] - t0 - BIG, None, ALU.add)
                J = JMAX[l]
                thr = rt(836, J)
                link(V.tensor_scalar(thr, iota[:, 1:J + 1], float(CAP), None, ALU.mult))
                v.wait_ge(s_rk.h, s_rk.at(l, 1))
                big = rt(900, E * 15)
                cnt = rt(844, E)
                link(V.tensor_copy(cnt, ps[:, 5, 128:160]))
                cmpj = big[:, 0:E * J].rearrange("p (e j) -> p e j", j=J)
                link(V.tensor_tensor(cmpj, cnt.unsqueeze(2).to_broadcast([P, E, J]), thr.unsqueeze(1).to_broadcast([P, E, J]), ALU.is_gt))
                nov = rt(1400, E)
                link(V.tensor_reduce(nov, cmpj, AX, ALU.add))
                inc = rt(1432, E)
                link(V.tensor_tensor_scan(inc, ones[:, 0:E], nov, 0.0, ALU.mult, ALU.add))
                base = rt(1464, E)
                link(V.tensor_tensor(base, inc, nov, ALU.subtract))
                rk = rt(1496, 2 * nt)
                bs = rt(1504, 2 * nt)
                prod = rt(900, 64 * nt).rearrange("p (k t e) -> p k t e", k=2, t=nt)
                for k in range(2):
                    ins = V.tensor_tensor(prod[:, k], oh[:, k], ps[:, 5, 0:E * nt].rearrange("p (t e) -> p t e", t=nt), ALU.mult)
                link(ins)
                link(V.tensor_reduce(rk, prod.rearrange("p k t e -> p (k t) e"), AX, ALU.add))
                link(V.tensor_tensor(prod.rearrange("p k t e -> p (k t) e"), oh.rearrange("p k t e -> p (k t) e"), base.unsqueeze(1).to_broadcast([P, 2 * nt, E]), ALU.mult))
                link(V.tensor_reduce(bs, prod.rearrange("p k t e -> p (k t) e"), AX, ALU.add))
                cj = big[:, 0:2 * nt * J].rearrange("p (a j) -> p a j", j=J)
                link(V.tensor_tensor(cj, rk.unsqueeze(2).to_broadcast([P, 2 * nt, J]), thr.unsqueeze(1).to_broadcast([P, 2 * nt, J]), ALU.is_ge))
                blk = rt(1512, 2 * nt)
                link(V.tensor_reduce(blk, cj, AX, ALU.add))
                slot = rt(1520, 2 * nt)
                V.scalar_tensor_tensor(out=slot, in0=blk, scalar=-float(CAP), in1=rk, op0=ALU.mult, op1=ALU.add)
                ef = eid.rearrange("p k t -> p (k t)")
                link(V.tensor_tensor(bs, bs, blk, ALU.add))
                link(V.scalar_tensor_tensor(out=bs, in0=bs, scalar=float(E - 1), in1=ef, op0=ALU.add, op1=ALU.subtract))
                link(V.tensor_scalar(blk, blk, 1.0, None, ALU.min))
                link(V.tensor_tensor(bs, bs, blk, ALU.mult))
                link(V.tensor_tensor(bs, bs, ef, ALU.add))
                Rm, Cm = a_(RTAB, 8 * P).rearrange("p (a n) -> p a n", a=8), a_(RTAB + 8 * P, 8 * NBT).rearrange("p (a n) -> p a n", a=8)
                for a in range(2 * nt):
                    k, t = a // nt, ta + a % nt
                    V.tensor_scalar(Rm[:, a, 0:64], iota, slot[:, a:a + 1], None, ALU.is_equal)
                    V.tensor_scalar(Rm[:, a, 64:128], iota, slot[:, a:a + 1], None, ALU.is_equal)
                    V.tensor_scalar(Cm[:, a, 0:NB], iota[:, 0:NB], bs[:, a:a + 1], tokid[:, t:t + 1], ALU.is_equal, ALU.mult)
                    V.tensor_scalar(Cm[:, a, NB:NBT], iota[:, 0:NB], bs[:, a:a + 1], dmb[:, k, t:t + 1], ALU.is_equal, ALU.mult).then_inc(s_tb.h, 1)
                m1 = big[0:1, 0:E * 15].rearrange("p (j e) -> p j e", e=E)
                m2 = a_(RTAB + 1776, E * 15)[0:1].rearrange("p (j e) -> p j e", e=E)
                jj = iota[0:1, 0:15].unsqueeze(2).to_broadcast([1, 15, E])
                V.tensor_tensor(m2, inc[0:1].unsqueeze(1).to_broadcast([1, 15, E]), jj, ALU.is_gt)
                link(V.tensor_tensor(m1, base[0:1].unsqueeze(1).to_broadcast([1, 15, E]), jj, ALU.is_le))
                link(V.tensor_tensor(m1, m1, m2, ALU.mult))
                link(V.tensor_tensor(m1, m1, iota[0:1, 0:E].unsqueeze(1).to_broadcast([1, 15, E]), ALU.mult))
                V.tensor_reduce(ovf[:, 1:16], m1, AX, ALU.add)
                link(V.tensor_copy(ovf[:, 0:1], inc[0:1, E - 1:E]))
                V.tensor_copy(ovi[:], ovf[:]).then_inc(s_ovi.h, 1)
                v.wait_ge(s_tbm.h, s_tbm.at(l, 1))
                V.tensor_scalar(idg[:], ps[:, 6, 0:NB], 2.0, cf[:, C_HALF:C_HALF + 1], ALU.mult, ALU.add)
                V.tensor_scalar(ids[:], ps[:, 6, NB:NBT], 2.0, halfb[:, 0:1], ALU.mult, ALU.add).then_inc(s_ix.h, 1)

                def hidden(q, s):
                    V.tensor_tensor(hid[0:64, :], sil[64:128, 0:256], ps[64:128, q, 0:256], ALU.mult)
                    V.tensor_tensor(hid[64:128, :], sil[64:128, 256:512], ps[64:128, q, 256:512], ALU.mult).then_inc(s, 1)

                def evac_hT(s):
                    V.tensor_copy(hidT[:], ps[:, 3, 0:256].rearrange("p (j n) -> p j n", j=4)).then_inc(s, 1)

                def expert(i, q):
                    e = 2 * i + q
                    v.wait_ge(s_sil.h, s_sil.at(l, e + 1))
                    if type(i) is not int or i > 0 or q:
                        v.wait_ge(s_ht.h, s_ht.at(l, e))
                    hidden(q, s_hid.h)
                    v.wait_ge(s_ht.h, s_ht.at(l, e + 1))
                    if type(i) is not int or i > 0 or q:
                        v.wait_ge(s_dn.h, s_dn.at(l, e))
                    evac_hT(s_htc.h)

                expert(0, 0)
                expert(0, 1)
                with v.Fori(1, E // 2) as i:
                    expert(i, 0)
                    expert(i, 1)
                v.wait_ge(s_dn.h, s_dn.at(l, E))
                v.wait_ge(s_ovi.h, s_ovi.at(l, 1))
                n_ov = v.value_load(ovi[0:1, 0:1], min_val=0, max_val=NOV[l])
                with v.Fori(0, NOV[l]) as j:
                    with v.If(j < n_ov):
                        v.wait_ge(s_ov[l], 11 * j + 6)
                        hidden(0, s_ov[l])
                        v.wait_ge(s_ov[l], 11 * j + 8)
                        evac_hT(s_ov[l])
                for n, t in enumerate(QTL[l]):
                    v.wait_ge(s_yl[n % 2], 16 * (n // 2 + 1 + 2 * l))
                    y0, y1 = yb[:, n % 2, 0], yb[:, n % 2, 1]
                    link(V.tensor_scalar(y0, y0, gw[:, t, 0:1], None, ALU.mult))
                    link(V.scalar_tensor_tensor(out=y0, in0=y1, scalar=gw[:, t, 1:2], in1=y0, op0=ALU.mult, op1=ALU.add))
                    link(V.tensor_tensor(y0, y0, row[3][t // 2], ALU.mult))
                    V.tensor_tensor(x[:, t, :], x[:, t, :], y0, ALU.add).then_inc(s_x2.h, 1)

        @block.gpsimd
        def _(g):
            G = nc.gpsimd
            link = chain(g, s_pool)
            for l in range(DEPTH):
                t0 = T0[l]
                if l == 1:
                    g.wait_ge(s_ix.h, s_ix.at(0, 1))
                if l == 0:
                    g.wait_ge(s_rvs, 1)
                    g.dma_start(rows_d, a_(CH + 128, P)).then_inc(s_rd, 16)
                    g.wait_ge(s_bf, 1)
                G.memset(up, 0.0).then_inc(s_up0, 1)
                g.wait_ge(s_ipa.h, s_ipa.at(l, 2))
                N = 4 * PADL
                link(G.tensor_tensor(w2[:, 0:N - 1], up[:, 0:N - 1], up[:, 1:N], ALU.add))
                link(G.tensor_tensor(w4[:, 0:N - 3], w2[:, 0:N - 3], w2[:, 2:N - 1], ALU.add))
                g.wait_ge(s_lw, 16 * 12 * (l + 1))
                if l == 0:
                    g.wait_ge(s_rd, 16)
                U4 = up.rearrange("p (i s t) -> p i s t", i=2, s=2)
                dst = pooled[:].rearrange("p i (s t) -> p i s t", s=2)

                def group(gi, src, w):
                    r, i = 64 * (gi % 2), gi // 2
                    a = 8 - (w - 1) // 2
                    s = src.rearrange("p (i s t) -> p i s t", i=2, s=2)[r:r + 64, i, l:2, a:a + 256]
                    ic = icnt[r:r + 64, i, :].unsqueeze(1).to_broadcast([64, 2 - l, 256])
                    link(G.tensor_tensor(dst[r:r + 64, i, l:2], s, ic, ALU.mult))
                    return G.tensor_tensor(dst[r:r + 64, i, l:2], dst[r:r + 64, i, l:2], U4[r:r + 64, i, l:2, 8:264], ALU.subtract)
                link(group(0, w2, 2))
                link(group(1, w4, 4))
                link(G.tensor_tensor(w2[:, 0:N - 7], w4[:, 0:N - 7], w4[:, 4:N - 3], ALU.add))
                link(group(2, w2, 8))
                link(G.tensor_tensor(w4[:, 0:N - 15], w2[:, 0:N - 15], w2[:, 8:N - 7], ALU.add))
                group(3, w4, 16).then_inc(s_pl.h, 1)
                g.wait_ge(s_pl.h, s_pl.at(l, 1))
                for t in range(NT):
                    h0 = 0 if l == 0 or t >= 2 else 8
                    nv = sum(1 for name, i, e in in_groups(l) if e == "v" and i <= t)
                    g.wait_ge(s_ipv.h, s_ipv.at(l, nv))
                    if t:
                        g.wait_ge(s_qss.h, s_qss.at(l, t))
                    qk = tok[:, t, 0:640].rearrange("p (h d) -> p h d", h=10)
                    G.tensor_tensor(qtmp[:, h0:], qk[:, h0:], qk[:, h0:], ALU.mult).then_inc(s_qsq.h, 1)
                g.wait_ge(s_qsd.h, s_qsd.at(l, 2))
                for t in range(NT):
                    h0 = 0 if l == 0 or t >= 2 else 8
                    qk = tok[:, t, 0:640].rearrange("p (h d) -> p h d", h=10)
                    ins = link(G.tensor_tensor(qk[:, h0:], qk[:, h0:], qss[:, t, h0:].unsqueeze(2).to_broadcast([P, 10 - h0, HD]), ALU.mult))
                    if h0 == 0:
                        G.tensor_tensor(qk[:, 0:8], qk[:, 0:8], gain[:, 0, :].unsqueeze(1).to_broadcast([P, 8, HD]), ALU.mult)
                    ins = G.tensor_tensor(qk[:, 8:], qk[:, 8:], gain[:, 1, :].unsqueeze(1).to_broadcast([P, 2, HD]), ALU.mult)
                    if t < 2:
                        ins.then_inc(s_qr.h, 1)
                    else:
                        link(ins)
                        cos = cf[:, C_COS + 64 * (t - 2):C_COS + 64 * (t - 1)]
                        sin = cf[:, C_SIN + 64 * (t - 2):C_SIN + 64 * (t - 1)]
                        G.tensor_tensor(qtmp[:, :, 0:32], qk[:, :, 32:64], sin[:, 0:32].unsqueeze(1).to_broadcast([P, 10, 32]), ALU.mult)
                        link(G.tensor_tensor(qtmp[:, :, 32:64], qk[:, :, 0:32], sin[:, 32:64].unsqueeze(1).to_broadcast([P, 10, 32]), ALU.mult))
                        link(G.tensor_tensor(qk, qk, cos.unsqueeze(1).to_broadcast([P, 10, HD]), ALU.mult))
                        G.tensor_tensor(qk, qk, qtmp, ALU.add).then_inc(s_qr.h, 1)
                g.wait_ge(s_b.h, s_b.at(l, 1))
                g.wait_ge(s_pl.h, s_pl.at(l, 1))
                for step in range(1, LEVELS + 1):
                    b = (step + 1) % 2
                    m = 1 << (step - 1)
                    nb = (T - t0) // (2 * m)
                    if step >= 2:
                        g.wait_ge(s_lv.h, s_lv.at(l, (step - 1) * len(QTL[l])))

                    def halves(a):
                        return a.rearrange("p i (n h m) -> p i n h m", h=2, m=m)
                    K, Q = halves(el[:, b, 0, :, t0:T]), halves(el[:, b, 1, :, t0:T])
                    bf, bw = halves(bb[:, 0, :, t0:T]), halves(bb[:, 1, :, t0:T])
                    rf = bf[:, :, :, 0, m - 1:m].to_broadcast([P, 2, nb, m])
                    rw = bw[:, :, :, 1, 0:1].to_broadcast([P, 2, nb, m])
                    G.tensor_tensor(K[:, :, :, 0, :], rf, bf[:, :, :, 0, :], ALU.subtract)
                    G.tensor_tensor(K[:, :, :, 1, :], rw, bw[:, :, :, 1, :], ALU.subtract)
                    G.tensor_tensor(Q[:, :, :, 1, :], bf[:, :, :, 1, :], rf, ALU.subtract)
                    G.tensor_tensor(Q[:, :, :, 0, :], bw[:, :, :, 0, :], rw, ALU.subtract).then_inc(s_elx.h, 1)
                for n, t in enumerate(QTL[l]):
                    g.wait_ge(s_h2.h, s_h2.at(l, n + 1))
                    g.dma_start(h2_d[l].rearrange("(t p two) n -> t p (two n)", p=P, two=2)[n], tok[:, t, :]).then_inc(s_h2d.h, 16)
                g.wait_ge(s_h2d.h, s_h2d.at(l, 16 * len(QTL[l])))
                g.wait_ge(s_ix.h, s_ix.at(l, 1))
                rows = 2 * TK[l]

                def gather(e, q, s):
                    G.tensor_copy(idgc[:, q:q + 1], idg[:, e:e + 1] if type(e) is int else idg[:, bass.ds(e, 1)]).then_inc(s_gi.h, 1)
                    g.wait_ge(s_gi.h, s_gi.at(l, e + 1))
                    g.sem_inc(s_go, 1)
                    gather_dma(q, s)

                def gather_dma(q, s):
                    g.indirect_dma_start(xg[:, q], None, h2_d[l], bass.IndirectOffsetOnAxis(ap=idgc[:, q:q + 1], axis=0),
                                         bounds_check=rows - 1, oob_is_err=False).then_inc(s, 16)

                def scatter(e, q, s):
                    G.tensor_copy(idsc[:, q:q + 1], ids[:, e:e + 1] if type(e) is int else ids[:, bass.ds(e, 1)]).then_inc(s_si.h, 1)
                    g.wait_ge(s_si.h, s_si.at(l, e + 1))
                    g.sem_inc(s_go, 1)
                    scatter_dma(q, s)

                def scatter_dma(q, s):
                    g.indirect_dma_start(y_d[l], bass.IndirectOffsetOnAxis(ap=idsc[:, q:q + 1], axis=0), ysb[:, q], None,
                                         bounds_check=2 * rows - 1, oob_is_err=False).then_inc(s, 16)

                def expert(i, q, last):
                    e = 2 * i + q
                    g.wait_ge(s_y.h, s_y.at(l, e + 1))
                    if type(i) is not int or i > 0:
                        g.wait_ge(s_scat[q].h, s_scat[q].at(l, 16 * i))
                    scatter(e, q, s_scat[q].h)
                    if not last:
                        g.wait_ge(s_gt.h, s_gt.at(l, e + 1))
                        g.wait_ge(s_xg[q].h, s_xg[q].at(l, 16 * i + 16))
                        gather(e + 2, q, s_xg[q].h)

                G.memset(junk[:], 0.0).then_inc(s_ov[l], 1)
                gather(0, 0, s_xg[0].h)
                gather(1, 1, s_xg[1].h)
                expert(0, 0, False)
                expert(0, 1, False)
                with g.Fori(1, E // 2 - 1) as i:
                    expert(i, 0, False)
                    expert(i, 1, False)
                expert(E // 2 - 1, 0, True)
                expert(E // 2 - 1, 1, True)
                g.wait_ge(s_scat[0].h, s_scat[0].at(l, 16 * E // 2))
                n_ov = g.value_load(ovi[0:1, 0:1], min_val=0, max_val=NOV[l])
                with g.Fori(0, NOV[l]) as j:
                    with g.If(j < n_ov):
                        g.wait_ge(s_ov[l], 11 * j + 1)
                        G.tensor_copy(idsc[:, 0:1], ids[:, bass.ds(j + E, 1)])
                        G.tensor_copy(idgc[:, 0:1], idg[:, bass.ds(j + E, 1)]).then_inc(s_ov[l], 1)
                        g.wait_ge(s_ov[l], 11 * j + 2)
                        g.sem_inc(s_go, 1)
                        gather_dma(0, s_ovx[l])
                        g.wait_ge(s_ov[l], 11 * j + 11)
                        g.sem_inc(s_go, 1)
                        scatter_dma(0, s_ovs[l])
                        g.wait_ge(s_ovs[l], 16 * j + 16)
                        G.tensor_tensor(junk[:], epsc[:], epsc[:], ALU.mult).then_inc(s_ov[l], 1)



def constants():
    cf = np.zeros((P, NCF), np.float32)
    cf[:, C_ID:C_ID + P] = np.eye(P)
    cf[:64, C_BLK:C_BLK + 64] = 1
    cf[64:, C_BLK + 64:C_BLK + P] = 1
    cf[:, C_ONE:C_ONE + P] = 1
    cf[:, C_IOTA:C_IOTA + 64] = np.arange(64)
    cf[:, C_TOK:C_TOK + NT] = np.arange(P)[:, None] + P * np.arange(NT)
    cf[:, C_HALF] = np.arange(P) // 64
    cf[0::32, C_SEL] = 1
    cf[1::32, C_SEL + 1] = 1
    pos = np.arange(SEQ)
    inv = (np.float32(10000.0) ** (-np.arange(0, 32, 2, dtype=np.float32) / np.float32(32))).astype(np.float32)
    ang = np.concatenate([(pos // 64).astype(np.float32)[:, None] * inv, (pos % 64).astype(np.float32)[:, None] * inv], 1)
    cos, sin = np.cos(ang).astype(np.float32), np.sin(ang).astype(np.float32)
    cos2 = np.concatenate([cos, cos], 1).reshape(2, P, 64)
    sin2 = np.concatenate([-sin, sin], 1).reshape(2, P, 64)
    cf[:, C_COS:C_COS + P] = cos2.transpose(1, 0, 2).reshape(P, P)
    cf[:, C_SIN:C_SIN + P] = sin2.transpose(1, 0, 2).reshape(P, P)
    cb = np.zeros((P, 640), np.float32)
    cb[:, 0:P] = np.arange(P)[:, None] < np.arange(P)[None, :]
    for b in range(2):
        q = b * P + np.arange(P)[:, None]
        cb[:, P + 256 * b:P + 256 * (b + 1)] = np.where(np.abs(q - np.arange(256)[None, :]) <= 128, 0.0, -1e30)
    mk = np.zeros((P, LEVELS, P), np.float32)
    i = np.arange(P)
    for s in range(LEVELS):
        m = 1 << s
        same = (i[:, None] // (2 * m)) == (i[None, :] // (2 * m))
        mk[:, s] = same & ((i[:, None] // m) != (i[None, :] // m))
    cnt = np.zeros((P, 2, 256), np.float32)
    t = np.arange(256)
    for gi, w in enumerate((2, 4, 8, 16)):
        lo, hi = np.clip(t - (w - 1) // 2, 0, 256), np.clip(t + w // 2 + 1, 0, 256)
        cnt[64 * (gi % 2):64 * (gi % 2) + 64, gi // 2] = np.float32(1) / (hi - lo).astype(np.float32)
    return {"const_f": cf, "const_b": cb, "const_mask": mk.reshape(P, -1), "const_cnt": cnt.reshape(P, -1)}


_INS = ["x", "c", "ctx", "c_ctx", "norm1_g", "norm2_g", "ada_w", "ada_b", "w_in", "w_out", "pool_w", "pool_scale",
        "q_norm_g", "k_norm_g", "attn_sink", "hgrn_lb", "hgrn_norm_g", "router_group_w", "router_group_b",
        "router_expert_w", "router_expert_b", "expert_w_gate", "expert_w_up", "expert_w_down"]


def kernel(**inputs):
    import concourse.bacc as bacc
    from concourse.bass_utils import run_bass_kernel_spmd

    nc = bacc.Bacc("TRN2", target_bir_lowering=False, num_devices=1)
    arrays, args = {}, []
    given = {**{n: inputs[n] for n in _INS}, **constants()}
    for name, a in given.items():
        a = np.ascontiguousarray(a)
        arrays[f"in_{name}"] = a
        args.append(nc.dram_tensor(f"in_{name}", a.shape, mybir.dt.from_np(a.dtype), kind="ExternalInput").ap())
    out = nc.dram_tensor("out", (1, SEQ, D), F32, kind="ExternalOutput").ap()
    backbone(nc, *args, out)
    r = run_bass_kernel_spmd(nc, [arrays], core_ids=[0])
    return r.results[0]["out"]
```

```python
from contextlib import ExitStack

import numpy as np
import concourse.bass as bass
from concourse import mybir

F32 = mybir.dt.float32
BF16 = mybir.dt.bfloat16
I8 = mybir.dt.int8
I32 = mybir.dt.int32
U32 = mybir.dt.uint32
ALU = mybir.AluOpType
ACT = mybir.ActivationFunctionType
AX = mybir.AxisListType.X

P = 128
DEPTH = 2
D = 1024
KT = D // P
CTX = 256
SEQ = 256
T = CTX + SEQ
NT = T // P
EPS = 1e-6
IN_COLS = 2304
HEADS, HD = 8, 64
LEVELS = 7
CAP = 64
E = 32
GROUPS, EPG = 4, 8
HID = 512
SLOT = 12288
FMIN = float(2.0 ** -63)
BIG = 4096.0
NEG = -3.0e38

RH, TOK, CH, BB, KK, EL = 0, 4096, 8192, 13312, 15360, 17408
ARENA = 21504
RT, RTAB = EL, EL + 1536
NB = E + 15
NBT = 2 * NB
SC, DG, PT = 8192, 10240, 0
QTO, KTO, PO = 20480, 22528, 23552
WOUT = SLOT
C_ID, C_BLK, C_ONE, C_IOTA, C_TOK, C_HALF, C_COS, C_SIN, C_SEL = 0, 128, 256, 384, 448, 452, 453, 581, 709
NCF = 711
B_ID, B_ONE, B_TRI, B_BAND = 0, 128, 256, 384
NCB = 896

WIN = [("u", SLOT, 256, [(0, 256)]),
       ("kvh", SLOT + 2048, 512, [(768, 256), (1280, 256)]),
       ("q", SLOT + 6144, 512, [(256, 512)]),
       ("z", 0, 512, [(1536, 512)]),
       ("hq", 4096, 256, [(1024, 256)]),
       ("gate", 6144, 256, [(2048, 256)])]
WIN_AT = {name: (i, off, w) for i, (name, off, w, _) in enumerate(WIN)}


UPFRONT = 6
LATE = [(0, c) for c in range(UPFRONT, 12)] + [(1, c) for c in range(12)]


class Layered:

    def __init__(self, handle, total):
        self.h, self.total = handle, total

    def at(self, l, value):
        return value + l * self.total


def in_groups(l):
    out = [("u", 0, "a"), ("u", 1, "a")]
    for t in range(NT):
        out.append(("kvh", t, "v"))
        if l == 0 or t >= 2:
            out.append(("q", t, "v"))
    out += [("z", i, "a") for i in range(4)]
    out += [("hq", 0, "a"), ("hq", 1, "a"), ("gate", 0, "a"), ("gate", 1, "a")]
    return out


def backbone(nc, x_in, c_in, ctx_in, cctx_in, norm1_g, norm2_g, ada_w, ada_b, w_in, w_out, pool_w,
             pool_scale, q_norm_g, k_norm_g, attn_sink, hgrn_lb, hgrn_norm_g, rg_w, rg_b, re_w, re_b,
             ew_gate, ew_up, ew_down, const_f, const_b, const_mask, const_cnt, out):
    with ExitStack() as ctx:
        def sb(name, shape, dt=F32):
            return ctx.enter_context(nc.sbuf_tensor(name, shape, dt))

        def sem(name):
            return ctx.enter_context(nc.semaphore(name))

        def layered(name, total):
            return Layered(sem(name), total)

        def sems(name):
            return [sem(f"{name}{l}") for l in range(DEPTH)]

        x = sb("x", [P, NT, D])
        wt = sb("wt", [P, 2 * SLOT])
        ar = sb("ar", [P, ARENA])
        cf = sb("cf", [P, NCF])
        cb = sb("cb", [P, NCB], BF16)
        mask = sb("mask", [P, LEVELS, P], I8)
        mod = sb("mod", [P, DEPTH, 6, KT, 2])
        A1 = sb("A1", [P, DEPTH, KT, 2])
        A2 = sb("A2", [P, DEPTH, KT, 2])
        cols = sb("cols", [P, 62])
        lb = sb("lb", [P, 4])
        omlb = sb("omlb", [P, 4])
        lbd = sb("lbd", [P, 4])
        wr = sb("wr", [P, KT, GROUPS + E])
        rb = sb("rb", [P, GROUPS + E])
        gain = sb("gain", [P, 2, HD])
        sink = sb("sink", [P, HEADS])
        epsc = sb("epsc", [P, 1])
        ss = sb("ss", [P, NT])
        rs = sb("rs", [P, NT])
        qss = sb("qss", [P, NT, 10])
        mx = sb("mx", [P, HEADS])
        mneg = sb("mneg", [P, 2, HEADS])
        den = sb("den", [P, 2, HEADS])
        esk = sb("esk", [P, HEADS])
        nsink = sb("nsink", [P, HEADS])
        dec = sb("dec", [P, 2, 2, NT])
        gw = sb("gw", [P, NT, 2])
        idg = sb("idg", [P, E + 15], U32)
        ids = sb("ids", [P, E + 15], U32)
        idgc = sb("idgc", [P, 2], U32)
        idsc = sb("idsc", [P, 2], U32)
        ovi = sb("ovi", [1, 16], I32)
        ovf = sb("ovf", [1, 16])
        halfb = sb("halfb", [P, 1])
        selb = sb("selb", [P, NT, E], BF16)
        junk = sb("junk", [P, 1])
        dmb = sb("dmb", [P, 2, NT])
        tokid = sb("tokid", [P, NT])
        ps = ctx.enter_context(nc.psum_tensor("ps", [P, 8, 512], F32))

        rows_d = nc.dram_tensor("rows_d", (P, P), F32, kind="Internal").ap()
        h2_d = [nc.dram_tensor(f"h2_d{l}", (2 * (T if l == 0 else SEQ), 512), F32, kind="Internal").ap()
                for l in range(DEPTH)]
        y_d = [nc.dram_tensor(f"y_d{l}", (4 * (T if l == 0 else SEQ), 512), F32, kind="Internal").ap()
               for l in range(DEPTH)]

        ident = cf[:, C_ID:C_ID + P]
        ones = cf[:, C_ONE:C_ONE + P]

        def a_(off, n):
            return ar[:, off:off + n]

        hT = a_(RH, 4096).rearrange("p (k t) -> p k t", k=KT)
        mixT = hT
        adrow = [r.rearrange("p (b n) -> p b n", b=2) for r in (a_(CH + 2048, 1024), wt[:, KTO:KTO + 1024])]
        adab = [sb("adab0", [P, 48])[:], a_(EL + 4032, 48)]
        rvc = a_(RH + 6 * T, 2 * P)
        silc = a_(EL + 3776, 32 * KT).rearrange("p (k s) -> p k s", s=32)
        tok = a_(TOK, 4096).rearrange("p (t n) -> p t n", t=NT)
        pooled = a_(CH, 1024).rearrange("p (i t) -> p i t", i=2)
        S_st = a_(CH, 1024).rearrange("p (d t h v) -> p d t h v", d=2, t=NT, h=2)
        hq = a_(CH + 1024, 1024).rearrange("p (i t) -> p i t", i=2)
        hg = a_(CH + 2048, 1024).rearrange("p (i t) -> p i t", i=2)
        sg = a_(CH + 3072, 2048).rearrange("p (d i t) -> p d i t", d=2, i=2)
        bb = a_(BB, 2048).rearrange("p (d i t) -> p d i t", d=2, i=2)
        kk = a_(KK, 2048).rearrange("p (d i t) -> p d i t", d=2, i=2)
        el = a_(EL, 4096).rearrange("p (b s i t) -> p b s i t", b=2, s=2, i=2)
        sc = wt[:, SC:SC + 2048].rearrange("p (c h t) -> p c h t", c=NT, h=4)
        pt = wt[:, PT:PT + 8192].rearrange("p (b k h t) -> p b k h t", b=2, k=4, h=HEADS)
        diag = wt[:, DG:DG + 2 * P].rearrange("p (b t) -> p b t", b=2)
        qT = wt[:, QTO:QTO + 2048].rearrange("p (h t) -> p h t", h=4)
        kT = wt[:, KTO:KTO + 1024].rearrange("p (h t) -> p h t", h=2)
        prob = wt[:, PO:PO + 1024].rearrange("p (b t) -> p b t", b=2)
        qtmp = wt[:, PO:PO + 640].rearrange("p (h d) -> p h d", h=10)
        PADL = 272
        up = a_(EL, 4 * PADL)
        w2 = a_(EL + 4 * PADL, 4 * PADL)
        w4 = a_(EL + 8 * PADL, 4 * PADL)
        icnt = a_(EL + 12 * PADL, 512).rearrange("p (i t) -> p i t", i=2)
        pwbd = sb("pwbd", [P, 2, P])
        row = [[a_(o + 1024 * s, 1024) for s in range(2)] for o in (BB, CH, CH + 2048, KK)]

        xg = a_(CH, 1024).rearrange("p (b n) -> p b n", b=2)
        hs = a_(CH + 1024, 1024).rearrange("p (b j n) -> p b j n", b=2, j=4)
        ysb = a_(CH + 2048, 1024).rearrange("p (b n) -> p b n", b=2)
        sil = a_(CH + 3072, 512)
        hid = a_(CH + 3584, 256)
        hidT = a_(CH + 4096, 256).rearrange("p (j n) -> p j n", j=4)
        yb = [a_(o, 2048).rearrange("p (k n) -> p k n", k=2) for o in (TOK, TOK + 2048, CH, CH + 2048)]

        s_cf, s_cb, s_rows, s_x, s_memz, s_up0 = (sem(n) for n in ("s_cf", "s_cb", "s_rows", "s_x", "s_memz", "s_up0"))
        s_dve, s_act, s_pool = sem("s_dve"), sem("s_act"), sem("s_pool")
        s_vt, s_cols, s_silc, s_lbd, s_sig, s_lb, s_bf = (sem(n) for n in ("s_vt", "s_cols", "s_silc", "s_lbd", "s_sig", "s_lb", "s_bf"))
        s_adaw = [sem(f"s_adaw{i}") for i in range(6)]
        s_adw1, s_adh = sem("s_adw1"), sem("s_adh")
        s_rvt, s_rv, s_rvs, s_rd = sem("s_rvt"), sem("s_rv"), sem("s_rvs"), sem("s_rd")
        s_win = [sem(f"s_win{i}") for i in range(len(WIN))]
        s_wout, s_lw = sem("s_wout"), sem("s_lw")
        s_out = sem("s_out")
        s_go = sem("s_go")
        s_ada = layered("s_ada", 12)
        s_adr = layered("s_adr", 12)
        s_adc = layered("s_adc", 12)
        s_mod = layered("s_mod", 1)
        s_ss = layered("s_ss", 4)
        s_var = layered("s_var", 1)
        s_sq = layered("s_sq", 1)
        s_xn = layered("s_xn", 4)
        s_tr = layered("s_tr", 8)
        s_trv = layered("s_trv", 4)
        s_tra = layered("s_tra", 4)
        s_ip = layered("s_ip", 18)
        s_ipa = layered("s_ipa", 10)
        s_ipv = layered("s_ipv", 8)
        s_pl = layered("s_pl", 1)
        s_ply = layered("s_ply", 2)
        s_plm = layered("s_plm", 2)
        s_qsq = layered("s_qsq", 4)
        s_qss = layered("s_qss", 4)
        s_qsd = layered("s_qsd", 2)
        s_qrs = layered("s_qrs", 1)
        s_qr = layered("s_qr", 4)
        s_qt = layered("s_qt", 5)
        s_qtv = layered("s_qtv", 4)
        s_qta = layered("s_qta", 3)
        s_f = layered("s_f", 1)
        s_g = layered("s_g", 1)
        s_b = layered("s_b", 1)
        s_elx = layered("s_elx", 7)
        s_ele = layered("s_ele", 7)
        s_elm = layered("s_elm", 8)
        s_elq = layered("s_elq", 7)
        s_lv = layered("s_lv", 32)
        s_sc = layered("s_sc", 32)
        s_kdx = layered("s_kdx", 1)
        s_kde = layered("s_kde", 1)
        s_kd = layered("s_kd", 2)
        s_kdt = layered("s_kdt", 4)
        s_kdc = layered("s_kdc", 4)
        s_qde = layered("s_qde", 1)
        s_qd = layered("s_qd", 1)
        s_dec = layered("s_dec", 1)
        s_U = layered("s_U", 2)
        s_S = layered("s_S", 1)
        s_o = layered("s_o", 1)
        s_osq = layered("s_osq", 2)
        s_ms = layered("s_ms", 2)
        s_r = layered("s_r", 1)
        s_hm = layered("s_hm", 2)
        s_s = layered("s_s", 32)
        s_mn = layered("s_mn", 32)
        s_e = layered("s_e", 32)
        s_p2 = layered("s_p2", 32)
        s_p2v = layered("s_p2v", 32)
        s_dg = layered("s_dg", 32)
        s_pv = layered("s_pv", 4)
        s_otc = layered("s_otc", 4)
        s_row1 = layered("s_row1", 32)
        s_row = layered("s_row", 96)
        s_op = layered("s_op", 8)
        s_x1 = layered("s_x1", 8)
        s_ss2 = layered("s_ss2", 4)
        s_var2 = layered("s_var2", 4)
        s_sq2 = layered("s_sq2", 4)
        s_h2 = layered("s_h2", 4)
        s_h2d = layered("s_h2d", 64)
        s_t2 = layered("s_t2", 4)
        s_t2v = layered("s_t2v", 4)
        s_t2a = layered("s_t2a", 4)
        s_lg = layered("s_lg", 1)
        s_r1 = layered("s_r1", 1)
        s_r2 = layered("s_r2", 1)
        s_r3 = layered("s_r3", 1)
        s_r4 = layered("s_r4", 1)
        s_oh = layered("s_oh", 1)
        s_rk = layered("s_rk", 1)
        s_tb = layered("s_tb", 1)
        s_tbm = layered("s_tbm", 1)
        s_ix = layered("s_ix", 1)
        s_ovi = layered("s_ovi", 1)
        s_gi = layered("s_gi", 32)
        s_si = layered("s_si", 32)
        s_gt = layered("s_gt", 32)
        s_gtc = layered("s_gtc", 32)
        s_gu = layered("s_gu", 32)
        s_sil = layered("s_sil", 32)
        s_hid = layered("s_hid", 32)
        s_ht = layered("s_ht", 32)
        s_htc = layered("s_htc", 32)
        s_dn = layered("s_dn", 32)
        s_y = layered("s_y", 32)
        s_c0 = layered("s_c0", 4)
        s_c1 = layered("s_c1", 4)
        s_x2 = layered("s_x2", 4)
        s_wgu = [layered(f"s_wgu{q}", 512) for q in range(2)]
        s_wdn = [layered(f"s_wdn{q}", 256) for q in range(2)]
        s_xg = [layered(f"s_xg{q}", 256) for q in range(2)]
        s_scat = [layered(f"s_scat{q}", 256) for q in range(2)]
        s_ov, s_ovw, s_ovx, s_ovs = (sems(n) for n in ("s_ov", "s_ovw", "s_ovx", "s_ovs"))
        s_yl = [sem(f"s_yl{n}") for n in range(NT)]
        block = ctx.enter_context(nc.Block())

        QTL = [[0, 1, 2, 3], [2, 3]]
        T0 = [0, CTX]
        TK = [T, SEQ]
        NOV = [2 * n // CAP - 1 for n in TK]
        JMAX = [n // CAP - 1 for n in TK]

        def chain(eng, s):
            n = [0]

            def link(ins):
                n[0] += 1
                ins.then_inc(s, 1)
                eng.wait_ge(s, n[0])
            return link

        def units(l, step):
            every = [(t, h) for t in QTL[l] for h in range(HEADS)]
            n = len(every) // 8
            return [(step * n + i, t, h) for i, (t, h) in enumerate(every[step * n:(step + 1) * n])]

        def seln(l):
            return selb[:, 0:len(QTL[l])]

        def count(l, n, eng):
            return sum(g[2] == eng for g in in_groups(l)[:n])

        @block.sync
        def _(sp):
            def one(w, l, e):
                return w[l, e] if type(e) is int else w[l, bass.ds(e, 1)].rearrange("o a b -> (o a) b")

            def load_gu(l, e, q, s):
                for j, w in enumerate((ew_gate, ew_up)):
                    sp.dma_start(wt[:, q * SLOT + j * 4096:q * SLOT + (j + 1) * 4096].rearrange("p (k n) -> p k n", k=KT),
                                 one(w, l, e).rearrange("(k p) n -> p k n", p=P)).then_inc(s, 16)

            def load_dn(l, e, q, s):
                sp.dma_start(wt[:, q * SLOT + 8192:(q + 1) * SLOT].rearrange("p (k n) -> p k n", k=4),
                             one(ew_down, l, e).rearrange("(k p) n -> p k n", p=P)).then_inc(s, 16)

            def load_win(l, i):
                name, off, w, srcs = WIN[i]
                a = 0
                for (c0, cw) in srcs:
                    sp.dma_start(wt[:, off:off + KT * w].rearrange("p (k n) -> p k n", k=KT)[:, :, a:a + cw],
                                 w_in[l, :, c0:c0 + cw].rearrange("(k p) n -> p k n", p=P)
                                 ).then_inc(s_win[i], 16)
                    a += cw

            sp.wait_ge(s_cf, 16)
            sp.wait_ge(s_rows, 16 * 9)
            def load_ada(l, c, q):
                return sp.dma_start(wt[:, q * 4096:(q + 1) * 4096].rearrange("p (k n) -> p k n", k=KT),
                                    ada_w[l, :, c * 512:(c + 1) * 512].rearrange("(k p) n -> p k n", p=P))

            for c in range(UPFRONT):
                load_ada(0, c, (c + 3) % 6).then_inc(s_adaw[c], 16)

            def load_late(k):
                l, c = LATE[k]
                for half, s in enumerate((s_adh, s_ada.h)):
                    sp.wait_ge(s, UPFRONT + k)
                    a = 2 * 4096 + 2048 * half
                    sp.dma_start(wt[:, a:a + 2048].rearrange("p (k n) -> p k n", k=4),
                                 ada_w[l, 512 * half:512 * half + 512, c * 512:(c + 1) * 512].rearrange("(k p) n -> p k n", p=P)
                                 ).then_inc(s_adw1, 16)

            for l in range(DEPTH):
                for i in range(6):
                    if l == 0:
                        name, off, w, _ = WIN[i]
                        sp.wait_ge(s_ada.h, s_ada.at(0, 1 + ((off + KT * w - 1) // 4096 + 3) % 6))
                    load_win(l, i)
                    if l == 0 and i >= 2:
                        load_late(i - 2)
                if l == 0:
                    for k in range(4, len(LATE)):
                        load_late(k)
                sp.wait_ge(s_ip.h, s_ip.at(l, len(in_groups(l))))
                sp.dma_start(wt[:, WOUT:WOUT + KT * D].rearrange("p (k n) -> p k n", k=KT),
                             w_out[l].rearrange("(k p) n -> p k n", p=P)).then_inc(s_wout, 16)

                def load_row(v, s_done):
                    for s in range(2):
                        if l == 0 or s == 1:
                            r0 = (l * 4 + v) * 16 + s * 8
                            sp.dma_start(row[v][s], rows_d[r0:r0 + 8, :].rearrange("a b -> (a b)").partition_broadcast(P)
                                         ).then_inc(s_done, 16)
                if l == 0:
                    sp.wait_ge(s_rd, 16)
                sp.wait_ge(s_qde.h, s_qde.at(l, 1))
                load_row(0, s_row1.h)
                sp.wait_ge(s_kd.h, s_kd.at(l, 2))
                sp.wait_ge(s_elm.h, s_elm.at(l, 8))
                load_row(3, s_row.h)
                sp.wait_ge(s_hm.h, s_hm.at(l, 2))
                load_row(1, s_row.h)
                load_row(2, s_row.h)
                sp.wait_ge(s_otc.h, s_otc.at(l, len(QTL[l])))
                load_gu(l, 0, 0, s_wgu[0].h)
                load_dn(l, 0, 0, s_wdn[0].h)
                sp.wait_ge(s_op.h, s_op.at(l, 2 * len(QTL[l])))
                load_gu(l, 1, 1, s_wgu[1].h)
                load_dn(l, 1, 1, s_wdn[1].h)
                with sp.Fori(1, E // 2) as i:
                    for q in range(2):
                        sp.wait_ge(s_gu.h, s_gu.at(l, 2 * i + q - 1))
                        load_gu(l, 2 * i + q, q, s_wgu[q].h)
                        sp.wait_ge(s_dn.h, s_dn.at(l, 2 * i + q - 1))
                        load_dn(l, 2 * i + q, q, s_wdn[q].h)
                sp.wait_ge(s_dn.h, s_dn.at(l, E - 1))
                sp.wait_ge(s_ovi.h, s_ovi.at(l, 1))
                n_ov = sp.value_load(ovi[0:1, 0:1], min_val=0, max_val=NOV[l])
                with sp.Fori(0, NOV[l]) as j:
                    with sp.If(j < n_ov):
                        e = sp.value_load(ovi[0:1, bass.ds(j + 1, 1)], min_val=0, max_val=E - 1)
                        sp.wait_ge(s_ov[l], 11 * j + 1)
                        load_gu(l, e, 0, s_ovw[l])
                        load_dn(l, e, 0, s_ovw[l])
                sp.wait_ge(s_dn.h, s_dn.at(l, E))
                sp.wait_ge(s_ov[l], 11 * n_ov + 1)
                for q in range(2):
                    sp.wait_ge(s_scat[q].h, s_scat[q].at(l, 16 * E // 2))
                for n, t in enumerate(QTL[l]):
                    sp.dma_start(yb[n], y_d[l].rearrange("(k t p two) n -> t p k (two n)", k=2, p=P, two=2)[t - T0[l] // P]
                                 ).then_inc(s_yl[n], 16)
                if l == 1:
                    for n in range(2):
                        sp.wait_ge(s_x2.h, s_x2.at(l, n + 1))
                        sp.dma_start(out[0, n * P:(n + 1) * P, :], x[:, 2 + n, :]).then_inc(s_out, 16)
                    sp.wait_ge(s_out, 32)
        @block.tensor
        def _(pe):
            mm = nc.tensor.matmul
            pe.wait_ge(s_cf, 16)
            pe.wait_ge(s_rows, 16 * 9)
            nc.tensor.transpose(ps[:, 6, 0:96], ar[0:96, TOK:TOK + P], ident[0:96, 0:96])
            nc.tensor.transpose(ps[:, 6, 96:158], ar[0:62, TOK + P:TOK + 2 * P], ident[0:62, 0:62]).then_inc(s_vt, 1)
            pe.wait_ge(s_silc, 1)
            def ada_product(q, bank):
                for half in range(2):
                    for g in range(4):
                        k = 4 * half + g
                        ins = mm(ps[32 * g:32 * g + 32, bank, :], silc[:, k, :], wt[:, q * 4096 + k * 512:q * 4096 + (k + 1) * 512],
                                 start=(half == 0), stop=(half == 1), tile_position=(0, 32 * g))
                    ins.then_inc((s_adh, s_ada.h)[half], 1)

            def ada_columns(l, c, late, b):
                pe.wait_ge(s_adr.h, s_adr.at(l, c + 1))
                for j in range(4):
                    ins = mm(ps[:, 7 - l, c * 8 + j * 2:c * 8 + j * 2 + 2], adrow[late][:, b, j * P:(j + 1) * P],
                             cf[:, C_SEL:C_SEL + 2], start=True, stop=True)
                ins.then_inc(s_adc.h, 1)
            def norm_T(l):
                pe.wait_ge(s_xn.h, s_xn.at(l, NT))
                for k in range(KT):
                    if k >= 4:
                        h = s_tra if k % 2 else s_trv
                        pe.wait_ge(h.h, h.at(l, k // 2 - 1))
                    for t in range(NT):
                        ins = nc.tensor.transpose(ps[:, k % 4, t * P:(t + 1) * P], tok[:, t, k * P:(k + 1) * P], ident)
                    ins.then_inc(s_tr.h, 1)

            for c in range(UPFRONT):
                pe.wait_ge(s_adaw[c], 16)
                if c >= 2:
                    pe.wait_ge(s_adr.h, s_adr.at(0, c - 1))
                ada_product((c + 3) % 6, c % 2)
                if c:
                    ada_columns(0, c - 1, 0, (c - 1) % 2)
            ada_columns(0, UPFRONT - 1, 0, (UPFRONT - 1) % 2)

            for l in range(DEPTH):
                t0 = T0[l]
                norm_T(l)
                pe.wait_ge(s_trv.h, s_trv.at(l, KT // 2))
                pe.wait_ge(s_tra.h, s_tra.at(l, KT // 2))
                groups = in_groups(l)
                for n, (name, i, _) in enumerate(groups):
                    gi, off, w = WIN_AT[name]
                    if n >= 4:
                        e = groups[n - 4][2]
                        h = s_ipa if e == "a" else s_ipv
                        pe.wait_ge(h.h, h.at(l, count(l, n - 3, e)))
                    pe.wait_ge(s_win[gi], (l + 1) * 16 * len(WIN[gi][3]))
                    W = wt[:, off:off + KT * w].rearrange("p (k n) -> p k n", k=KT)
                    for k in range(KT):
                        if name in ("kvh", "q"):
                            ins = mm(ps[:, n % 4, :], hT[:, k, i * P:(i + 1) * P], W[:, k, :], start=(k == 0), stop=(k == KT - 1))
                        else:
                            a = 0 if name == "z" else t0
                            ins = mm(ps[:, n % 4, a:T], W[:, k, i * P:(i + 1) * P], hT[:, k, a:T], start=(k == 0), stop=(k == KT - 1))
                    ins.then_inc(s_ip.h, 1)
                    if l == 0:
                        pe.wait_ge(s_adw1, 32 * (n + 1))
                        ada_product(2, 4 + n % 2)
                        if n == 0:
                            pe.wait_ge(s_mod.h, s_mod.at(0, 1))
                        else:
                            ada_columns(*LATE[n - 1], 1, (n - 1) % 2)
                if l == 0:
                    ada_columns(*LATE[-1], 1, (len(LATE) - 1) % 2)
                pe.wait_ge(s_pl.h, s_pl.at(l, 1))
                pe.wait_ge(s_lw, 16 * 12 * (l + 1))
                for i in range(2):
                    mm(ps[:, 4 + i, t0:T], pwbd[:, i, :], pooled[:, i, t0:T], start=True, stop=True).then_inc(s_ply.h, 1)
                pe.wait_ge(s_ipa.h, s_ipa.at(l, count(l, len(groups), "a")))
                pe.wait_ge(s_ipv.h, s_ipv.at(l, count(l, len(groups), "v")))
                for j in range(5):
                    b = j % 4
                    tiles = QTL[l] if j < 4 else range(NT)
                    pe.wait_ge(s_qr.h, s_qr.at(l, NT))
                    if j == 4:
                        pe.wait_ge(s_qtv.h, s_qtv.at(l, 1))
                    for t in tiles:
                        c0 = j * P
                        ins = nc.tensor.transpose(ps[:, b, t * P:(t + 1) * P], tok[:, t, c0:c0 + P], ident)
                    ins.then_inc(s_qt.h, 1)
                pe.wait_ge(s_qtv.h, s_qtv.at(l, 4))
                pe.wait_ge(s_qta.h, s_qta.at(l, 3))
                pe.wait_ge(s_plm.h, s_plm.at(l, 2))

                def attn_scores(u, t, h):
                    b = 4 + u % 2
                    r = 64 * (h % 2)
                    if u >= 2:
                        pe.wait_ge(s_e.h, s_e.at(l, u - 1))
                    n = T if t >= 2 else CTX
                    ins = mm(ps[:, b, 0:n], qT[r:r + 64, h // 2, t * P:(t + 1) * P], kT[r:r + 64, h // 4, 0:n],
                             start=True, stop=(t < 2))
                    if t >= 2:
                        ins = mm(ps[:, b, CTX:T], cb[:, B_ID:B_ID + P], cb[:, B_BAND + (t - 2) * 256:B_BAND + (t - 1) * 256],
                                 start=False, stop=True)
                    ins.then_inc(s_s.h, 1)

                def attn_transpose(u, t, h):
                    nk = 4 if t >= 2 else 2
                    pe.wait_ge(s_dg.h, s_dg.at(l, u + 1))
                    if u >= 1:
                        pe.wait_ge(s_p2v.h, s_p2v.at(l, u))
                    for j in range(nk):
                        ins = mm(ps[:, 6, j * P:(j + 1) * P], prob[:, u % 2, j * P:(j + 1) * P], diag[:, u % 2], start=True, stop=True)
                    ins.then_inc(s_p2.h, 1)

                def attn_pv(u, t, h):
                    nk = 4 if t >= 2 else 2
                    w = u // HEADS
                    pe.wait_ge(s_p2v.h, s_p2v.at(l, u + 1))
                    if w:
                        pe.wait_ge(s_otc.h, s_otc.at(l, w))
                    for j in range(nk):
                        for g in range(2):
                            ins = mm(ps[64 * g:64 * g + 64, 7, :], tok[:, j, 640 + 64 * g:704 + 64 * g],
                                     pt[:, w % 2, j, 4 * g:4 * g + 4, :].rearrange("p h t -> p (h t)"), start=(j == 0), stop=(j == nk - 1))
                    ins.then_inc(s_pv.h, 1)

                every = [un for step in range(LEVELS + 1) for un in units(l, step)]

                def attention(r):
                    if r < len(every):
                        attn_scores(*every[r])
                    if 2 <= r < len(every) + 2:
                        attn_transpose(*every[r - 2])
                    if r >= 3 and every[r - 3][2] == HEADS - 1:
                        attn_pv(*every[r - 3])

                for step in range(LEVELS + 1):
                    pe.wait_ge(s_elm.h, s_elm.at(l, step + 1))
                    if step:
                        pe.wait_ge(s_elq.h, s_elq.at(l, step))
                    buf = (step + 1) % 2
                    if step == 0:
                        for i in range(2):
                            for odd in range(2):
                                r = 64 * odd
                                mm(ps[:, 2 * i + odd, t0:T], ones[r:r + 64, :], el[r:r + 64, 1, 0, i, t0:T], start=True, stop=True).then_inc(s_lv.h, 1)
                    for n in range(0, len(QTL[l]) if step else 0, 2):
                        pe.wait_ge(s_sc.h, s_sc.at(l, 4 + (step - 1) * len(QTL[l])) if step == 1 else s_sc.at(l, 4 + (step - 2) * len(QTL[l]) + n + 2))
                        q = el[:, buf, 1]
                        for j in range(4):
                            c, i = QTL[l][n] + j // 2, j % 2
                            for odd in range(2):
                                r = 64 * odd
                                ins = mm(ps[:, QTL[l][n] + odd, j * P:(j + 1) * P], el[r:r + 64, buf, 0, i, c * P:(c + 1) * P],
                                         q[r:r + 64, i, c * P:(c + 1) * P], start=True, stop=True)
                                if j == 3:
                                    ins.then_inc(s_lv.h, 1)
                    for (u, t, h) in units(l, step):
                        attention(u)
                def keys_T(chunks):
                    for c in chunks:
                        pe.wait_ge(s_kd.h, s_kd.at(l, 2))
                        pe.wait_ge(s_sc.h, s_sc.at(l, 4 + 7 * len(QTL[l])))
                        for j in range(4):
                            ins = nc.tensor.transpose(ps[:, c, j * P:(j + 1) * P], sg[:, j // 2, j % 2, c * P:(c + 1) * P], ident)
                        ins.then_inc(s_kdt.h, 1)

                attention(len(every))
                keys_T((0, 1))
                attention(len(every) + 1)
                keys_T((2, 3))
                kdt = a_(EL + 2048, 2048).rearrange("p (c j n) -> p c j n", c=NT, j=4)
                pe.wait_ge(s_kdc.h, s_kdc.at(l, NT))
                for d in range(2):
                    for c in range(NT):
                        for h in range(4):
                            r = 64 * (h % 2)
                            o = c * P + (h // 2) * 64
                            ins = mm(ps[r:r + 64, d, o:o + 64], kdt[:, c, 2 * d + h // 2, r:r + 64],
                                     tok[:, c, 768 + 64 * h:832 + 64 * h], start=True, stop=True)
                    ins.then_inc(s_U.h, 1)
                attention(len(every) + 2)
                if l == 0:
                    pe.wait_ge(s_rvt, 1)
                    nc.tensor.transpose(ps[:, 5, 0:P], rvc[:, 0:P], ident).then_inc(s_rv, 1)
                pe.wait_ge(s_S.h, s_S.at(l, 1))
                pe.wait_ge(s_qd.h, s_qd.at(l, 1))
                qd = a_(EL, 2048).rearrange("p (d i t) -> p d i t", d=2, i=2)
                for c in QTL[l]:
                    for h in range(4):
                        r = 64 * (h % 2)
                        i = h // 2
                        o = ps[r:r + 64, 2 + i, c * P:(c + 1) * P]
                        mm(o, tok[:, c, 768 + 64 * h:832 + 64 * h], sc[:, c - c % 2 + h % 2, 2 * (c % 2) + i, :], start=True, stop=False)
                        dirs = [d for d in range(2) if c != d]
                        for d in dirs:
                            ins = mm(o, S_st[r:r + 64, d, c, i, :], qd[r:r + 64, d, i, c * P:(c + 1) * P],
                                     start=False, stop=(d == dirs[-1]))
                ins.then_inc(s_o.h, 1)
                for i in range(2):
                    pe.wait_ge(s_osq.h, s_osq.at(l, i + 1))
                    mm(ps[:, i, t0:T], cf[:, C_BLK:C_BLK + P], a_(EL + 2048 + 512 * i, 512)[:, t0:T], start=True, stop=True).then_inc(s_ms.h, 1)
                pe.wait_ge(s_hm.h, s_hm.at(l, 2))
                pe.wait_ge(s_otc.h, s_otc.at(l, len(QTL[l])))
                pe.wait_ge(s_plm.h, s_plm.at(l, 2))
                pe.wait_ge(s_wout, 16 * (l + 1))
                ta = t0 // P
                nt = NT - ta

                def h2_T(n):
                    t = ta + n
                    pe.wait_ge(s_h2.h, s_h2.at(l, n + 1))
                    if n:
                        pe.wait_ge(s_t2v.h, s_t2v.at(l, n))
                        pe.wait_ge(s_t2a.h, s_t2a.at(l, n))
                    for k in range(KT):
                        ins = nc.tensor.transpose(ps[:, k // 4, (k % 4) * P:(k % 4 + 1) * P], tok[:, t, k * P:(k + 1) * P], ident)
                    ins.then_inc(s_t2.h, 1)

                def logits(n):
                    t = ta + n
                    pe.wait_ge(s_t2v.h, s_t2v.at(l, n + 1))
                    pe.wait_ge(s_t2a.h, s_t2a.at(l, n + 1))
                    for k in range(KT):
                        ins = mm(ps[:, 2, t * 36:(t + 1) * 36], hT[:, k, t * P:(t + 1) * P], wr[:, k, :], start=(k == 0), stop=(k == KT - 1))
                    return ins

                for n, t in enumerate(QTL[l]):
                    for hf in range(2):
                        m = 2 * n + hf
                        if m >= 4:
                            pe.wait_ge(s_x1.h, s_x1.at(l, m - 3))
                        for k in range(KT):
                            ins = mm(ps[:, 4 + m % 4, :], mixT[:, k, t * P:(t + 1) * P],
                                     wt[:, WOUT + k * D + hf * 512:WOUT + k * D + (hf + 1) * 512], start=(k == 0), stop=(k == KT - 1))
                        ins.then_inc(s_op.h, 1)
                    if n >= 1:
                        h2_T(n - 1)
                    if n >= 2:
                        logits(n - 2)
                logits(nt - 2)
                h2_T(nt - 1)
                logits(nt - 1).then_inc(s_lg.h, 1)
                S = seln(l)
                pe.wait_ge(s_oh.h, s_oh.at(l, 1))
                for t in range(nt):
                    for u in range(t + 1):
                        mm(ps[:, 5, t * E:(t + 1) * E], cb[:, B_TRI:B_TRI + P] if u == t else cb[:, B_ONE:B_ONE + P], S[:, u, :],
                           start=(u == 0), stop=(u == t))
                for u in range(nt):
                    ins = mm(ps[:, 5, 128:160], cb[:, B_ONE:B_ONE + P], S[:, u, :], start=(u == 0), stop=(u == nt - 1))
                ins.then_inc(s_rk.h, 1)
                Rm, Cm = a_(RTAB, 8 * P).rearrange("p (a n) -> p a n", a=8), a_(RTAB + 8 * P, 8 * NBT).rearrange("p (a n) -> p a n", a=8)
                pe.wait_ge(s_tb.h, s_tb.at(l, 1))
                for a in range(2 * nt):
                    ins = mm(ps[:, 6, 0:NBT], Rm[:, a, :], Cm[:, a, :], start=(a == 0), stop=(a == 2 * nt - 1))
                ins.then_inc(s_tbm.h, 1)

                def gather_T(q, src, s):
                    for j in range(4):
                        ins = nc.tensor.transpose(ps[:, 2, j * P:(j + 1) * P], src[:, j * P:(j + 1) * P], ident)
                    ins.then_inc(s, 1)

                def gate_up(q, w0, s):
                    for k in range(KT):
                        for u in range(2):
                            ins = mm(ps[64 * u:64 * u + 64, q, :], hs[:, q, k % 4, 64 * (k // 4):64 * (k // 4) + 64],
                                     wt[:, w0 + u * 4096 + k * 512:w0 + u * 4096 + (k + 1) * 512], start=(k == 0), stop=(k == KT - 1))
                    ins.then_inc(s, 1)

                def hid_T(s):
                    for c in range(2):
                        ins = nc.tensor.transpose(ps[:, 3, c * P:(c + 1) * P], hid[:, c * P:(c + 1) * P], ident)
                    ins.then_inc(s, 1)

                def down(q, w0, s):
                    for j in range(4):
                        for u in range(2):
                            ins = mm(ps[64 * u:64 * u + 64, 4 + q, :], hidT[:, 2 * (j % 2) + j // 2, :],
                                     wt[:, w0 + 8192 + j * D + u * 512:w0 + 8192 + j * D + (u + 1) * 512], start=(j == 0), stop=(j == 3))
                    ins.then_inc(s, 1)

                def expert(i, q, last):
                    e = 2 * i + q
                    pe.wait_ge(s_gtc.h, s_gtc.at(l, e + 1))
                    pe.wait_ge(s_wgu[q].h, s_wgu[q].at(l, 32 * i + 32))
                    gate_up(q, q * SLOT, s_gu.h)
                    if not last:
                        pe.wait_ge(s_xg[1 - q].h, s_xg[1 - q].at(l, 16 * i + 16 * (q + 1) if q == 1 else 16 * i + 16))
                        gather_T(1 - q, xg[:, 1 - q], s_gt.h)
                    pe.wait_ge(s_hid.h, s_hid.at(l, e + 1))
                    hid_T(s_ht.h)
                    pe.wait_ge(s_htc.h, s_htc.at(l, e + 1))
                    pe.wait_ge(s_wdn[q].h, s_wdn[q].at(l, 16 * i + 16))
                    if type(i) is not int or i > 0:
                        pe.wait_ge(s_y.h, s_y.at(l, e - 1))
                    down(q, q * SLOT, s_dn.h)

                pe.wait_ge(s_xg[0].h, s_xg[0].at(l, 16))
                gather_T(0, xg[:, 0], s_gt.h)
                expert(0, 0, False)
                expert(0, 1, False)
                with pe.Fori(1, E // 2 - 1) as i:
                    expert(i, 0, False)
                    expert(i, 1, False)
                expert(E // 2 - 1, 0, False)
                expert(E // 2 - 1, 1, True)
                pe.wait_ge(s_y.h, s_y.at(l, E))
                pe.wait_ge(s_ovi.h, s_ovi.at(l, 1))
                n_ov = pe.value_load(ovi[0:1, 0:1], min_val=0, max_val=NOV[l])
                with pe.Fori(0, NOV[l]) as j:
                    with pe.If(j < n_ov):
                        pe.wait_ge(s_ovx[l], 16 * j + 16)
                        gather_T(0, xg[:, 0], s_ov[l])
                        pe.wait_ge(s_ov[l], 11 * j + 4)
                        pe.wait_ge(s_ovw[l], 48 * j + 48)
                        gate_up(0, 0, s_ov[l])
                        pe.wait_ge(s_ov[l], 11 * j + 7)
                        hid_T(s_ov[l])
                        pe.wait_ge(s_ov[l], 11 * j + 9)
                        down(0, 0, s_ov[l])

        @block.scalar
        def _(act):
            A = nc.scalar.activation
            link = chain(act, s_act)
            act.dma_start(cf[:, :], const_f).then_inc(s_cf, 16)
            r0 = TOK
            act.dma_start(ar[0:96, r0:r0 + P], ada_b.rearrange("l (a p) -> (l a) p", p=P)).then_inc(s_rows, 16)
            r0 = TOK + P
            act.dma_start(ar[0:8, r0:r0 + P], cctx_in.rearrange("(a p) -> a p", p=P)).then_inc(s_rows, 16)
            act.dma_start(ar[8:16, r0:r0 + P], c_in.rearrange("b (a p) -> (b a) p", p=P)).then_inc(s_rows, 16)
            act.dma_start(ar[16:32, r0:r0 + P], norm1_g.rearrange("l (a p) -> (l a) p", p=P)).then_inc(s_rows, 16)
            act.dma_start(ar[32:48, r0:r0 + P], norm2_g.rearrange("l (a p) -> (l a) p", p=P)).then_inc(s_rows, 16)
            act.dma_start(ar[48:52, r0:r0 + P], pool_scale.rearrange("l (a p) -> (l a) p", p=P)).then_inc(s_rows, 16)
            act.dma_start(ar[52:60, r0:r0 + P], hgrn_lb.rearrange("l d (a p) -> (l d a) p", p=P)).then_inc(s_rows, 16)
            act.dma_start(ar[60:62, r0:r0 + 64], hgrn_norm_g).then_inc(s_rows, 16)
            act.dma_start(ar[60:62, r0 + 64:r0 + P], hgrn_norm_g).then_inc(s_rows, 16)
            act.dma_start(x[:, 0:2, :], ctx_in.rearrange("b (t p) n -> p (b t) n", p=P)).then_inc(s_x, 16)
            act.dma_start(x[:, 2:4, :], x_in.rearrange("b (t p) n -> p (b t) n", p=P)).then_inc(s_x, 16)
            act.dma_start(a_(EL, 640), const_b).then_inc(s_cb, 16)
            act.dma_start(a_(EL + 640, LEVELS * P), const_mask).then_inc(s_cb, 16)

            act.wait_ge(s_memz, 1)
            act.wait_ge(s_cols, 1)
            A(silc[:, :, 0:2].rearrange("p k s -> p s k"), cols[:, 0:16].rearrange("p (s k) -> p s k", s=2), ACT.Silu).then_inc(s_silc, 1)
            act.wait_ge(s_lbd, 1)
            A(lb[:, :], lbd[:, :], ACT.Sigmoid).then_inc(s_sig, 1)

            def params(l):
                act.dma_start(gain[:, 0, :], q_norm_g[l].partition_broadcast(P)).then_inc(s_lw, 16)
                act.dma_start(gain[:, 1, :], k_norm_g[l].partition_broadcast(P)).then_inc(s_lw, 16)
                act.dma_start(sink[:], attn_sink[l].partition_broadcast(P)).then_inc(s_lw, 16)
                act.dma_start(rb[:, 0:GROUPS], rg_b[l].partition_broadcast(P)).then_inc(s_lw, 16)
                act.dma_start(rb[:, GROUPS:], re_b[l].partition_broadcast(P)).then_inc(s_lw, 16)
                act.dma_start(wr[:, :, 0:GROUPS], rg_w[l].rearrange("(k p) n -> p k n", p=P)).then_inc(s_lw, 16)
                act.dma_start(wr[:, :, GROUPS:], re_w[l].rearrange("(k p) n -> p k n", p=P)).then_inc(s_lw, 16)
                if l == 0:
                    act.wait_ge(s_memz, 1)
                for g in range(4):
                    r = 64 * (g % 2)
                    act.dma_start(pwbd[r:r + 64, g // 2, r:r + 64], pool_w[l, g]).then_inc(s_lw, 16)

            def counts():
                act.dma_start(icnt, const_cnt.rearrange("p (i t) -> p i t", i=2)).then_inc(s_lw, 16)

            def square(l, t):
                if l == 1:
                    act.wait_ge(s_x2.h, s_x2.at(0, t + 1))
                if t:
                    act.wait_ge(s_ss.h, s_ss.at(l, t))
                A(ps[:, 2:4, :].rearrange("p a n -> p (a n)"), x[:, t, :], ACT.Square, accum_out=ss[:, t:t + 1]).then_inc(s_ss.h, 1)

            def norm_in(l):
                if l == 0:
                    act.wait_ge(s_x, 32)
                for t in range(NT) if l == 0 else (NT - 1,):
                    square(l, t)
                act.wait_ge(s_var.h, s_var.at(l, 1))
                A(rs[:, :], ss[:, :], ACT.Sqrt).then_inc(s_sq.h, 1)

            def norm_out(l):
                act.wait_ge(s_mod.h, s_mod.at(l, 1))
                for k in range(1, KT, 2):
                    act.wait_ge(s_tr.h, s_tr.at(l, k + 1))
                    for s in range(2):
                        ins = A(hT[:, k, s * CTX:(s + 1) * CTX], ps[:, k % 4, s * CTX:(s + 1) * CTX], ACT.Identity,
                                scale=A1[:, l, k, s:s + 1], bias=mod[:, l, 0, k, s:s + 1])
                    ins.then_inc(s_tra.h, 1)

            params(0)
            act.wait_ge(s_bf, 1)
            counts()
            norm_in(0)
            with act.Fori(0, UPFRONT // 2) as i:
                for b in range(2):
                    act.wait_ge(s_ada.h, s_ada.at(0, 2 * i + b + 1))
                    A(adrow[0][:, b], ps[:, b, :], ACT.Copy).then_inc(s_adr.h, 1)
            for l in range(DEPTH):
                t0 = T0[l]
                if l:
                    norm_in(l)
                norm_out(l)
                act.wait_ge(s_up0, l + 1)
                def late_rows(k):
                    act.wait_ge(s_ada.h, s_ada.at(0, UPFRONT + k + 1))
                    A(adrow[1][:, k % 2], ps[:, 4 + k % 2, :], ACT.Copy).then_inc(s_adr.h, 1)

                for n, (name, i, e) in enumerate(in_groups(l)):
                    if l == 0 and n:
                        late_rows(n - 1)
                    if e != "a":
                        continue
                    if name == "hq" and i == 0:
                        act.wait_ge(s_f.h, s_f.at(l, 1))
                        A(sg[:], sg[:], ACT.Ln).then_inc(s_g.h, 1)
                    act.wait_ge(s_ip.h, s_ip.at(l, n + 1))
                    b = n % 4
                    if name == "u":
                        v = up.rearrange("p (i s t) -> p i s t", i=2, s=2)[:, i, l:2, 8:8 + 256]
                        A(v, ps[:, b, t0:T].rearrange("p (s t) -> p s t", t=256), ACT.Copy).then_inc(s_ipa.h, 1)
                    elif name == "z":
                        A(sg[:, i // 2, i % 2, :], ps[:, b, :], ACT.Sigmoid)
                        A(kk[:, i // 2, i % 2, :], ps[:, b, :], ACT.Sigmoid, scale=-1.0).then_inc(s_ipa.h, 1)
                    else:
                        A((hq if name == "hq" else hg)[:, i, t0:T], ps[:, b, t0:T], ACT.Silu).then_inc(s_ipa.h, 1)
                    if name == "z" and i == 0:
                        act.wait_ge(s_qsd.h, s_qsd.at(l, 1))
                        A(qss[:].rearrange("p t h -> p (t h)"), qss[:].rearrange("p t h -> p (t h)"), ACT.Sqrt).then_inc(s_qrs.h, 1)
                if l == 0:
                    late_rows(len(LATE) - 1)
                for i in range(2):
                    act.wait_ge(s_ply.h, s_ply.at(l, i + 1))
                    A(mixT[:, i, t0:T], ps[:, 4 + i, t0:T], ACT.Copy, scale=cols[:, 48 + 2 * l + i:49 + 2 * l + i]).then_inc(s_plm.h, 1)
                for j in (1, 3):
                    act.wait_ge(s_qt.h, s_qt.at(l, j + 1))
                    A(qT[:, j, t0:T], ps[:, j, t0:T], ACT.Copy).then_inc(s_qta.h, 1)
                act.wait_ge(s_qt.h, s_qt.at(l, 5))
                A(kT[0:64, 0, :], ps[0:64, 0, :], ACT.Copy)
                A(kT[64:128, 0, :], ps[0:64, 0, :], ACT.Copy).then_inc(s_qta.h, 1)

                def softmax(u, t, h):
                    n = T if t >= 2 else CTX
                    b = u // HEADS % 2
                    act.wait_ge(s_mn.h, s_mn.at(l, u + 1))
                    A(esk[:, h:h + 1], sink[:, h:h + 1], ACT.Exp, bias=mneg[:, b, h:h + 1])
                    if u >= 2:
                        act.wait_ge(s_p2.h, s_p2.at(l, u - 1))
                    A(prob[:, u % 2, 0:n], ps[:, 4 + u % 2, 0:n], ACT.Exp, bias=mneg[:, b, h:h + 1], scale=HD ** -0.5,
                      accum_out=den[:, b, h:h + 1]).then_inc(s_e.h, 1)

                def evac_p(u, t, h):
                    nk = 4 if t >= 2 else 2
                    w = u // HEADS
                    act.wait_ge(s_p2.h, s_p2.at(l, u + 1))
                    if h == 0 and w >= 2:
                        act.wait_ge(s_pv.h, s_pv.at(l, w - 1))
                    A(pt[:, w % 2, 0:nk, h, :], ps[:, 6, 0:nk * P].rearrange("p (k t) -> p k t", k=nk), ACT.Copy).then_inc(s_p2v.h, 1)

                every = [un for step in range(LEVELS + 1) for un in units(l, step)]

                def attention(r):
                    if 2 <= r:
                        evac_p(*every[r - 2])
                    if r < len(every):
                        softmax(*every[r])

                act.wait_ge(s_kdx.h, s_kdx.at(l, 1))
                A(sg[:], sg[:], ACT.Exp).then_inc(s_kde.h, 1)
                bc = bb[:].rearrange("p d i (c t) -> p d i c t", c=NT)
                A(dec[:, 0], bc[:, 0, :, :, P - 1], ACT.Exp)
                A(dec[:, 1], bc[:, 1, :, :, 0], ACT.Exp).then_inc(s_dec.h, 1)
                for step in range(LEVELS + 1):
                    if step < LEVELS:
                        act.wait_ge(s_elx.h, s_elx.at(l, step + 1))
                        v = el[:, step % 2, :, :, t0:T]
                        v = v.rearrange("p s i t -> p (s i) t")
                        A(v, v, ACT.Exp).then_inc(s_ele.h, 1)
                    for un in units(l, step):
                        attention(un[0])
                act.wait_ge(s_lv.h, s_lv.at(l, 4 + 7 * len(QTL[l])))
                qd = a_(EL, 2048).rearrange("p (j t) -> p j t", j=4)
                A(qd[:, :, t0:T], bb[:].rearrange("p d i t -> p (d i) t")[:, :, t0:T], ACT.Exp).then_inc(s_qde.h, 1)
                for r in range(2):
                    attention(len(every) + r)
                nc.scalar.preload_act_table_set("natural_log_exp_and_others")
                for i in range(2):
                    act.wait_ge(s_o.h, s_o.at(l, 1))
                    A(a_(EL + 2048 + 512 * i, 512)[:, t0:T], ps[:, 2 + i, t0:T], ACT.Square).then_inc(s_osq.h, 1)
                r = a_(EL, 1024).rearrange("p (i t) -> p i t", i=2)[:, :, t0:T]
                act.wait_ge(s_ms.h, s_ms.at(l, 2))
                link(A(r, ps[:, 0:2, t0:T], ACT.Ln, scale=1.0 / HD, bias=epsc[:, 0:1]))
                A(r, r, ACT.Exp, scale=-0.5).then_inc(s_r.h, 1)
                ta = t0 // P

                def evac_h2(n):
                    act.wait_ge(s_t2.h, s_t2.at(l, n + 1))
                    A(hT[:, 4:8, t0 + n * P:t0 + (n + 1) * P], ps[:, 1, :].rearrange("p (k t) -> p k t", k=4), ACT.Copy).then_inc(s_t2a.h, 1)

                for n, t in enumerate(QTL[l]):
                    act.wait_ge(s_x1.h, s_x1.at(l, 2 * n + 2))
                    A(tok[:, t, :], x[:, t, :], ACT.Square, accum_out=ss[:, t:t + 1]).then_inc(s_ss2.h, 1)
                    act.wait_ge(s_var2.h, s_var2.at(l, n + 1))
                    A(rs[:, t:t + 1], ss[:, t:t + 1], ACT.Sqrt).then_inc(s_sq2.h, 1)
                    if n:
                        evac_h2(n - 1)
                evac_h2(len(QTL[l]) - 1)
                act.wait_ge(s_r1.h, s_r1.at(l, 1))
                g4 = a_(RT + 144, 16)[:, 4 * ta:]
                A(g4, g4, ACT.Exp).then_inc(s_r2.h, 1)
                act.wait_ge(s_r3.h, s_r3.at(l, 1))
                dv = a_(RT + 160, 4)[:, ta:]
                A(dv, dv, ACT.Exp).then_inc(s_r4.h, 1)
                if l == 0:
                    params(1)

                def evac_hs(q, s):
                    A(hs[:, q], ps[:, 2, :].rearrange("p (j n) -> p j n", j=4), ACT.Copy).then_inc(s, 1)

                def evac_y(q, s):
                    A(ysb[:, q], ps[:, 4 + q, :], ACT.Copy).then_inc(s, 1)

                def silu(q, s):
                    A(sil[64:128, :], ps[0:64, q, :], ACT.Silu).then_inc(s, 1)

                def expert(i, q, last):
                    e = 2 * i + q
                    if not last:
                        act.wait_ge(s_gt.h, s_gt.at(l, e + 2))
                        if type(i) is not int or i > 0 or q:
                            act.wait_ge(s_gu.h, s_gu.at(l, e))
                        evac_hs(1 - q, s_gtc.h)
                    act.wait_ge(s_gu.h, s_gu.at(l, e + 1))
                    if type(i) is not int or i > 0 or q:
                        act.wait_ge(s_hid.h, s_hid.at(l, e))
                    silu(q, s_sil.h)
                    act.wait_ge(s_dn.h, s_dn.at(l, e + 1))
                    if type(i) is not int or i > 0:
                        act.wait_ge(s_scat[q].h, s_scat[q].at(l, 16 * i))
                    evac_y(q, s_y.h)

                act.wait_ge(s_gt.h, s_gt.at(l, 1))
                evac_hs(0, s_gtc.h)
                expert(0, 0, False)
                expert(0, 1, False)
                with act.Fori(1, E // 2 - 1) as i:
                    expert(i, 0, False)
                    expert(i, 1, False)
                expert(E // 2 - 1, 0, False)
                expert(E // 2 - 1, 1, True)
                act.wait_ge(s_scat[0].h, s_scat[0].at(l, 16 * E // 2))
                n_ov = act.value_load(ovi[0:1, 0:1], min_val=0, max_val=NOV[l])
                with act.Fori(0, NOV[l]) as j:
                    with act.If(j < n_ov):
                        act.wait_ge(s_ov[l], 11 * j + 3)
                        evac_hs(0, s_ov[l])
                        act.wait_ge(s_ov[l], 11 * j + 5)
                        silu(0, s_ov[l])
                        act.wait_ge(s_ov[l], 11 * j + 10)
                        evac_y(0, s_ov[l])
                if l == 0:
                    counts()
                for n, t in enumerate(QTL[l]):
                    act.wait_ge(s_yl[n], 16 * (l + 1))
                    A(yb[n][:, 0], yb[n][:, 0], ACT.Copy, scale=gw[:, t, 0:1]).then_inc(s_c0.h, 1)
                    if l == 0 and n:
                        square(1, n - 1)

        @block.vector
        def _(v):
            V = nc.vector
            link = chain(v, s_dve)
            V.memset(epsc[:], EPS)
            V.memset(cb[:, B_ONE:B_ONE + P], 1.0)
            V.memset(silc[:], 0.0)
            V.memset(pwbd[:], 0.0).then_inc(s_memz, 1)
            v.wait_ge(s_vt, 1)
            for l in range(DEPTH):
                V.tensor_copy(adab[l], ps[:, 6, 48 * l:48 * (l + 1)])
            V.tensor_copy(cols[:], ps[:, 6, 96:158]).then_inc(s_cols, 1)
            v.wait_ge(s_cols, 1)
            V.tensor_tensor(lbd[:], cols[:, 56:60], cols[:, 52:56], ALU.subtract).then_inc(s_lbd, 1)
            v.wait_ge(s_sig, 1)
            V.tensor_scalar(omlb[:], lb[:], -1.0, 1.0, ALU.mult, ALU.add).then_inc(s_lb, 1)
            v.wait_ge(s_cf, 16)
            v.wait_ge(s_cb, 32)
            V.tensor_scalar(halfb[:], cf[:, C_HALF:C_HALF + 1], 2.0 * BIG, None, ALU.add)
            V.tensor_copy(cb[:, B_ID:B_ID + P], ident)
            V.tensor_copy(mask[:].rearrange("p l t -> p (l t)"), a_(EL + 640, LEVELS * P))
            V.tensor_copy(cb[:, B_TRI:], a_(EL, 640)).then_inc(s_bf, 1)
            rv = rvc[:, 0:P].rearrange("p (l v s k) -> p l v s k", l=2, v=4, s=2)

            def modulation(l, parts):
                a, b = parts
                return V.tensor_tensor(mod[:, l, a:b].rearrange("p a k s -> p (a k) s"),
                                       ps[:, 7 - l, 16 * a:16 * b].rearrange("p (a s) -> p a s", s=2),
                                       adab[l][:, 8 * a:8 * b].unsqueeze(2).to_broadcast([P, 8 * (b - a), 2]), ALU.add)

            def modulated_gain(l, Ax, part, g0):
                g = cols[:, g0 + 8 * l:g0 + 8 * l + 8].unsqueeze(2).to_broadcast([P, KT, 2])
                return V.scalar_tensor_tensor(out=Ax[:, l], in0=mod[:, l, part], scalar=1.0, in1=g, op0=ALU.add, op1=ALU.mult)

            def norm_in(l):
                v.wait_ge(s_ss.h, s_ss.at(l, NT))
                V.tensor_scalar(ss[:], ss[:], 1.0 / D, EPS, ALU.mult, ALU.add).then_inc(s_var.h, 1)
                v.wait_ge(s_sq.h, s_sq.at(l, 1))
                link(V.reciprocal(rs[:], rs[:]))
                for t in range(NT):
                    V.tensor_scalar(tok[:, t, :], x[:, t, :], rs[:, t:t + 1], None, ALU.mult).then_inc(s_xn.h, 1)

            def norm_out(l):
                v.wait_ge(s_mod.h, s_mod.at(l, 1))
                for k in range(0, KT, 2):
                    v.wait_ge(s_tr.h, s_tr.at(l, k + 1))
                    for s in range(2):
                        ins = V.tensor_scalar(hT[:, k, s * CTX:(s + 1) * CTX], ps[:, k % 4, s * CTX:(s + 1) * CTX],
                                              A1[:, l, k, s:s + 1], mod[:, l, 0, k, s:s + 1], ALU.mult, ALU.add)
                    ins.then_inc(s_trv.h, 1)

            norm_in(0)
            v.wait_ge(s_adc.h, s_adc.at(0, UPFRONT))
            link(modulation(0, (0, 2)))
            modulated_gain(0, A1, 1, 16).then_inc(s_mod.h, 1)
            for l in range(DEPTH):
                t0 = T0[l]
                if l:
                    norm_in(l)
                norm_out(l)
                for n, (name, i, e) in enumerate(in_groups(l)):
                    if e != "v":
                        continue
                    v.wait_ge(s_ip.h, s_ip.at(l, n + 1))
                    dst = tok[:, i, 512:1024] if name == "kvh" else tok[:, i, 0:512]
                    V.tensor_copy(dst, ps[:, n % 4, :]).then_inc(s_ipv.h, 1)
                for t in range(NT):
                    v.wait_ge(s_qsq.h, s_qsq.at(l, t + 1))
                    h0 = 0 if l == 0 or t >= 2 else 8
                    V.tensor_reduce(qss[:, t, h0:], qtmp[:, h0:, :], AX, ALU.add).then_inc(s_qss.h, 1)
                v.wait_ge(s_qss.h, s_qss.at(l, NT))
                q40 = qss[:].rearrange("p t h -> p (t h)")
                V.tensor_scalar(q40, q40, 1.0 / HD, EPS, ALU.mult, ALU.add).then_inc(s_qsd.h, 1)
                v.wait_ge(s_qrs.h, s_qrs.at(l, 1))
                V.reciprocal(q40, q40).then_inc(s_qsd.h, 1)
                v.wait_ge(s_ipa.h, s_ipa.at(l, count(l, len(in_groups(l)) - 4, "a")))
                if l == 1:
                    for d in range(2):
                        for i in range(2):
                            j = 2 * d + i
                            V.tensor_scalar(sg[:, d, i], sg[:, d, i], omlb[:, j:j + 1], lb[:, j:j + 1], ALU.mult, ALU.add)
                            link(V.tensor_scalar(kk[:, d, i], kk[:, d, i], omlb[:, j:j + 1], None, ALU.mult))
                V.tensor_scalar(sg[:], sg[:], FMIN, None, ALU.max).then_inc(s_f.h, 1)
                v.wait_ge(s_g.h, s_g.at(l, 1))
                for d in range(2):
                    for i in range(2):
                        for c in range(NT):
                            s = slice(c * P, (c + 1) * P)
                            ins = V.tensor_tensor_scan(bb[:, d, i, s], ones, sg[:, d, i, s], 0.0, ALU.mult, ALU.add)
                link(ins)
                bc = bb[:].rearrange("p d i (c t) -> p d (i c) t", c=NT)
                sgc = sg[:].rearrange("p d i (c t) -> p d (i c) t", c=NT)
                link(V.tensor_tensor(sgc[:, 1], sgc[:, 1], bc[:, 1], ALU.subtract))
                tot = den[:].rearrange("p a b -> p (a b)")[:, 0:8]
                link(V.tensor_copy(tot, bc[:, 1, :, P - 1]))
                V.tensor_tensor(bc[:, 1], sgc[:, 1], tot.unsqueeze(2).to_broadcast([P, 8, P]), ALU.add).then_inc(s_b.h, 1)
                v.wait_ge(s_b.h, s_b.at(l, 1))
                for d in range(2):
                    e = bc[:, d, :, P - 1] if d == 0 else bc[:, d, :, 0]
                    ins = V.tensor_tensor(sgc[:, d], e.unsqueeze(2).to_broadcast([P, 8, P]), bc[:, d], ALU.subtract)
                ins.then_inc(s_kdx.h, 1)
                if l == 0:
                    v.wait_ge(s_adc.h, s_adc.at(1, 12))
                    modulation(0, (2, 6))
                    link(modulation(1, (0, 6)))
                    modulated_gain(0, A2, 4, 32)
                    modulated_gain(1, A1, 1, 16)
                    modulated_gain(1, A2, 4, 32).then_inc(s_mod.h, 1)
                for j in (0, 2):
                    v.wait_ge(s_qt.h, s_qt.at(l, j + 1))
                    V.tensor_copy(qT[:, j, t0:T], ps[:, j, t0:T]).then_inc(s_qtv.h, 1)
                v.wait_ge(s_qt.h, s_qt.at(l, 5))
                V.tensor_copy(kT[0:64, 1, :], ps[64:128, 0, :]).then_inc(s_qtv.h, 1)
                V.tensor_copy(kT[64:128, 1, :], ps[64:128, 0, :]).then_inc(s_qtv.h, 1)

                if l == 0:
                    v.wait_ge(s_mod.h, s_mod.at(1, 1))
                    v.wait_ge(s_ip.h, s_ip.at(0, len(in_groups(0))))
                    for m in range(DEPTH):
                        for i, src in enumerate((mod[:, m, 2], A2[:, m], mod[:, m, 3], mod[:, m, 5])):
                            ins = V.tensor_copy(rv[:, m, i], src.rearrange("p k s -> p s k"))
                    ins.then_inc(s_rvt, 1)

                def rowmax(u, t, h):
                    n = T if t >= 2 else CTX
                    b = u // HEADS % 2
                    v.wait_ge(s_s.h, s_s.at(l, u + 1))
                    link(V.reduce_max(mx[:, h:h + 1], ps[:, 4 + u % 2, 0:n], AX))
                    V.tensor_scalar(mneg[:, b, h:h + 1], mx[:, h:h + 1], -HD ** -0.5, nsink[:, h:h + 1], ALU.mult, ALU.min).then_inc(s_mn.h, 1)

                def inverse(u, t, h):
                    b = u // HEADS % 2
                    v.wait_ge(s_e.h, s_e.at(l, u + 1))
                    link(V.tensor_tensor(den[:, b, h:h + 1], den[:, b, h:h + 1], esk[:, h:h + 1], ALU.add))
                    link(V.reciprocal(den[:, b, h:h + 1], den[:, b, h:h + 1]))
                    V.tensor_scalar(diag[:, u % 2], ident, den[:, b, h:h + 1], None, ALU.mult).then_inc(s_dg.h, 1)

                def finish(u, t, h):
                    w = u // HEADS
                    v.wait_ge(s_pv.h, s_pv.at(l, w + 1))
                    for g in range(2):
                        for o in range(2):
                            src = ps[64 * g:64 * g + 64, 7, :].rearrange("p (m o t) -> p o m t", m=2, o=2)[:, o]
                            ins = V.tensor_copy(mixT[64 * o:64 * o + 64, 2 + 2 * g:4 + 2 * g, t * P:(t + 1) * P], src)
                    ins.then_inc(s_otc.h, 1)

                every = [un for step in range(LEVELS + 1) for un in units(l, step)]

                def attention(r):
                    if r < len(every):
                        rowmax(*every[r])
                    if 1 <= r < len(every) + 1:
                        inverse(*every[r - 1])
                    if r >= 4 and every[r - 4][2] == HEADS - 1:
                        finish(*every[r - 4])

                v.wait_ge(s_lw, 16 * 12 * (l + 1))
                V.tensor_scalar(nsink[:], sink[:], -1.0, None, ALU.mult)
                v.wait_ge(s_ipa.h, s_ipa.at(l, count(l, len(in_groups(l)), "a")))
                link(V.tensor_tensor(el[:, 1, 0, :, t0:T], kk[:, 0, :, t0:T], kk[:, 1, :, t0:T], ALU.add))
                V.tensor_tensor(el[:, 1, 0, :, t0:T], el[:, 1, 0, :, t0:T], hq[:, :, t0:T], ALU.mult).then_inc(s_elm.h, 1)

                def operands(step):
                    b = (step + 1) % 2
                    m = 1 << (step - 1)
                    v.wait_ge(s_ele.h, s_ele.at(l, step))

                    def halves(a):
                        return a.rearrange("p i (n h m) -> p i n h m", h=2, m=m)
                    K = halves(el[:, b, 0, :, t0:T])
                    kf, kb = halves(kk[:, 0, :, t0:T]), halves(kk[:, 1, :, t0:T])
                    V.tensor_tensor(K[:, :, :, 0, :], K[:, :, :, 0, :], kf[:, :, :, 0, :], ALU.mult)
                    V.tensor_tensor(K[:, :, :, 1, :], K[:, :, :, 1, :], kb[:, :, :, 1, :], ALU.mult).then_inc(s_elm.h, 1)

                for step in range(LEVELS + 1):
                    if step == 0:
                        s6 = sc.rearrange("p (g odd) (c i) t -> p g odd c i t", odd=2, i=2)
                        for i in range(2):
                            for odd in range(2):
                                v.wait_ge(s_lv.h, s_lv.at(l, 2 * i + odd + 1))
                                src = ps[:, 2 * i + odd, t0:T].rearrange("p (g c t) -> p g c t", c=2, t=P)
                                V.tensor_tensor(s6[:, t0 // CTX:, odd, :, i, :], src, ident.unsqueeze(1).unsqueeze(1).to_broadcast([P, 2 - t0 // CTX, 2, P]),
                                                ALU.mult).then_inc(s_sc.h, 1)
                    for n, c in enumerate(QTL[l] if step else []):
                        v.wait_ge(s_lv.h, s_lv.at(l, 4 + (step - 1) * len(QTL[l]) + n + 1))
                        src = ps[:, c, :].rearrange("p (h t) -> p h t", h=4)
                        if n == 0:
                            v.wait_ge(s_sc.h, s_sc.at(l, 4 + (step - 1) * len(QTL[l])))
                        V.copy_predicated(sc[:, c], mask[:, step - 1].unsqueeze(1).to_broadcast([P, 4, P]), src).then_inc(s_sc.h, 1)
                    for n, un in enumerate(units(l, step)):
                        attention(un[0])
                        if n == 0 and step < LEVELS:
                            operands(step + 1)
                    if step == 2:
                        v.wait_ge(s_kde.h, s_kde.at(l, 1))
                        for d in range(2):
                            V.tensor_tensor(sg[:, d], sg[:, d], kk[:, d], ALU.mult).then_inc(s_kd.h, 1)
                kdt = a_(EL + 2048, 2048).rearrange("p (c n) -> p c n", c=NT)

                def evac_keys(chunks):
                    for c in chunks:
                        v.wait_ge(s_kdt.h, s_kdt.at(l, c + 1))
                        V.tensor_copy(kdt[:, c], ps[:, c, :]).then_inc(s_kdc.h, 1)

                attention(len(every))
                evac_keys((0, 1))
                attention(len(every) + 1)
                attention(len(every) + 2)
                evac_keys((2, 3))
                v.wait_ge(s_qde.h, s_qde.at(l, 1))
                qd = a_(EL, 2048).rearrange("p (d i t) -> p d i t", d=2, i=2)
                for d in range(2):
                    ins = V.tensor_tensor(qd[:, d, :, t0:T], qd[:, d, :, t0:T], hq[:, :, t0:T], ALU.mult)
                ins.then_inc(s_qd.h, 1)
                v.wait_ge(s_U.h, s_U.at(l, 2))
                v.wait_ge(s_dec.h, s_dec.at(l, 1))
                for d, order in ((0, (0, 1, 2, 3)), (1, (1, 0, 3, 2))):
                    U = ps[:, d, :].rearrange("p (c i v) -> p c i v", c=NT, i=2)
                    link(V.tensor_copy(S_st[:, d, order[1]], U[:, order[0]]))
                    for a, b in ((order[1], order[2]), (order[2], order[3])):
                        for i in range(2):
                            ins = V.scalar_tensor_tensor(out=S_st[:, d, b, i], in0=S_st[:, d, a, i], scalar=dec[:, d, i, a:a + 1],
                                                         in1=U[:, a, i], op0=ALU.mult, op1=ALU.add)
                        link(ins)
                V.tensor_copy(mx[:, 0:1], epsc[:, 0:1]).then_inc(s_S.h, 1)
                attention(len(every) + 3)
                if l == 0:
                    v.wait_ge(s_rv, 1)
                    V.tensor_copy(rvc[:, P:], ps[:, 5, 0:P]).then_inc(s_rvs, 1)
                if l == 0:
                    v.wait_ge(s_rd, 16)
                for i in range(2):
                    r = a_(EL + 512 * i, 512)[:, t0:T]
                    v.wait_ge(s_r.h, s_r.at(l, 1))
                    link(V.tensor_tensor(r, r, ps[:, 2 + i, t0:T], ALU.mult))
                    V.scalar_tensor_tensor(out=mixT[:, 6 + i, t0:T], in0=r, scalar=cols[:, 60 + l:61 + l], in1=hg[:, i, t0:T],
                                           op0=ALU.mult, op1=ALU.mult).then_inc(s_hm.h, 1)
                v.wait_ge(s_row1.h, s_row1.at(l, 16 * (2 - l)))
                def evac_h2(n):
                    v.wait_ge(s_t2.h, s_t2.at(l, n + 1))
                    V.tensor_copy(hT[:, 0:4, t0 + n * P:t0 + (n + 1) * P], ps[:, 0, :].rearrange("p (k t) -> p k t", k=4)).then_inc(s_t2v.h, 1)

                for n, t in enumerate(QTL[l]):
                    for hf in range(2):
                        m = 2 * n + hf
                        tmp = a_(EL + 1024 + 512 * (m % 2), 512)
                        v.wait_ge(s_op.h, s_op.at(l, m + 1))
                        link(V.tensor_tensor(tmp, ps[:, 4 + m % 4, :], row[0][t // 2][:, hf * 512:(hf + 1) * 512], ALU.mult))
                        V.tensor_tensor(x[:, t, hf * 512:(hf + 1) * 512], x[:, t, hf * 512:(hf + 1) * 512], tmp, ALU.add).then_inc(s_x1.h, 1)
                    v.wait_ge(s_row.h, s_row.at(l, 48 * (2 - l)))
                    v.wait_ge(s_ss2.h, s_ss2.at(l, n + 1))
                    V.tensor_scalar(ss[:, t:t + 1], ss[:, t:t + 1], 1.0 / D, EPS, ALU.mult, ALU.add).then_inc(s_var2.h, 1)
                    v.wait_ge(s_sq2.h, s_sq2.at(l, n + 1))
                    link(V.reciprocal(rs[:, t:t + 1], rs[:, t:t + 1]))
                    link(V.scalar_tensor_tensor(out=tok[:, t, :], in0=x[:, t, :], scalar=rs[:, t:t + 1], in1=row[1][t // 2], op0=ALU.mult, op1=ALU.mult))
                    V.tensor_tensor(tok[:, t, :], tok[:, t, :], row[2][t // 2], ALU.add).then_inc(s_h2.h, 1)
                    if n:
                        evac_h2(n - 1)
                evac_h2(len(QTL[l]) - 1)
                ta = t0 // P
                nt = NT - ta

                iota = cf[:, C_IOTA:C_IOTA + 64]

                def rt(off, n):
                    return a_(RT + off, n)
                L = rt(0, 36 * nt).rearrange("p (t n) -> p t n", t=nt)
                v.wait_ge(s_lg.h, s_lg.at(l, 1))
                link(V.tensor_tensor(L, ps[:, 2, 36 * ta:144].rearrange("p (t n) -> p t n", t=nt), rb[:].unsqueeze(1).to_broadcast([P, nt, 36]), ALU.add))
                g8 = rt(200, 8 * nt).rearrange("p (t n) -> p t n", t=nt)
                link(V.memset(g8, NEG))
                link(V.tensor_copy(g8[:, :, 0:4], L[:, :, 0:4]))
                gm = rt(240, 8 * nt).rearrange("p (t n) -> p t n", t=nt)
                gi = rt(280, 8 * nt).bitcast(U32).rearrange("p (t n) -> p t n", t=nt)
                for t in range(nt):
                    ins = V.max(gm[:, t], g8[:, t])
                link(ins)
                for t in range(nt):
                    ins = V.max_index(gi[:, t], gm[:, t], g8[:, t])
                link(ins)
                ex = rt(144, 16)[:, 4 * ta:].rearrange("p (t n) -> p t n", t=nt)
                V.tensor_tensor(ex, L[:, :, 0:4], gm[:, :, 0:1].to_broadcast([P, nt, 4]), ALU.subtract).then_inc(s_r1.h, 1)
                gidx = rt(320, nt)
                link(V.tensor_copy(gidx, gi[:, :, 0]))
                oh4 = rt(324, 4 * nt).rearrange("p (t n) -> p t n", t=nt)
                link(V.tensor_tensor(oh4, iota[:, 0:4].unsqueeze(1).to_broadcast([P, nt, 4]), gidx.unsqueeze(2).to_broadcast([P, nt, 4]), ALU.is_equal))
                sel = rt(340, 32 * nt)
                link(V.tensor_tensor(sel.rearrange("p (t g e) -> p t g e", t=nt, g=4), L[:, :, 4:36].rearrange("p t (g e) -> p t g e", g=4),
                                     oh4.unsqueeze(3).to_broadcast([P, nt, 4, 8]), ALU.mult))
                le = rt(468, 8 * nt).rearrange("p (t n) -> p t n", t=nt)
                link(V.tensor_reduce(le, sel.rearrange("p (t g e) -> p t e g", t=nt, g=4), AX, ALU.add))
                lm = rt(500, 8 * nt).rearrange("p (t n) -> p t n", t=nt)
                li = rt(532, 8 * nt).bitcast(U32).rearrange("p (t n) -> p t n", t=nt)
                for t in range(nt):
                    ins = V.max(lm[:, t], le[:, t])
                link(ins)
                for t in range(nt):
                    ins = V.max_index(li[:, t], lm[:, t], le[:, t])
                link(ins)
                dv = rt(160, 4)[:, ta:]
                V.tensor_tensor(dv, lm[:, :, 1], lm[:, :, 0], ALU.subtract).then_inc(s_r3.h, 1)
                eid = rt(564, 2 * nt).rearrange("p (k t) -> p k t", k=2)
                link(V.tensor_copy(eid, li[:, :, 0:2].rearrange("p t k -> p k t")))
                link(V.scalar_tensor_tensor(out=eid, in0=gidx.unsqueeze(1).to_broadcast([P, 2, nt]), scalar=8.0, in1=eid, op0=ALU.mult, op1=ALU.add))
                oh = rt(572, 64 * nt).rearrange("p (k t e) -> p k t e", k=2, t=nt)
                for k in range(2):
                    ins = V.tensor_tensor(oh[:, k], iota[:, 0:E].unsqueeze(1).to_broadcast([P, nt, E]), eid[:, k].unsqueeze(2).to_broadcast([P, nt, E]), ALU.is_equal)
                link(ins)
                V.tensor_tensor(seln(l), oh[:, 0], oh[:, 1], ALU.add).then_inc(s_oh.h, 1)
                pg = rt(828, nt)
                v.wait_ge(s_r2.h, s_r2.at(l, 1))
                link(V.tensor_reduce(pg, ex, AX, ALU.add))
                link(V.reciprocal(pg, pg))
                v.wait_ge(s_r4.h, s_r4.at(l, 1))
                w0 = rt(832, nt)
                link(V.tensor_scalar(w0, dv, 1.0, None, ALU.add))
                link(V.reciprocal(w0, w0))
                link(V.tensor_tensor(gw[:, ta:, 0], w0, pg, ALU.mult))
                V.tensor_tensor(gw[:, ta:, 1], gw[:, ta:, 0], dv, ALU.mult)
                V.tensor_scalar(tokid[:, ta:], cf[:, C_TOK + ta:C_TOK + NT], -float(t0) - BIG, None, ALU.add)
                for k in range(2):
                    V.tensor_scalar(dmb[:, k, ta:], cf[:, C_TOK + ta:C_TOK + NT], k * TK[l] - t0 - BIG, None, ALU.add)
                J = JMAX[l]
                thr = rt(836, J)
                link(V.tensor_scalar(thr, iota[:, 1:J + 1], float(CAP), None, ALU.mult))
                v.wait_ge(s_rk.h, s_rk.at(l, 1))
                big = rt(900, E * 15)
                cnt = rt(844, E)
                link(V.tensor_copy(cnt, ps[:, 5, 128:160]))
                cmpj = big[:, 0:E * J].rearrange("p (e j) -> p e j", j=J)
                link(V.tensor_tensor(cmpj, cnt.unsqueeze(2).to_broadcast([P, E, J]), thr.unsqueeze(1).to_broadcast([P, E, J]), ALU.is_gt))
                nov = rt(1400, E)
                link(V.tensor_reduce(nov, cmpj, AX, ALU.add))
                inc = rt(1432, E)
                link(V.tensor_tensor_scan(inc, ones[:, 0:E], nov, 0.0, ALU.mult, ALU.add))
                base = rt(1464, E)
                link(V.tensor_tensor(base, inc, nov, ALU.subtract))
                rk = rt(1496, 2 * nt)
                bs = rt(1504, 2 * nt)
                prod = rt(900, 64 * nt).rearrange("p (k t e) -> p k t e", k=2, t=nt)
                for k in range(2):
                    ins = V.tensor_tensor(prod[:, k], oh[:, k], ps[:, 5, 0:E * nt].rearrange("p (t e) -> p t e", t=nt), ALU.mult)
                link(ins)
                link(V.tensor_reduce(rk, prod.rearrange("p k t e -> p (k t) e"), AX, ALU.add))
                link(V.tensor_tensor(prod.rearrange("p k t e -> p (k t) e"), oh.rearrange("p k t e -> p (k t) e"), base.unsqueeze(1).to_broadcast([P, 2 * nt, E]), ALU.mult))
                link(V.tensor_reduce(bs, prod.rearrange("p k t e -> p (k t) e"), AX, ALU.add))
                cj = big[:, 0:2 * nt * J].rearrange("p (a j) -> p a j", j=J)
                link(V.tensor_tensor(cj, rk.unsqueeze(2).to_broadcast([P, 2 * nt, J]), thr.unsqueeze(1).to_broadcast([P, 2 * nt, J]), ALU.is_ge))
                blk = rt(1512, 2 * nt)
                link(V.tensor_reduce(blk, cj, AX, ALU.add))
                slot = rt(1520, 2 * nt)
                V.scalar_tensor_tensor(out=slot, in0=blk, scalar=-float(CAP), in1=rk, op0=ALU.mult, op1=ALU.add)
                ef = eid.rearrange("p k t -> p (k t)")
                link(V.tensor_tensor(bs, bs, blk, ALU.add))
                link(V.scalar_tensor_tensor(out=bs, in0=bs, scalar=float(E - 1), in1=ef, op0=ALU.add, op1=ALU.subtract))
                link(V.tensor_scalar(blk, blk, 1.0, None, ALU.min))
                link(V.tensor_tensor(bs, bs, blk, ALU.mult))
                link(V.tensor_tensor(bs, bs, ef, ALU.add))
                Rm, Cm = a_(RTAB, 8 * P).rearrange("p (a n) -> p a n", a=8), a_(RTAB + 8 * P, 8 * NBT).rearrange("p (a n) -> p a n", a=8)
                n2 = 2 * nt
                V.tensor_tensor(Rm[:, 0:n2].rearrange("p a (two n) -> p a two n", two=2), iota.unsqueeze(1).unsqueeze(1).to_broadcast([P, n2, 2, 64]),
                                slot.unsqueeze(2).unsqueeze(2).to_broadcast([P, n2, 2, 64]), ALU.is_equal)
                link(V.tensor_tensor(Cm[:, 0:n2, 0:NB], iota[:, 0:NB].unsqueeze(1).to_broadcast([P, n2, NB]), bs.unsqueeze(2).to_broadcast([P, n2, NB]), ALU.is_equal))
                for k in range(2):
                    ak = slice(k * nt, (k + 1) * nt)
                    V.tensor_tensor(Cm[:, ak, NB:NBT], Cm[:, ak, 0:NB], dmb[:, k, ta:].unsqueeze(2).to_broadcast([P, nt, NB]), ALU.mult)
                for k in range(2):
                    ak = slice(k * nt, (k + 1) * nt)
                    ins = V.tensor_tensor(Cm[:, ak, 0:NB], Cm[:, ak, 0:NB], tokid[:, ta:].unsqueeze(2).to_broadcast([P, nt, NB]), ALU.mult)
                ins.then_inc(s_tb.h, 1)
                v.wait_ge(s_tbm.h, s_tbm.at(l, 1))
                V.tensor_scalar(idg[:], ps[:, 6, 0:NB], 2.0, halfb[:, 0:1], ALU.mult, ALU.add)
                V.tensor_scalar(ids[:], ps[:, 6, NB:NBT], 2.0, halfb[:, 0:1], ALU.mult, ALU.add).then_inc(s_ix.h, 1)
                m1 = big[0:1, 0:E * 15].rearrange("p (j e) -> p j e", e=E)
                m2 = a_(RTAB + 1776, E * 15)[0:1].rearrange("p (j e) -> p j e", e=E)
                jj = iota[0:1, 0:15].unsqueeze(2).to_broadcast([1, 15, E])
                V.tensor_tensor(m2, inc[0:1].unsqueeze(1).to_broadcast([1, 15, E]), jj, ALU.is_gt)
                link(V.tensor_tensor(m1, base[0:1].unsqueeze(1).to_broadcast([1, 15, E]), jj, ALU.is_le))
                link(V.tensor_tensor(m1, m1, m2, ALU.mult))
                link(V.tensor_tensor(m1, m1, iota[0:1, 0:E].unsqueeze(1).to_broadcast([1, 15, E]), ALU.mult))
                V.tensor_reduce(ovf[:, 1:16], m1, AX, ALU.add)
                link(V.tensor_copy(ovf[:, 0:1], inc[0:1, E - 1:E]))
                V.tensor_copy(ovi[:], ovf[:]).then_inc(s_ovi.h, 1)

                def hidden(q, s):
                    V.tensor_tensor(hid[0:64, :], sil[64:128, 0:256], ps[64:128, q, 0:256], ALU.mult)
                    V.tensor_tensor(hid[64:128, :], sil[64:128, 256:512], ps[64:128, q, 256:512], ALU.mult).then_inc(s, 1)

                def evac_hT(s):
                    V.tensor_copy(hidT[:], ps[:, 3, 0:256].rearrange("p (j n) -> p j n", j=4)).then_inc(s, 1)

                def expert(i, q):
                    e = 2 * i + q
                    v.wait_ge(s_sil.h, s_sil.at(l, e + 1))
                    if type(i) is not int or i > 0 or q:
                        v.wait_ge(s_ht.h, s_ht.at(l, e))
                    hidden(q, s_hid.h)
                    v.wait_ge(s_ht.h, s_ht.at(l, e + 1))
                    if type(i) is not int or i > 0 or q:
                        v.wait_ge(s_dn.h, s_dn.at(l, e))
                    evac_hT(s_htc.h)

                expert(0, 0)
                expert(0, 1)
                with v.Fori(1, E // 2) as i:
                    expert(i, 0)
                    expert(i, 1)
                v.wait_ge(s_dn.h, s_dn.at(l, E))
                v.wait_ge(s_ovi.h, s_ovi.at(l, 1))
                n_ov = v.value_load(ovi[0:1, 0:1], min_val=0, max_val=NOV[l])
                with v.Fori(0, NOV[l]) as j:
                    with v.If(j < n_ov):
                        v.wait_ge(s_ov[l], 11 * j + 6)
                        hidden(0, s_ov[l])
                        v.wait_ge(s_ov[l], 11 * j + 8)
                        evac_hT(s_ov[l])
                for n, t in enumerate(QTL[l]):
                    v.wait_ge(s_yl[n], 16 * (l + 1))
                    y0, y1 = yb[n][:, 0], yb[n][:, 1]
                    v.wait_ge(s_c0.h, s_c0.at(l, n + 1))
                    link(V.scalar_tensor_tensor(out=y0, in0=y1, scalar=gw[:, t, 1:2], in1=y0, op0=ALU.mult, op1=ALU.add))
                    V.tensor_tensor(y0, y0, row[3][t // 2], ALU.mult).then_inc(s_c1.h, 1)

        @block.gpsimd
        def _(g):
            G = nc.gpsimd
            link = chain(g, s_pool)
            for l in range(DEPTH):
                t0 = T0[l]
                if l == 1:
                    g.wait_ge(s_ovi.h, s_ovi.at(0, 1))
                if l == 0:
                    g.wait_ge(s_bf, 1)
                G.memset(up, 0.0).then_inc(s_up0, 1)
                g.wait_ge(s_ipa.h, s_ipa.at(l, 2))
                N = 4 * PADL
                link(G.tensor_tensor(w2[:, 0:N - 1], up[:, 0:N - 1], up[:, 1:N], ALU.add))
                link(G.tensor_tensor(w4[:, 0:N - 3], w2[:, 0:N - 3], w2[:, 2:N - 1], ALU.add))
                g.wait_ge(s_lw, 16 * 12 * (l + 1))
                U4 = up.rearrange("p (i s t) -> p i s t", i=2, s=2)
                dst = pooled[:].rearrange("p i (s t) -> p i s t", s=2)

                def group(gi, src, w):
                    r, i = 64 * (gi % 2), gi // 2
                    a = 8 - (w - 1) // 2
                    s = src.rearrange("p (i s t) -> p i s t", i=2, s=2)[r:r + 64, i, l:2, a:a + 256]
                    ic = icnt[r:r + 64, i, :].unsqueeze(1).to_broadcast([64, 2 - l, 256])
                    link(G.tensor_tensor(dst[r:r + 64, i, l:2], s, ic, ALU.mult))
                    return G.tensor_tensor(dst[r:r + 64, i, l:2], dst[r:r + 64, i, l:2], U4[r:r + 64, i, l:2, 8:264], ALU.subtract)
                link(group(0, w2, 2))
                link(group(1, w4, 4))
                link(G.tensor_tensor(w2[:, 0:N - 7], w4[:, 0:N - 7], w4[:, 4:N - 3], ALU.add))
                link(group(2, w2, 8))
                link(G.tensor_tensor(w4[:, 0:N - 15], w2[:, 0:N - 15], w2[:, 8:N - 7], ALU.add))
                group(3, w4, 16).then_inc(s_pl.h, 1)
                g.wait_ge(s_pl.h, s_pl.at(l, 1))
                for t in range(NT):
                    h0 = 0 if l == 0 or t >= 2 else 8
                    nv = sum(1 for name, i, e in in_groups(l) if e == "v" and i <= t)
                    g.wait_ge(s_ipv.h, s_ipv.at(l, nv))
                    if t:
                        g.wait_ge(s_qss.h, s_qss.at(l, t))
                    qk = tok[:, t, 0:640].rearrange("p (h d) -> p h d", h=10)
                    G.tensor_tensor(qtmp[:, h0:], qk[:, h0:], qk[:, h0:], ALU.mult).then_inc(s_qsq.h, 1)
                g.wait_ge(s_qsd.h, s_qsd.at(l, 2))
                for t in range(NT):
                    h0 = 0 if l == 0 or t >= 2 else 8
                    qk = tok[:, t, 0:640].rearrange("p (h d) -> p h d", h=10)
                    ins = link(G.tensor_tensor(qk[:, h0:], qk[:, h0:], qss[:, t, h0:].unsqueeze(2).to_broadcast([P, 10 - h0, HD]), ALU.mult))
                    if h0 == 0:
                        G.tensor_tensor(qk[:, 0:8], qk[:, 0:8], gain[:, 0, :].unsqueeze(1).to_broadcast([P, 8, HD]), ALU.mult)
                    ins = G.tensor_tensor(qk[:, 8:], qk[:, 8:], gain[:, 1, :].unsqueeze(1).to_broadcast([P, 2, HD]), ALU.mult)
                    if t < 2:
                        ins.then_inc(s_qr.h, 1)
                    else:
                        link(ins)
                        cos = cf[:, C_COS + 64 * (t - 2):C_COS + 64 * (t - 1)]
                        sin = cf[:, C_SIN + 64 * (t - 2):C_SIN + 64 * (t - 1)]
                        G.tensor_tensor(qtmp[:, :, 0:32], qk[:, :, 32:64], sin[:, 0:32].unsqueeze(1).to_broadcast([P, 10, 32]), ALU.mult)
                        link(G.tensor_tensor(qtmp[:, :, 32:64], qk[:, :, 0:32], sin[:, 32:64].unsqueeze(1).to_broadcast([P, 10, 32]), ALU.mult))
                        link(G.tensor_tensor(qk, qk, cos.unsqueeze(1).to_broadcast([P, 10, HD]), ALU.mult))
                        G.tensor_tensor(qk, qk, qtmp, ALU.add).then_inc(s_qr.h, 1)
                g.wait_ge(s_b.h, s_b.at(l, 1))
                g.wait_ge(s_pl.h, s_pl.at(l, 1))
                for step in range(1, LEVELS + 1):
                    b = (step + 1) % 2
                    m = 1 << (step - 1)
                    nb = (T - t0) // (2 * m)
                    if step >= 2:
                        g.wait_ge(s_lv.h, s_lv.at(l, 4 + (step - 2) * len(QTL[l])))

                    def halves(a):
                        return a.rearrange("p i (n h m) -> p i n h m", h=2, m=m)
                    K, Q = halves(el[:, b, 0, :, t0:T]), halves(el[:, b, 1, :, t0:T])
                    bf, bw = halves(bb[:, 0, :, t0:T]), halves(bb[:, 1, :, t0:T])
                    rf = bf[:, :, :, 0, m - 1:m].to_broadcast([P, 2, nb, m])
                    rw = bw[:, :, :, 1, 0:1].to_broadcast([P, 2, nb, m])
                    G.tensor_tensor(K[:, :, :, 0, :], rf, bf[:, :, :, 0, :], ALU.subtract)
                    G.tensor_tensor(K[:, :, :, 1, :], rw, bw[:, :, :, 1, :], ALU.subtract)
                    G.tensor_tensor(Q[:, :, :, 1, :], bf[:, :, :, 1, :], rf, ALU.subtract)
                    G.tensor_tensor(Q[:, :, :, 0, :], bw[:, :, :, 0, :], rw, ALU.subtract).then_inc(s_elx.h, 1)
                    g.wait_ge(s_ele.h, s_ele.at(l, step))
                    g.wait_ge(s_ipa.h, s_ipa.at(l, count(l, len(in_groups(l)), "a")))
                    G.tensor_tensor(el[:, b, 1, :, t0:T], el[:, b, 1, :, t0:T], hq[:, :, t0:T], ALU.mult).then_inc(s_elq.h, 1)
                if l == 0:
                    g.wait_ge(s_rvs, 1)
                    g.dma_start(rows_d, rvc[:, P:]).then_inc(s_rd, 16)
                for n, t in enumerate(QTL[l]):
                    g.wait_ge(s_h2.h, s_h2.at(l, n + 1))
                    g.dma_start(h2_d[l].rearrange("(t p two) n -> t p (two n)", p=P, two=2)[n], tok[:, t, :]).then_inc(s_h2d.h, 16)
                g.wait_ge(s_h2d.h, s_h2d.at(l, 16 * len(QTL[l])))
                g.wait_ge(s_ix.h, s_ix.at(l, 1))
                rows = 2 * TK[l]

                def gather(e, q, s):
                    G.tensor_copy(idgc[:, q:q + 1], idg[:, e:e + 1] if type(e) is int else idg[:, bass.ds(e, 1)]).then_inc(s_gi.h, 1)
                    g.wait_ge(s_gi.h, s_gi.at(l, e + 1))
                    g.sem_inc(s_go, 1)
                    gather_dma(q, s)

                def gather_dma(q, s):
                    g.indirect_dma_start(xg[:, q], None, h2_d[l], bass.IndirectOffsetOnAxis(ap=idgc[:, q:q + 1], axis=0),
                                         bounds_check=rows - 1, oob_is_err=False).then_inc(s, 16)

                def scatter(e, q, s):
                    G.tensor_copy(idsc[:, q:q + 1], ids[:, e:e + 1] if type(e) is int else ids[:, bass.ds(e, 1)]).then_inc(s_si.h, 1)
                    g.wait_ge(s_si.h, s_si.at(l, e + 1))
                    g.sem_inc(s_go, 1)
                    scatter_dma(q, s)

                def scatter_dma(q, s):
                    g.indirect_dma_start(y_d[l], bass.IndirectOffsetOnAxis(ap=idsc[:, q:q + 1], axis=0), ysb[:, q], None,
                                         bounds_check=2 * rows - 1, oob_is_err=False).then_inc(s, 16)

                def expert(i, q, last):
                    e = 2 * i + q
                    g.wait_ge(s_y.h, s_y.at(l, e + 1))
                    if type(i) is not int or i > 0:
                        g.wait_ge(s_scat[q].h, s_scat[q].at(l, 16 * i))
                    scatter(e, q, s_scat[q].h)
                    if not last:
                        g.wait_ge(s_gt.h, s_gt.at(l, e + 1))
                        g.wait_ge(s_xg[q].h, s_xg[q].at(l, 16 * i + 16))
                        gather(e + 2, q, s_xg[q].h)

                G.memset(junk[:], 0.0).then_inc(s_ov[l], 1)
                gather(0, 0, s_xg[0].h)
                gather(1, 1, s_xg[1].h)
                expert(0, 0, False)
                expert(0, 1, False)
                with g.Fori(1, E // 2 - 1) as i:
                    expert(i, 0, False)
                    expert(i, 1, False)
                expert(E // 2 - 1, 0, True)
                expert(E // 2 - 1, 1, True)
                g.wait_ge(s_scat[0].h, s_scat[0].at(l, 16 * E // 2))
                n_ov = g.value_load(ovi[0:1, 0:1], min_val=0, max_val=NOV[l])
                with g.Fori(0, NOV[l]) as j:
                    with g.If(j < n_ov):
                        g.wait_ge(s_ov[l], 11 * j + 1)
                        G.tensor_copy(idsc[:, 0:1], ids[:, bass.ds(j + E, 1)])
                        G.tensor_copy(idgc[:, 0:1], idg[:, bass.ds(j + E, 1)]).then_inc(s_ov[l], 1)
                        g.wait_ge(s_ov[l], 11 * j + 2)
                        g.sem_inc(s_go, 1)
                        gather_dma(0, s_ovx[l])
                        g.wait_ge(s_ov[l], 11 * j + 11)
                        g.sem_inc(s_go, 1)
                        scatter_dma(0, s_ovs[l])
                        g.wait_ge(s_ovs[l], 16 * j + 16)
                        G.tensor_tensor(junk[:], epsc[:], epsc[:], ALU.mult).then_inc(s_ov[l], 1)
                for n, t in enumerate(QTL[l]):
                    g.wait_ge(s_c1.h, s_c1.at(l, n + 1))
                    G.tensor_tensor(x[:, t, :], x[:, t, :], yb[n][:, 0], ALU.add).then_inc(s_x2.h, 1)



def constants():
    cf = np.zeros((P, NCF), np.float32)
    cf[:, C_ID:C_ID + P] = np.eye(P)
    cf[:64, C_BLK:C_BLK + 64] = 1
    cf[64:, C_BLK + 64:C_BLK + P] = 1
    cf[:, C_ONE:C_ONE + P] = 1
    cf[:, C_IOTA:C_IOTA + 64] = np.arange(64)
    cf[:, C_TOK:C_TOK + NT] = np.arange(P)[:, None] + P * np.arange(NT)
    cf[:, C_HALF] = np.arange(P) // 64
    cf[0::32, C_SEL] = 1
    cf[1::32, C_SEL + 1] = 1
    pos = np.arange(SEQ)
    inv = (np.float32(10000.0) ** (-np.arange(0, 32, 2, dtype=np.float32) / np.float32(32))).astype(np.float32)
    ang = np.concatenate([(pos // 64).astype(np.float32)[:, None] * inv, (pos % 64).astype(np.float32)[:, None] * inv], 1)
    cos, sin = np.cos(ang).astype(np.float32), np.sin(ang).astype(np.float32)
    cos2 = np.concatenate([cos, cos], 1).reshape(2, P, 64)
    sin2 = np.concatenate([-sin, sin], 1).reshape(2, P, 64)
    cf[:, C_COS:C_COS + P] = cos2.transpose(1, 0, 2).reshape(P, P)
    cf[:, C_SIN:C_SIN + P] = sin2.transpose(1, 0, 2).reshape(P, P)
    cb = np.zeros((P, 640), np.float32)
    cb[:, 0:P] = np.arange(P)[:, None] < np.arange(P)[None, :]
    for b in range(2):
        q = b * P + np.arange(P)[:, None]
        cb[:, P + 256 * b:P + 256 * (b + 1)] = np.where(np.abs(q - np.arange(256)[None, :]) <= 128, 0.0, -1e30)
    mk = np.zeros((P, LEVELS, P), np.float32)
    i = np.arange(P)
    for s in range(LEVELS):
        m = 1 << s
        same = (i[:, None] // (2 * m)) == (i[None, :] // (2 * m))
        mk[:, s] = same & ((i[:, None] // m) != (i[None, :] // m))
    cnt = np.zeros((P, 2, 256), np.float32)
    t = np.arange(256)
    for gi, w in enumerate((2, 4, 8, 16)):
        lo, hi = np.clip(t - (w - 1) // 2, 0, 256), np.clip(t + w // 2 + 1, 0, 256)
        cnt[64 * (gi % 2):64 * (gi % 2) + 64, gi // 2] = np.float32(1) / (hi - lo).astype(np.float32)
    return {"const_f": cf, "const_b": cb, "const_mask": mk.reshape(P, -1), "const_cnt": cnt.reshape(P, -1)}


_INS = ["x", "c", "ctx", "c_ctx", "norm1_g", "norm2_g", "ada_w", "ada_b", "w_in", "w_out", "pool_w", "pool_scale",
        "q_norm_g", "k_norm_g", "attn_sink", "hgrn_lb", "hgrn_norm_g", "router_group_w", "router_group_b",
        "router_expert_w", "router_expert_b", "expert_w_gate", "expert_w_up", "expert_w_down"]


def kernel(**inputs):
    import concourse.bacc as bacc
    from concourse.bass_utils import run_bass_kernel_spmd

    nc = bacc.Bacc("TRN2", target_bir_lowering=False, num_devices=1)
    arrays, args = {}, []
    given = {**{n: inputs[n] for n in _INS}, **constants()}
    for name, a in given.items():
        a = np.ascontiguousarray(a)
        arrays[f"in_{name}"] = a
        args.append(nc.dram_tensor(f"in_{name}", a.shape, mybir.dt.from_np(a.dtype), kind="ExternalInput").ap())
    out = nc.dram_tensor("out", (1, SEQ, D), F32, kind="ExternalOutput").ap()
    backbone(nc, *args, out)
    r = run_bass_kernel_spmd(nc, [arrays], core_ids=[0])
    return r.results[0]["out"]
```
